# Optimizing a Trainium2 kernel written in Bass

```python
import math
import jax, jax.numpy as jnp
from jax import lax
import numpy as np

D_MODEL = 1024
BATCH = 1
SEQ = 128
DEPTH = 2
DEC_BATCH = 1
DEC_SEQ = 256
PAST_LEN = 128

GRID_W = 64
N_HEADS = 8
N_KV_HEADS = 4
HEAD_DIM = 64
KV_GROUP = N_HEADS // N_KV_HEADS
ROPE_THETA = 10000.0
Q_BLOCK = 128
ATTN_Q_W = N_HEADS * HEAD_DIM
ATTN_KV_W = N_KV_HEADS * HEAD_DIM
GMLP_GROUPS = 4
GMLP_CHUNK = 128
GMLP_GROUP_W = 128
GMLP_W = GMLP_GROUPS * GMLP_GROUP_W
DN_HEADS = 4
DN_DK = 128
DN_DV = 128
DN_W = DN_HEADS * DN_DV
DN_CHUNK = 64
CONV_K = 5
N_DIR = 2
N_BRANCH = 3
BRANCH_W = 512
IN_SIZES = (ATTN_Q_W, ATTN_KV_W, ATTN_KV_W, GMLP_W, GMLP_W, 3 * DN_W, N_DIR * DN_HEADS, N_DIR * DN_HEADS, DN_W, N_BRANCH * D_MODEL)
IN_W = sum(IN_SIZES)
FFN_DIM = 2816
N_EXPERTS = 8
TOP_K = 2
EXPERT_DIM = 1408
N_MOD = 6
EPS = 1e-6

kernel_name = 'hybrid_diffusion_prefix_trunk_step'

def rmsnorm(x, gain):
    xf = x.astype(jnp.float32)
    y = xf * lax.rsqrt(jnp.mean(xf * xf, axis=-1, keepdims=True) + EPS)
    return (y * gain.astype(jnp.float32)).astype(x.dtype)

def l2norm(x):
    return x * lax.rsqrt(jnp.sum(x * x, axis=-1, keepdims=True) + EPS)

def rope_2d(x, row, col):
    half = HEAD_DIM // 2
    quarter = half // 2
    freqs = 1.0 / (ROPE_THETA ** (jnp.arange(quarter, dtype=jnp.float32) / quarter))

    def rot(xp, pos):
        ang = pos.astype(jnp.float32)[:, None] * freqs[None, :]
        cos = jnp.cos(ang)[None, :, None, :]
        sin = jnp.sin(ang)[None, :, None, :]
        x1, x2 = xp[..., :quarter], xp[..., quarter:]
        return jnp.concatenate([x1 * cos - x2 * sin, x1 * sin + x2 * cos], axis=-1)

    xf = x.astype(jnp.float32)
    out = jnp.concatenate([rot(xf[..., :half], row), rot(xf[..., half:], col)], axis=-1)
    return out.astype(x.dtype)

def block_attention(q, k, v):
    B, Sq = q.shape[0], q.shape[1]
    nb = Sq // Q_BLOCK
    qb = q.reshape(B, nb, Q_BLOCK, N_KV_HEADS, KV_GROUP, HEAD_DIM).swapaxes(0, 1)
    scale = HEAD_DIM ** -0.5

    def one_block(q_blk):
        s = jnp.einsum('bqhgd,bkhd->bhgqk', q_blk, k).astype(jnp.float32) * scale
        p = jax.nn.softmax(s, axis=-1).astype(v.dtype)
        return jnp.einsum('bhgqk,bkhd->bqhgd', p, v)

    o = lax.map(one_block, qb)
    return o.swapaxes(0, 1).reshape(B, Sq, ATTN_Q_W)

def chunk_gmlp(u, v, gain, w_s, b_s):
    B, S, _ = u.shape
    n = S // GMLP_CHUNK
    vn = rmsnorm(v, gain).reshape(B, n, GMLP_CHUNK, GMLP_GROUPS, GMLP_GROUP_W)
    sv = jnp.einsum('gpq,bnqgc->bnpgc', w_s, vn) + b_s.T[None, None, :, :, None]
    return u * sv.reshape(B, S, GMLP_W)

def short_conv(x, w):
    C = x.shape[-1]
    pad = CONV_K // 2
    return lax.conv_general_dilated(x, w[:, None, :].astype(x.dtype), window_strides=(1,), padding=[(pad, pad)],
                                    dimension_numbers=('NWC', 'WIO', 'NWC'), feature_group_count=C)

def gated_delta_chunked(q, k, v, g, beta, s0):
    B, S, H, _ = q.shape
    n = S // DN_CHUNK

    def to_chunks(t):
        t = t.reshape((B, n, DN_CHUNK, H) + t.shape[3:])
        return jnp.moveaxis(t, (1, 3), (0, 2))

    qc, kc, vc, bc = to_chunks(q), to_chunks(k), to_chunks(v), to_chunks(beta)
    gc = jnp.cumsum(to_chunks(g), axis=-1)
    idx = jnp.arange(DN_CHUNK)
    incl = idx[:, None] >= idx[None, :]
    strict = idx[:, None] > idx[None, :]
    diff = gc[..., :, None] - gc[..., None, :]
    decay = jnp.where(incl, jnp.exp(jnp.where(incl, diff, 0.0)), 0.0)
    kb = kc * bc[..., None]
    m = jnp.where(strict, jnp.einsum('nbhid,nbhjd->nbhij', kb, kc) * decay, 0.0)
    eye = jnp.eye(DN_CHUNK, dtype=m.dtype)
    t_inv = lax.linalg.triangular_solve(eye + m, jnp.broadcast_to(eye, m.shape), left_side=True, lower=True,
                                        unit_diagonal=True)
    u = jnp.einsum('nbhij,nbhje->nbhie', t_inv, vc * bc[..., None])
    w = jnp.einsum('nbhij,nbhjd->nbhid', t_inv, kb * jnp.exp(gc)[..., None])
    qk = jnp.einsum('nbhid,nbhjd->nbhij', qc, kc) * decay

    def step(state, inp):
        q_i, k_i, u_i, w_i, qk_i, g_i = inp
        v_new = u_i - jnp.einsum('bhcd,bhde->bhce', w_i, state)
        o_i = (jnp.einsum('bhcd,bhde->bhce', q_i * jnp.exp(g_i)[..., None], state)
               + jnp.einsum('bhij,bhje->bhie', qk_i, v_new))
        g_last = g_i[..., -1]
        k_dec = k_i * jnp.exp(g_last[..., None] - g_i)[..., None]
        state = state * jnp.exp(g_last)[..., None, None] + jnp.einsum('bhcd,bhce->bhde', k_dec, v_new)
        return state, o_i

    s_fin, o = lax.scan(step, s0, (qc, kc, u, w, qk, gc))
    return o.transpose(1, 0, 3, 2, 4).reshape(B, S, H, -1), s_fin

def deltanet_mixer(qkv, b_raw, a_raw, z, conv_w, a_log, dt_bias, norm_g, s0):
    B, S, _ = qkv.shape
    f32 = jnp.float32
    hqkv = jax.nn.silu(short_conv(qkv, conv_w)).astype(f32)
    q, k, v = jnp.split(hqkv, 3, axis=-1)
    q = l2norm(q.reshape(B, S, DN_HEADS, DN_DK)) * (DN_DK ** -0.5)
    k = l2norm(k.reshape(B, S, DN_HEADS, DN_DK))
    v = v.reshape(B, S, DN_HEADS, DN_DV)
    beta = jax.nn.sigmoid(b_raw.astype(f32)).reshape(B, S, N_DIR, DN_HEADS)
    g = -jnp.exp(a_log.astype(f32)) * jax.nn.softplus(a_raw.astype(f32).reshape(B, S, N_DIR, DN_HEADS) + dt_bias.astype(f32))
    s0 = s0.astype(f32)
    o_f, s_f = gated_delta_chunked(q, k, v, g[:, :, 0], beta[:, :, 0], s0[:, 0])
    flip = lambda t: jnp.flip(t, axis=1)
    o_r, s_r = gated_delta_chunked(flip(q), flip(k), flip(v), flip(g[:, :, 1]), flip(beta[:, :, 1]), s0[:, 1])
    o = rmsnorm(o_f + flip(o_r), norm_g) * jax.nn.silu(z.astype(f32)).reshape(B, S, DN_HEADS, DN_DV)
    return o.reshape(B, S, DN_W).astype(qkv.dtype), jnp.stack([s_f, s_r], axis=1)

def swiglu(h, w_gate, w_up, w_down):
    return (jax.nn.silu(h @ w_gate) * (h @ w_up)) @ w_down

def moe_swiglu(h, router, w_gate, w_up, w_down):
    probs = jax.nn.softmax((h @ router).astype(jnp.float32), axis=-1)
    top_p, top_i = lax.top_k(probs, TOP_K)
    top_p = top_p / jnp.sum(top_p, axis=-1, keepdims=True)
    combine = jnp.sum(jax.nn.one_hot(top_i, N_EXPERTS, dtype=jnp.float32) * top_p[..., None], axis=-2).astype(h.dtype)
    a = jnp.einsum('bsd,edf->bsef', h, w_gate)
    u = jnp.einsum('bsd,edf->bsef', h, w_up)
    hid = jax.nn.silu(a) * u * combine[..., None]
    return jnp.einsum('bsef,efd->bsd', hid, w_down)

def trunk_layer(x, mod, p, ffn, is_moe, grid_pos, ctx_k, ctx_v, s0):
    B, S, _ = x.shape
    shift1, scale1, gate1, shift2, scale2, gate2 = jnp.split(mod, N_MOD, axis=-1)
    h = rmsnorm(x, p['norms'][0]) * (1.0 + scale1) + shift1
    z = h @ p['w_in']
    split_idx = np.cumsum(np.array(IN_SIZES))[:-1].tolist()
    qa, ka, va, ub, vb, qkvc, bc, ac, zc, gates = jnp.split(z, split_idx, axis=-1)
    qa = rmsnorm(qa.reshape(B, S, N_HEADS, HEAD_DIM), p['qk_norm'][0])
    ka = rmsnorm(ka.reshape(B, S, N_KV_HEADS, HEAD_DIM), p['qk_norm'][1])
    va = va.reshape(B, S, N_KV_HEADS, HEAD_DIM)
    if grid_pos is None:
        k_all, v_all = ka, va
    else:
        row, col = grid_pos
        qa = rope_2d(qa, row, col)
        ka = rope_2d(ka, row, col)
        k_all = jnp.concatenate([ctx_k.astype(ka.dtype), ka], axis=1)
        v_all = jnp.concatenate([ctx_v.astype(va.dtype), va], axis=1)
    o_a = block_attention(qa, k_all, v_all)
    o_b = chunk_gmlp(jax.nn.gelu(ub), jax.nn.gelu(vb), p['gmlp_norm'], p['gmlp_ws'], p['gmlp_bs'])
    o_c, s_fin = deltanet_mixer(qkvc, bc, ac, zc, p['dn_conv'], p['dn_a_log'], p['dn_dt_bias'], p['dn_norm'], s0)
    g_a, g_b, g_c = jnp.split(jax.nn.sigmoid(gates), N_BRANCH, axis=-1)
    wb = p['w_branch']
    merged = g_a * (o_a @ wb[0]) + g_b * (o_b @ wb[1]) + g_c * (o_c @ wb[2])
    x = x + gate1 * rmsnorm(merged @ p['w_out'], p['norms'][1])
    h2 = rmsnorm(x, p['norms'][2]) * (1.0 + scale2) + shift2
    f = moe_swiglu(h2, *ffn) if is_moe else swiglu(h2, *ffn)
    x = x + gate2 * rmsnorm(f, p['norms'][3])
    return x, ka, va, s_fin

def setup_inputs(seed: int = 0) -> dict:
    key = jax.random.key(seed)
    ks = jax.random.split(key, 32)
    f32 = jnp.float32
    n_dense = (DEPTH + 1) // 2
    n_moe = DEPTH // 2

    def nrm(k, shape, scale):
        return jax.random.normal(k, shape, f32) * scale

    dt = jnp.exp(jax.random.uniform(ks[20], (DEPTH, N_DIR, DN_HEADS), f32, math.log(1e-3), math.log(1e-1)))
    return {
        'x_prompt': nrm(ks[0], (BATCH, SEQ, D_MODEL), 1.0),
        'x_sample': nrm(ks[1], (DEC_BATCH, DEC_SEQ, D_MODEL), 1.0),
        'cache_attn_k': nrm(ks[2], (DEC_BATCH, DEPTH, PAST_LEN, N_KV_HEADS, HEAD_DIM), 1.0),
        'cache_attn_v': nrm(ks[3], (DEC_BATCH, DEPTH, PAST_LEN, N_KV_HEADS, HEAD_DIM), 1.0),
        'state_delta': nrm(ks[4], (DEC_BATCH, DEPTH, N_DIR, DN_HEADS, DN_DK, DN_DV), 0.1),
        'c': nrm(ks[5], (DEC_BATCH, D_MODEL), 1.0),
        'c_ctx': nrm(ks[6], (D_MODEL,), 1.0),
        'ada_w': nrm(ks[7], (DEPTH, D_MODEL, N_MOD * D_MODEL), 0.5 * D_MODEL ** -0.5),
        'ada_b': nrm(ks[8], (DEPTH, N_MOD * D_MODEL), 0.02),
        'norms': 1.0 + nrm(ks[9], (DEPTH, 4, D_MODEL), 0.05),
        'w_in': nrm(ks[10], (DEPTH, D_MODEL, IN_W), D_MODEL ** -0.5),
        'qk_norm': 1.0 + nrm(ks[11], (DEPTH, 2, HEAD_DIM), 0.05),
        'gmlp_norm': 1.0 + nrm(ks[12], (DEPTH, GMLP_W), 0.05),
        'gmlp_ws': nrm(ks[13], (DEPTH, GMLP_GROUPS, GMLP_CHUNK, GMLP_CHUNK), GMLP_CHUNK ** -0.5),
        'gmlp_bs': 1.0 + nrm(ks[14], (DEPTH, GMLP_GROUPS, GMLP_CHUNK), 0.05),
        'dn_conv': nrm(ks[15], (DEPTH, CONV_K, 3 * DN_W), CONV_K ** -0.5),
        'dn_a_log': jnp.log(jax.random.uniform(ks[16], (DEPTH, N_DIR, DN_HEADS), f32, 1.0, 16.0)),
        'dn_dt_bias': dt + jnp.log(-jnp.expm1(-dt)),
        'dn_norm': 1.0 + nrm(ks[17], (DEPTH, DN_DV), 0.05),
        'w_branch': nrm(ks[18], (DEPTH, N_BRANCH, BRANCH_W, D_MODEL), BRANCH_W ** -0.5),
        'w_out': nrm(ks[19], (DEPTH, D_MODEL, D_MODEL), D_MODEL ** -0.5),
        'ffn_w_gate': nrm(ks[21], (n_dense, D_MODEL, FFN_DIM), D_MODEL ** -0.5),
        'ffn_w_up': nrm(ks[22], (n_dense, D_MODEL, FFN_DIM), D_MODEL ** -0.5),
        'ffn_w_down': nrm(ks[23], (n_dense, FFN_DIM, D_MODEL), FFN_DIM ** -0.5),
        'moe_router': nrm(ks[24], (n_moe, D_MODEL, N_EXPERTS), D_MODEL ** -0.5),
        'moe_w_gate': nrm(ks[25], (n_moe, N_EXPERTS, D_MODEL, EXPERT_DIM), D_MODEL ** -0.5),
        'moe_w_up': nrm(ks[26], (n_moe, N_EXPERTS, D_MODEL, EXPERT_DIM), D_MODEL ** -0.5),
        'moe_w_down': nrm(ks[27], (n_moe, N_EXPERTS, EXPERT_DIM, D_MODEL), EXPERT_DIM ** -0.5),
    }

def reference(x_prompt, x_sample, cache_attn_k, cache_attn_v, state_delta, c, c_ctx, ada_w, ada_b, norms, w_in,
              qk_norm, gmlp_norm, gmlp_ws, gmlp_bs, dn_conv, dn_a_log, dn_dt_bias, dn_norm, w_branch, w_out,
              ffn_w_gate, ffn_w_up, ffn_w_down, moe_router, moe_w_gate, moe_w_up, moe_w_down):
    rows = x_sample.shape[1] // GRID_W
    row = jnp.repeat(jnp.arange(rows), GRID_W)
    col = jnp.tile(jnp.arange(GRID_W), rows)
    s0_ctx = jnp.zeros((x_prompt.shape[0], N_DIR, DN_HEADS, DN_DK, DN_DV), jnp.float32)
    xp, xs = x_prompt, x_sample
    new_k, new_v, new_s = [], [], []
    for l in range(DEPTH):
        p = {'norms': norms[l], 'w_in': w_in[l], 'qk_norm': qk_norm[l], 'gmlp_norm': gmlp_norm[l],
             'gmlp_ws': gmlp_ws[l], 'gmlp_bs': gmlp_bs[l], 'dn_conv': dn_conv[l], 'dn_a_log': dn_a_log[l],
             'dn_dt_bias': dn_dt_bias[l], 'dn_norm': dn_norm[l], 'w_branch': w_branch[l], 'w_out': w_out[l]}
        is_moe = (l % 2 == 1)
        j = l // 2
        if is_moe:
            ffn = (moe_router[j], moe_w_gate[j], moe_w_up[j], moe_w_down[j])
        else:
            ffn = (ffn_w_gate[j], ffn_w_up[j], ffn_w_down[j])
        mod_ctx = (jax.nn.silu(c_ctx) @ ada_w[l] + ada_b[l])[None, None, :]
        xp, k_ctx, v_ctx, s_ctx = trunk_layer(xp, mod_ctx, p, ffn, is_moe, None, None, None, s0_ctx)
        new_k.append(k_ctx)
        new_v.append(v_ctx)
        new_s.append(s_ctx)
        mod_lat = (jax.nn.silu(c) @ ada_w[l] + ada_b[l])[:, None, :]
        xs, _, _, _ = trunk_layer(xs, mod_lat, p, ffn, is_moe, (row, col), cache_attn_k[:, l], cache_attn_v[:, l],
                                  state_delta[:, l])
    return (xp, xs, jnp.stack(new_k, axis=1), jnp.stack(new_v, axis=1), jnp.stack(new_s, axis=1))


_drawn_inputs = setup_inputs


def setup_inputs(seed=0):
    import zlib

    import numpy as np

    out = dict(_drawn_inputs(seed))
    spreads = {}
    factors = {}
    for name, (base, spread) in spreads.items():
        noise = np.random.default_rng([zlib.crc32(name.encode()), seed]).standard_normal(out[name].shape)
        drawn = base * np.exp(spread * noise) if base else spread * noise
        out[name] = __import__('jax').numpy.asarray(drawn.astype(out[name].dtype))
    for name, factor in factors.items():
        out[name] = (out[name] * factor).astype(out[name].dtype)
    return out
```

```python
import math
from contextlib import ExitStack

import numpy as np

import concourse.bass as bass
from concourse import mybir

F32 = mybir.dt.float32
BF16 = mybir.dt.bfloat16
U32 = mybir.dt.uint32
ALU = mybir.AluOpType
ACT = mybir.ActivationFunctionType
AX = mybir.AxisListType

P = 128
D = 1024
KT = D // P
DEPTH = 2
CTX, LAT = 128, 256
TOK = CTX + LAT
NT = TOK // P
HEADS, KVH, HD = 8, 4, 64
ROPE_THETA, GRID_W = 10000.0, 64
DNH, DK = 4, 128
CHUNK = 64
CONV_K = 5
FFN = 2816
NE, ED = 8, 1408
EPS = 1e-6
FG, FE = FFN // P, ED // P

C_QA, C_KA, C_U, C_V, C_DN, C_BA, C_Z, C_GATE = 0, 512, 1024, 1536, 2048, 3584, 3600, 4112

NSLOT = 4
SLOT = 4096
CROW = CTX + LAT + 4 * (CONV_K // 2)
COUT = CROW - (CONV_K - 1)
LAT0 = CTX + 4
SEG = ((0, 0, CTX), (1, CTX, TOK))

T_QKV, T_BA, T_A, T_UV, T_G, T_Z = 0, 12, 15, 21, 27, 51
N_PROJ = 54
LEVELS = (1, 2, 4, 8, 16, 32)

PER = dict(proj_mm=N_PROJ, proj_ev=N_PROJ, sq=4, stat=4, root=4, rinv=4, xn=2, h_a=8, h_v=8, x_new=2,
           pads=1, conv=12, silu=3, dsq=1, dst=8, droot=8, qkn=1, kvt_mm=6, kvt_ev=6,
           ba_v=1, ba_l=1, g_ok=1, gc_mm=1, gc_v=1, gc_e=1, beg=1,
           a_sq=1, a_ss=1, a_rt=1, a_ok=1, tr_mm=6, tr_ev=6, v_ss=1, v_rt=1, v_ok=1,
           at_s=24, at_m=24, at_e=24, at_p=24, at_t=24, at_pt=24, at_pv=24, at_o=3,
           b_mm=3, b_v=3, b_t=3, b_ev=3,
           d_in=6, d_d0=6, d_e=6, d_pool=6, d_m=6, d_mt=6, d_mtc=6, d_t1=6, d_ct=30, d_w=30, d_we=30,
           d_du=30, d_up=30, d_uw=6, d_uwe=6, d_kd=6, s_ws=12, s_vn=12, s_o=12, s_st=12, s_or=6,
           oc_sq=1, oc_ss=1, oc_rt=1, oc_v=1, oc_mm=3, oc_ev=3, gsig=1,
           br_mm=8, br_ev=8, wo_mm=8, wo_ev=8)


TILE = ((0, 0), (1, 2), (2, 1))
TCOL = (0, LAT0, LAT0 + P)


def constants():
    i, j = np.arange(P)[:, None], np.arange(P)[None, :]
    same = (i // CHUNK) == (j // CHUNK)
    parts = [np.eye(P), (i >= j) & same, (i <= j) & same, same, np.ones((P, P))]
    quarter = HD // 4
    freqs = (1.0 / (np.float32(ROPE_THETA) ** (np.arange(quarter, dtype=np.float32) / quarter))).astype(np.float32)
    rope = np.zeros((P, 2, 2, 2, quarter), np.float32)
    for t in range(LAT // P):
        pos = t * P + np.arange(P)
        for a, x in enumerate((pos // GRID_W, pos % GRID_W)):
            ang = x[:, None].astype(np.float32) * freqs[None]
            rope[:, t, 0, a], rope[:, t, 1, a] = np.cos(ang), np.sin(ang)
    parts.append(rope.reshape(P, -1))
    parts.append(np.stack([np.arange(P) < CHUNK, np.arange(P) >= CHUNK], 1))
    parts.append(np.tile([EPS, DK * EPS, 1.0], (P, 1)))
    parts.append(np.tile(np.arange(NE), (P, 1)))
    for s in LEVELS:
        low = (i // (2 * s) == j // (2 * s)) & (i % (2 * s) >= s) & (j % (2 * s) < s)
        parts += [-1.0 * low, -1.0 * low.T]
    return np.ascontiguousarray(np.concatenate([np.asarray(x, np.float32) for x in parts], 1))


NRES = 5 * P + 128 + 2 + 3 + NE
NCST = NRES + 2 * len(LEVELS) * P


def build(nc, cst_d, x_prompt, x_sample, cache_k, cache_v, state_in, c, c_ctx, ada_w, ada_b, norms, w_in, qk_norm,
          gmlp_norm, gmlp_ws, gmlp_bs, dn_conv, dn_a_log, dn_dt_bias, dn_norm, w_branch, w_out, ffn_g, ffn_u, ffn_d,
          router, moe_g, moe_u, moe_d, xpark, y_prompt, y_sample, new_k, new_v, new_s):
    ctx = ExitStack()
    with ctx:
        def sb(name, n, dt=F32):
            return ctx.enter_context(nc.sbuf_tensor(name, [P, n], dt))

        def sem(name):
            return ctx.enter_context(nc.semaphore(name))

        ring = sb("ring", NSLOT * SLOT)
        H = sb("hT", KT * TOK)
        GT = sb("gates", 24 * TOK)
        CV = sb("conv", 12 * COUT)
        KK_ = sb("ktok", NT * 512)
        OT = sb("oT", 12 * TOK)
        RX = sb("work", 10240)
        cst = sb("cst", NRES)
        lmask = sb("lmask", 2 * len(LEVELS) * P, BF16)
        rows = sb("rowsT", 64 + 96 + 24 + 120)
        modv = sb("modv", DEPTH * 96)
        sm = sb("small", 768)

        def v3(ap, a):
            return ap.rearrange("p (a b) -> p a b", a=a)

        hT, xT = v3(H[:, :], KT), v3(RX[:, 0:KT * TOK], KT)
        yT = v3(RX[:, 3072:6144], KT)
        sqT, sqP = v3(GT[:, 0:3072], KT), v3(CV[:, 0:3072], KT)
        gates = v3(GT[:, :], 24)
        pre = v3(GT[:, 0:12 * CROW], 12)
        dsq = v3(GT[:, 12 * CROW:12 * CROW + 8 * COUT], 8)
        cv = v3(CV[:, :], 12)
        vtok = CV[:, 8 * COUT:8 * COUT + 1536].rearrange("p (t h e) -> p t h e", t=NT, h=DNH)
        ktok = KK_[:, :].rearrange("p (t h e) -> p t h e", t=NT, h=DNH)
        oT = OT[:, :].rearrange("p (b k n) -> p b k n", b=3, k=4)
        ident, inclL, inclU, same, ones = (cst[:, i * P:(i + 1) * P] for i in range(5))
        rope = cst[:, 640:768].rearrange("p (t f a q) -> p t f a q", t=2, f=2, a=2)
        chsel = cst[:, 768:770]
        eps1, eps128, one1 = (cst[:, 770 + i:771 + i] for i in range(3))
        iota8 = cst[:, 773:773 + NE]
        lm = lmask[:, :].rearrange("p (s f n) -> p s f n", s=len(LEVELS), f=2)
        nrmT = rows[:, 0:64].rearrange("p (l a k) -> p l a k", l=DEPTH, a=4)
        adab = rows[:, 64:160].rearrange("p (l m) -> p l m", l=DEPTH)
        scT = rows[:, 160:176].rearrange("p (s k) -> p s k", s=2)
        bsT = rows[:, 176:184].rearrange("p (l g) -> p l g", l=DEPTH)
        cwT = rows[:, 184:304].rearrange("p (l j n) -> p l j n", l=DEPTH, j=CONV_K)
        mod = modv[:, :].rearrange("p (l a k s) -> p l a k s", l=DEPTH, a=6, k=KT)

        qkv = v3(RX[:, 0:3072], NT)
        qTt = v3(RX[:, 3072:4608], 4)
        kTt = v3(RX[:, 4608:5632], 2)
        Pb = v3(RX[:, 5632:6400], 2)
        PTb = v3(RX[:, 6400:7168], 2)
        uB, vB = v3(RX[:, 7168:8704], NT), v3(RX[:, 8704:10240], NT)
        wsT = OT[:, 3072:3584]
        ggain = OT[:, 3584:4096]
        qkgain = OT[:, 4096:4224]
        asq = v3(OT[:, 0:2304], NT)
        kcache, vcache = GT[:, 8192:8448], GT[:, 8448:8704]
        wsraw = v3(GT[:, 8704:9216], 4)
        gsc = GT[:, 7168:7680]
        rt = [GT[:, 384 * i:384 * (i + 1)].rearrange("p (h a q) -> p h a q", h=12, a=2) for i in range(4)]

        def dn(d, i):
            return v3(RX[:, (9 * d + i) * 512:(9 * d + i + 1) * 512], DNH)
        B_M, B_QK, B_QEG, B_MT, B_T, B_U, B_W, B_VU, B_KW = range(9)
        B_CT, B_KD, B_VN = B_M, B_MT, B_T
        state = RX[:, 9216:10240].rearrange("p (d h e) -> p d h e", d=2, h=DNH)
        osum = v3(OT[:, 3072:4608], NT)
        zs = v3(CV[:, 0:1536], NT)
        merged = v3(CV[:, 1536:4608], KT)
        btmp = [RX[:, 6144 + 384 * i:6528 + 384 * i] for i in range(3)]
        sgb = v3(RX[:, 6144:6912], 2)
        hid = v3(GT[:, 0:FG * TOK], FG)
        combB = v3(GT[:, 4224:4224 + NE * TOK], NE)

        off = [0]

        def small(n):
            off[0] += n
            assert off[0] <= 768
            return sm[:, off[0] - n:off[0]]
        ba = v3(small(48), NT)
        beta, gg, t1, t2, beg, edec, eg = (v3(small(24), NT) for _ in range(7))
        gcs, glr = v3(small(24), NT), v3(small(24), NT)
        gm = small(48).rearrange("p (t c n) -> p t c n", t=NT, c=2)
        egl = small(48).rearrange("p (t c n) -> p t c n", t=NT, c=2)
        expa, dtb = small(8), small(8)
        ass, amx, anm, ars = small(36), small(24), small(24), small(24)
        vss, oss = small(3), small(12)
        m8, i8, i8f = small(24), small(24), small(24)
        oh0, oh1, comb = (v3(small(24), NT) for _ in range(3))
        baw = OT[:, 4224:4352]
        dngain = sb("dngain", DK)
        rs = sb("rstd", TOK)
        rtw = sb("routerw", KT * NE)

        B = [ctx.enter_context(nc.psum_tensor(f"bank{i}", [P, 512], F32)) for i in range(8)]

        s_slot = [sem(f"slot{i}_full") for i in range(NSLOT)]
        S = {n: sem(n) for n in PER}
        (cst_in, rows_in, x_in, bf_ok, rt_mm, rt_ev, sc_ok, xt_mm, xt_ev, ada_mm, mod_ok, lw_in, cache_in, dn_in, parked,
         unparked, kv_out, st_out, st_in, y_out, gu_g, gu_u, gu_s, gu_m, gu_h, down_mm, down_ev, rl_mm, rl_c, rl_e, rl_ok, rb_mm, rb_ev,
         xo_mm, xo_ev, sp_turn, act_step, dve_step, pool_step) = (sem(n) for n in (
            "cst_in rows_in x_in bf_ok rt_mm rt_ev sc_ok xt_mm xt_ev ada_mm mod_ok lw_in cache_in dn_in parked "
            "unparked kv_out st_out st_in y_out gu_g gu_u gu_s gu_m gu_h down_mm down_ev rl_mm rl_c rl_e rl_ok rb_mm rb_ev "
            "xo_mm xo_ev sp_turn act_step dve_step pool_step").split())

        def wait(eng, name, layer, n):
            if PER[name] * layer + n > 0:
                eng.wait_ge(S[name], PER[name] * layer + n)

        def linker(eng, step):
            n = [0]

            def link(ins):
                n[0] += 1
                ins.then_inc(step, 1)
                eng.wait_ge(step, n[0])
            return link

        U_ADA, U_W, U_DENSE = 0, 24, 44
        U_W1 = U_DENSE + 11 + 8
        U_MOE = U_W1 + 20
        MOE_U = 10
        WIN = [C_DN, C_DN + 512, C_DN + 1024, C_QA, C_KA, C_U, C_V] + [C_GATE + 512 * i for i in range(6)] + [C_Z]
        WIN_END = [4, 8, 12, T_A + 3, T_A + 6, T_UV + 3, T_UV + 6] + [T_G + 4 * (i + 1) for i in range(6)] + [T_Z + 3]

        def u_layer(layer):
            return U_W if layer == 0 else U_W1

        def slot(unit):
            return unit % NSLOT

        def wslot(unit, k, n):
            s = slot(unit)
            return ring[:, s * SLOT:s * SLOT + k * n].rearrange("p (k n) -> p k n", k=k)

        def dmas(unit):
            if U_DENSE <= unit < U_DENSE + 11:
                return 2
            return 2 if unit >= U_MOE and (unit - U_MOE) % MOE_U < 6 else 1

        def full(unit):
            return 16 * sum(dmas(u) for u in range(unit % NSLOT, unit + 1, NSLOT))

        block = ctx.enter_context(nc.Block())

        @block.sync
        def _(sp):
            def load(unit, dst, src):
                sp.dma_start(dst, src).then_inc(s_slot[slot(unit)], 16)

            for n in range(24):
                if n >= NSLOT:
                    sp.wait_ge(ada_mm, n - NSLOT + 1)
                layer, i = divmod(n, 12)
                load(n, wslot(n, KT, 512), ada_w[layer, :, 512 * i:512 * (i + 1)].rearrange("(k p) n -> p k n", p=P))

            def freed(unit):
                u = unit - NSLOT
                if u < U_W:
                    sp.wait_ge(ada_mm, u + 1)
                elif u < U_DENSE or U_W1 <= u < U_MOE:
                    layer = 0 if u < U_DENSE else 1
                    i = u - u_layer(layer)
                    if i < 14:
                        wait(sp, "proj_mm", layer, WIN_END[i])
                    elif i < 18:
                        wait(sp, "br_mm", layer, 2 * (i - 13))
                    else:
                        wait(sp, "wo_mm", layer, 4 * (i - 17))
                elif u < U_DENSE + 11:
                    sp.wait_ge(gu_u, 2 * (u - U_DENSE + 1))
                else:
                    sp.wait_ge(down_mm, u - U_DENSE - 10)

            for layer in range(DEPTH):
                u0 = u_layer(layer)
                for i in range(20):
                    if i == 4:
                        wait(sp, "xn", layer, 1)
                        wait(sp, "sq", layer, 1)
                        sp.dma_start(xpark.rearrange("p (k n) -> p k n", k=KT), xT).then_inc(parked, 16)
                    freed(u0 + i)
                    if i < 14:
                        src = w_in[layer, :, WIN[i]:WIN[i] + 512].rearrange("(k p) n -> p k n", p=P)
                        load(u0 + i, wslot(u0 + i, KT, 512), src)
                    elif i < 18:
                        n0 = 256 * (i - 14)
                        src = w_branch[layer, :, :, n0:n0 + 256].rearrange("b (k p) n -> p (b k) n", p=P)
                        load(u0 + i, wslot(u0 + i, 12, 256), src)
                    else:
                        n0 = 512 * (i - 18)
                        load(u0 + i, wslot(u0 + i, KT, 512), w_out[layer, :, n0:n0 + 512].rearrange("(k p) n -> p k n", p=P))
                if layer == 0:
                    for i in range(11):
                        u = U_DENSE + i
                        freed(u)
                        d = ring[:, slot(u) * SLOT:(slot(u) + 1) * SLOT].rearrange("p (g k n) -> p g k n", g=2, k=KT)
                        n0 = 256 * i
                        sp.dma_start(d[:, 0], ffn_g[0, :, n0:n0 + 256].rearrange("(k p) n -> p k n", p=P)).then_inc(s_slot[slot(u)], 16)
                        sp.dma_start(d[:, 1], ffn_u[0, :, n0:n0 + 256].rearrange("(k p) n -> p k n", p=P)).then_inc(s_slot[slot(u)], 16)
                    for i in range(8):
                        u = U_DENSE + 11 + i
                        freed(u)
                        load(u, wslot(u, FG, P), ffn_d[0, :, P * i:P * (i + 1)].rearrange("(k p) n -> p k n", p=P))

            def moe_load(e, j, slot_unit):
                k = slot(slot_unit)
                if j < 6:
                    n = 256 if j < 5 else P
                    d = ring[:, k * SLOT:k * SLOT + 16 * n].rearrange("p (g k n) -> p g k n", g=2, k=KT)
                    for g, w in enumerate((moe_g, moe_u)):
                        src = w[0, bass.ds(e, 1), :, 256 * j:256 * j + n].rearrange("a (k p) n -> p (a k) n", p=P)
                        sp.dma_start(d[:, g], src).then_inc(s_slot[k], 16)
                else:
                    n0 = 256 * (j - 6)
                    src = moe_d[0, bass.ds(e, 1), :, n0:n0 + 256].rearrange("a (k p) n -> p (a k) n", p=P)
                    sp.dma_start(wslot(slot_unit, FE, 256), src).then_inc(s_slot[k], 16)

            def moe_freed(e, j):
                if j < 4:
                    sp.wait_ge(down_mm, 8 + 8 * (e - 1) + 2 * (j + 1))
                elif j < 10:
                    sp.wait_ge(gu_u, FG + FE * e + min(2 * (j - 3), FE))
                sp.sem_inc(sp_turn, 1)

            for j in range(4):
                freed(U_MOE + j)
                moe_load(0, j, U_MOE + j)
            with sp.Fori(0, NE // 2 - 1) as i:
                for n in range(4, 24):
                    e, j = divmod(n, MOE_U)
                    moe_freed(2 * i + e, j)
                    moe_load(2 * i + e, j, U_MOE + n)
            for n in range(4, 2 * MOE_U):
                e, j = NE - 2 + n // MOE_U, n % MOE_U
                moe_freed(e, j)
                moe_load(e, j, U_MOE + n)
            for t in range(NT):
                sp.wait_ge(xo_ev, 2 * t + 2)
                dst = y_prompt[0] if t == 0 else y_sample[0, (t - 1) * P:t * P, :]
                sp.dma_start(dst, v3(GT[:, 0:3072], NT)[:, t]).then_inc(y_out, 16)
            sp.wait_ge(y_out, 16 * NT)

        @block.gpsimd
        def _(pool):
            link = linker(pool, pool_step)

            def bc(ap, n):
                return ap.unsqueeze(2).to_broadcast([P, ap.shape[1], n])

            pool.dma_start(cst[:, :], cst_d[:, 0:NRES]).then_inc(cst_in, 16)
            pool.dma_start(RX[:, 6144:6144 + NCST - NRES], cst_d[:, NRES:NCST]).then_inc(cst_in, 16)
            st = v3(RX[:, 8192:8704], 4)
            link(nc.gpsimd.memset(st, 0.0))
            pool.dma_start(st[0:64, 0], norms.rearrange("l a (k p) -> (l a k) p", p=P)).then_inc(rows_in, 16)
            pool.dma_start(st[0:96, 1], ada_b.rearrange("l (m p) -> (l m) p", p=P)).then_inc(rows_in, 16)
            pool.dma_start(st[0:8, 2], c_ctx.rearrange("(k p) -> k p", p=P)).then_inc(rows_in, 16)
            pool.dma_start(st[8:16, 2], c.rearrange("s (k p) -> (s k) p", p=P)).then_inc(rows_in, 16)
            pool.dma_start(st[16:24, 2], gmlp_bs.rearrange("l g p -> (l g) p")).then_inc(rows_in, 16)
            pool.dma_start(st[0:120, 3], dn_conv.rearrange("l j (n p) -> (l j n) p", p=P)).then_inc(rows_in, 16)
            xtok = v3(RX[:, 3072:6144], NT)
            pool.dma_start(xtok[:, 0], x_prompt[0]).then_inc(x_in, 16)
            for t in (1, 2):
                pool.dma_start(xtok[:, t], x_sample[0, (t - 1) * P:t * P, :]).then_inc(x_in, 16)

            for layer in range(DEPTH):
                wait(pool, "x_new", layer, 0)
                for dst, src in ((v3(baw, KT), w_in[layer, :, C_BA:C_BA + 16].rearrange("(k p) n -> p k n", p=P)),
                                 (ggain, gmlp_norm[layer].partition_broadcast(P)),
                                 (qkgain, qk_norm[layer].rearrange("a d -> (a d)").partition_broadcast(P)),
                                 (expa, dn_a_log[layer].rearrange("a d -> (a d)").partition_broadcast(P)),
                                 (dtb, dn_dt_bias[layer].rearrange("a d -> (a d)").partition_broadcast(P)),
                                 (dngain[:, :], dn_norm[layer].partition_broadcast(P))):
                    pool.dma_start(dst, src).then_inc(lw_in, 16)
                if layer == 0:
                    pool.dma_start(v3(rtw[:, :], KT), router[0].rearrange("(k p) n -> p k n", p=P)).then_inc(lw_in, 16)
                pool.dma_start(wsraw, gmlp_ws[layer].rearrange("g q r -> q g r")).then_inc(cache_in, 16)
                pool.dma_start(kcache, cache_k[0, layer].rearrange("t h d -> t (h d)")).then_inc(cache_in, 16)
                pool.dma_start(vcache, cache_v[0, layer].rearrange("t h d -> t (h d)")).then_inc(cache_in, 16)
                wait(pool, "a_ok", layer, 1)
                pool.dma_start(new_k[0, layer].rearrange("t h d -> t (h d)"), qkv[:, 0, 512:768]).then_inc(kv_out, 16)
                pool.dma_start(new_v[0, layer].rearrange("t h d -> t (h d)"), qkv[:, 0, 768:1024]).then_inc(kv_out, 16)
                pool.wait_ge(kv_out, 32 * (layer + 1))
                wait(pool, "b_ev", layer, 3)
                wait(pool, "at_pv", layer, 24)
                wait(pool, "at_pt", layer, 24)
                link(nc.gpsimd.memset(state, 0.0))
                wait(pool, "kvt_ev", layer, 6)
                wait(pool, "beg", layer, 1)
                for pair in range(3):
                    for d in range(2):
                        g = 2 * pair + d
                        t = TILE[pair][d]
                        h4 = slice(4 * d, 4 * d + 4)
                        if pair:
                            wait(pool, "s_or", layer, g - 1)
                        nc.gpsimd.tensor_tensor(dn(d, B_VU), vtok[:, t], bc(beta[:, t, h4], DK), ALU.mult)
                        link(nc.gpsimd.tensor_tensor(dn(d, B_KW), ktok[:, t], bc(beg[:, t, h4], DK), ALU.mult))
                        wait(pool, "d_e", layer, g + 1)
                        nc.gpsimd.tensor_tensor(dn(d, B_M), dn(d, B_M), bc(beta[:, t, h4], P), ALU.mult)
                        incl = inclU if d == 0 else inclL
                        nc.gpsimd.tensor_tensor(dn(d, B_QK), dn(d, B_QK), incl.unsqueeze(1).to_broadcast([P, DNH, P]), ALU.mult)
                        nc.gpsimd.tensor_tensor(dn(d, B_QEG), dn(d, B_QEG), cv[:, 0:4, TCOL[t]:TCOL[t] + P],
                                                ALU.mult).then_inc(S["d_pool"], 1)
                    for s in range(1, len(LEVELS)):
                        for d in range(2):
                            g = 2 * pair + d
                            if s == 1:
                                wait(pool, "d_mtc", layer, g + 1)
                                wait(pool, "d_t1", layer, g + 1)
                            else:
                                wait(pool, "d_w", layer, 10 * pair + 2 * (s - 2) + d + 1)
                            nc.gpsimd.tensor_tensor(dn(d, B_CT), dn(d, B_MT),
                                                    lm[:, s, 1 - d].unsqueeze(1).to_broadcast([P, DNH, P]),
                                                    ALU.mult).then_inc(S["d_ct"], 1)
                    for d in range(2):
                        t = TILE[pair][d]
                        wait(pool, "d_ct", layer, 10 * pair + 8 + d + 1)
                        nc.gpsimd.tensor_tensor(dn(d, B_KD), ktok[:, t], bc(edec[:, t, 4 * d:4 * d + 4], DK),
                                                ALU.mult).then_inc(S["d_kd"], 1)
                    if pair == 0:
                        wait(pool, "s_st", layer, 4)
                        for d in range(2):
                            pool.dma_start(new_s[0, layer, d].rearrange("h k e -> k h e"), state[:, d]).then_inc(st_out, 16)
                        pool.wait_ge(st_out, 32 * (layer + 1))
                        for d in range(2):
                            pool.dma_start(state[:, d], state_in[0, layer, d].rearrange("h k e -> k h e")).then_inc(st_in, 16)
                wait(pool, "s_or", layer, 6)
                wait(pool, "s_st", layer, 12)
                wait(pool, "oc_mm", layer, 3)
                pool.dma_start(xT, xpark.rearrange("p (k n) -> p k n", k=KT)).then_inc(unparked, 16)
            pool.wait_ge(unparked, 16 * DEPTH)
            pool.wait_ge(kv_out, 32 * DEPTH)
            pool.wait_ge(st_out, 32 * DEPTH)

        @block.tensor
        def _(pe):
            mm = nc.tensor.matmul

            def tr(out, in_):
                return nc.tensor.transpose(out, in_, ident)

            def arrived(unit):
                pe.wait_ge(s_slot[slot(unit)], full(unit))

            pe.wait_ge(cst_in, 32)
            pe.wait_ge(rows_in, 96)
            st = v3(RX[:, 8192:8704], 4)
            for i in range(4):
                tr(B[0][:, i * P:(i + 1) * P], st[:, i]).then_inc(rt_mm, 1)
            pe.wait_ge(x_in, 16 * NT)
            xtok = v3(RX[:, 3072:6144], NT)
            for t in range(NT):
                for half in range(2):
                    for k in range(4):
                        last = tr(B[2 + 2 * t + half][:, k * P:(k + 1) * P], xtok[:, t, (4 * half + k) * P:(4 * half + k + 1) * P])
                    last.then_inc(xt_mm, 1)
            pe.wait_ge(sc_ok, 1)
            for layer in range(DEPTH):
                if layer:
                    pe.wait_ge(xt_ev, 2 * NT)
                dst = B[1 + layer]
                for i in range(12):
                    u = U_ADA + 12 * layer + i
                    arrived(u)
                    w = wslot(u, KT, 512)
                    for m in range(4):
                        for k in range(KT):
                            n = 2 * (4 * i + m)
                            last = mm(dst[:, n:n + 2], w[:, k, m * P:(m + 1) * P], scT[:, :, k], start=k == 0, stop=k == KT - 1)
                    last.then_inc(ada_mm, 1)

            def sum_squares(layer, q, sq):
                wait(pe, "sq", layer, q)
                for k in range(KT):
                    last = mm(B[2][:, 0:TOK], ones, sq[:, k], start=k == 0, stop=k == KT - 1)
                last.then_inc(S["stat"], 1)

            def bank_free(layer, n):
                wait(pe, "proj_ev", layer, n - 1)

            def feature_tile(layer, n, unit, m):
                bank_free(layer, n)
                w = wslot(unit, KT, 512)
                for k in range(KT):
                    last = mm(B[n % 2][:, 0:TOK], w[:, k, m * P:(m + 1) * P], hT[:, k], start=k == 0, stop=k == KT - 1)
                last.then_inc(S["proj_mm"], 1)

            def token_tiles(layer, n, unit):
                arrived(unit)
                w = wslot(unit, KT, 512)
                for t in range(NT):
                    bank_free(layer, n + t)
                    for k in range(KT):
                        last = mm(B[(n + t) % 2][:, :], hT[:, k, t * P:(t + 1) * P], w[:, k], start=k == 0, stop=k == KT - 1)
                    last.then_inc(S["proj_mm"], 1)

            for layer in range(DEPTH):
                u0 = u_layer(layer)
                wait(pe, "x_new", layer, 0)
                pe.wait_ge(mod_ok, DEPTH)
                sum_squares(layer, 1, sqT)
                wait(pe, "h_a", layer, 4)
                wait(pe, "h_v", layer, 4)
                for i in range(3):
                    arrived(u0 + i)
                    for m in range(4):
                        feature_tile(layer, 4 * i + m, u0 + i, m)
                pe.wait_ge(lw_in, 16 * (7 + 6 * layer))
                for t in range(NT):
                    n = T_BA + t
                    bank_free(layer, n)
                    for k in range(KT):
                        last = mm(B[n % 2][:, 0:16], hT[:, k, t * P:(t + 1) * P], v3(baw, KT)[:, k], start=k == 0, stop=k == KT - 1)
                    last.then_inc(S["proj_mm"], 1)
                token_tiles(layer, T_A, u0 + 3)
                token_tiles(layer, T_A + 3, u0 + 4)
                wait(pe, "dsq", layer, 1)
                for j in range(8):
                    if j >= 2:
                        wait(pe, "droot", layer, j - 1)
                    mm(B[2 + j % 2][:, 0:COUT], ones, dsq[:, j], start=True, stop=True).then_inc(S["dst"], 1)
                token_tiles(layer, T_UV, u0 + 5)
                token_tiles(layer, T_UV + 3, u0 + 6)
                wait(pe, "g_ok", layer, 1)
                for t in range(NT):
                    c0 = 32 * t
                    mm(B[4][:, c0:c0 + 4], inclU, gg[:, t, 0:4], start=True, stop=True)
                    mm(B[4][:, c0 + 4:c0 + 8], inclL, gg[:, t, 4:8], start=True, stop=True)
                    mm(B[4][:, c0 + 8:c0 + 16], same, gg[:, t], start=True, stop=True)
                    last = mm(B[4][:, c0 + 16:c0 + 32], ones, gm[:, t].rearrange("p c n -> p (c n)"), start=True, stop=True)
                last.then_inc(S["gc_mm"], 1)
                wait(pe, "qkn", layer, 1)
                wait(pe, "droot", layer, 8)
                for i, j0 in ((0, 8), (1, 4)):
                    for t in range(NT):
                        b = (5, 6, 7, 2, 3, 4)[3 * i + t]
                        if b == 4:
                            wait(pe, "gc_v", layer, 1)
                        for h in range(DNH):
                            last = tr(B[b][:, h * P:(h + 1) * P], cv[:, j0 + h, TCOL[t]:TCOL[t] + P])
                        last.then_inc(S["kvt_mm"], 1)
                wait(pe, "a_ok", layer, 1)
                pe.wait_ge(cache_in, 48 * (layer + 1))
                wait(pe, "kvt_ev", layer, 6)
                for t in range(NT):
                    for j in range(4):
                        last = tr(B[2 + t][:, j * P:(j + 1) * P], qkv[:, t, j * P:(j + 1) * P])
                    last.then_inc(S["tr_mm"], 1)
                for half in range(2):
                    for a in range(2):
                        for n in range(2):
                            src = (kcache if n else qkv[:, 0, 512:768]) if half == 0 else qkv[:, 1 + n, 512:768]
                            j = 2 * a + n
                            last = tr(B[5 + half][:, j * P:(j + 1) * P], src[:, a * P:(a + 1) * P])
                    last.then_inc(S["tr_mm"], 1)
                for g in range(4):
                    last = tr(B[7][:, g * P:(g + 1) * P], wsraw[:, g])
                last.then_inc(S["tr_mm"], 1)
                wait(pe, "tr_ev", layer, 6)
                wait(pe, "v_ok", layer, 1)
                for t in range(NT):
                    for g in range(4):
                        last = mm(B[2 + t][:, g * P:(g + 1) * P], v3(wsT, 4)[:, g], vB[:, t, g * P:(g + 1) * P], start=True, stop=True)
                    last.then_inc(S["b_mm"], 1)
                for t in range(NT):
                    wait(pe, "b_v", layer, t + 1)
                    for g in range(4):
                        last = tr(B[5 + t][:, g * P:(g + 1) * P], uB[:, t, g * P:(g + 1) * P])
                    last.then_inc(S["b_t"], 1)
                wait(pe, "b_ev", layer, 3)

                def scores(i):
                    t, h = divmod(i, HEADS)
                    a, b, cc = h // 4, h // 2 % 2, h % 2
                    if i >= 2:
                        wait(pe, "at_e", layer, i - 1)
                    keys = kTt[64 * b:64 * b + 64, a, 0:P] if t == 0 else kTt[64 * b:64 * b + 64, a, P:512]
                    q = qTt[64 * b:64 * b + 64, 2 * a + cc, t * P:(t + 1) * P]
                    mm(B[2 + i % 2][:, 0:P if t == 0 else TOK], q, keys, start=True, stop=True).then_inc(S["at_s"], 1)

                def flip(i):
                    wait(pe, "at_p", layer, i + 1)
                    if i >= 2:
                        wait(pe, "at_pt", layer, i - 1)
                    n = 1 if i < HEADS else 3
                    for kt in range(n):
                        last = tr(B[4 + i % 2][:, kt * P:(kt + 1) * P], Pb[:, i % 2, kt * P:(kt + 1) * P])
                    last.then_inc(S["at_t"], 1)

                def weigh(i):
                    t, h = divmod(i, HEADS)
                    wait(pe, "at_pt", layer, i + 1)
                    if h == 0 and t == 2:
                        wait(pe, "at_o", layer, 1)
                    g = h // 2
                    vs = [qkv[:, 0, 768:1024]] if t == 0 else [vcache, qkv[:, 1, 768:1024], qkv[:, 2, 768:1024]]
                    out = B[6 + t % 2][64 * (h % 2):64 * (h % 2) + 64, (h // 2) * P:(h // 2 + 1) * P]
                    for kt, v in enumerate(vs):
                        last = mm(out, v[:, HD * g:HD * (g + 1)], PTb[:, i % 2, kt * P:(kt + 1) * P],
                                  start=kt == 0, stop=kt == len(vs) - 1)
                    last.then_inc(S["at_pv"], 1)

                for i in range(NT * HEADS + 2):
                    if i < NT * HEADS:
                        scores(i)
                    if 1 <= i <= NT * HEADS:
                        flip(i - 1)
                    if i >= 2:
                        weigh(i - 2)

                nfill = [0]

                def fill():
                    n = nfill[0]
                    nfill[0] += 1
                    if n % 4 == 0:
                        arrived(u0 + 7 + n // 4)
                    feature_tile(layer, T_G + n, u0 + 7 + n // 4, n % 4)

                wait(pe, "at_o", layer, 3)
                for pair in range(3):
                    fill()
                    for d in range(2):
                        t = TILE[pair][d]
                        g = 2 * pair + d
                        X, Y, Z = B[2 + 3 * d], B[3 + 3 * d], B[4 + 3 * d]
                        if pair:
                            wait(pe, "s_or", layer, g - 1)
                        cols = slice(TCOL[t], TCOL[t] + P)
                        for h in range(DNH):
                            hs = slice(h * P, (h + 1) * P)
                            mm(X[:, hs], gg[:, t, 4 * d + h:4 * d + h + 1].to_broadcast([P, P]), inclU if d == 0 else inclL, start=True, stop=True)
                        for h in range(DNH):
                            hs = slice(h * P, (h + 1) * P)
                            mm(Y[:, hs], cv[:, 4 + h, cols], cv[:, 4 + h, cols], start=True, stop=True)
                        for h in range(DNH):
                            hs = slice(h * P, (h + 1) * P)
                            last = mm(Z[:, hs], cv[:, 4 + h, cols], cv[:, h, cols], start=True, stop=True)
                        last.then_inc(S["d_in"], 1)
                    fill()
                    for d in range(2):
                        wait(pe, "d_m", layer, 2 * pair + d + 1)
                        for h in range(DNH):
                            last = tr(B[2 + 3 * d][:, h * P:(h + 1) * P], dn(d, B_M)[:, h])
                        last.then_inc(S["d_mt"], 1)
                    for s in range(1, len(LEVELS)):
                        fill()
                        for d in range(2):
                            n = 10 * pair + 2 * (s - 1) + d + 1
                            wait(pe, "d_ct", layer, n)
                            if s == 1:
                                wait(pe, "d_t1", layer, 2 * pair + d + 1)
                            else:
                                wait(pe, "d_up", layer, n - 2)
                            for h in range(DNH):
                                last = mm(B[2 + 3 * d][:, h * P:(h + 1) * P], dn(d, B_CT)[:, h], dn(d, B_T)[:, h], start=True, stop=True)
                            last.then_inc(S["d_w"], 1)
                        for d in range(2):
                            n = 10 * pair + 2 * (s - 1) + d + 1
                            wait(pe, "d_we", layer, n)
                            for h in range(DNH):
                                hs = slice(h * P, (h + 1) * P)
                                if s < len(LEVELS) - 1:
                                    mm(B[3 + 3 * d][:, hs], dn(d, B_U)[:, h], dn(d, B_W)[:, h], start=True, stop=True)
                            for h in range(DNH):
                                hs = slice(h * P, (h + 1) * P)
                                last = mm(B[4 + 3 * d][:, hs], dn(d, B_W)[:, h], dn(d, B_U)[:, h], start=True, stop=True)
                            last.then_inc(S["d_du"], 1)
                    for d in range(2):
                        g = 2 * pair + d
                        wait(pe, "d_up", layer, 10 * pair + 8 + d + 1)
                        for h in range(DNH):
                            mm(B[2 + 3 * d][:, h * P:(h + 1) * P], dn(d, B_U)[:, h], dn(d, B_VU)[:, h], start=True, stop=True)
                        for h in range(DNH):
                            last = mm(B[3 + 3 * d][:, h * P:(h + 1) * P], dn(d, B_KW)[:, h], dn(d, B_U)[:, h], start=True, stop=True)
                        last.then_inc(S["d_uw"], 1)
                    for step in range(2):
                        for d in range(2):
                            g, n = 2 * pair + d, 4 * pair + 2 * step + d
                            X = B[2 + 3 * d]
                            ch = step if d == 0 else 1 - step
                            r = slice(CHUNK * ch, CHUNK * (ch + 1))
                            wait(pe, "d_uwe", layer, g + 1)
                            if step:
                                wait(pe, "s_st", layer, n - 1)
                            elif pair == 1:
                                pe.wait_ge(st_in, 32 * (layer + 1))
                            for h in range(DNH):
                                last = mm(X[r, h * P:(h + 1) * P], dn(d, B_KW)[:, h, r], state[:, d, h], start=True, stop=True)
                            last.then_inc(S["s_ws"], 1)
                        if step == 0:
                            fill()
                        for d in range(2):
                            g, n = 2 * pair + d, 4 * pair + 2 * step + d
                            Y, Z = B[3 + 3 * d], B[4 + 3 * d]
                            ch = step if d == 0 else 1 - step
                            r = slice(CHUNK * ch, CHUNK * (ch + 1))
                            wait(pe, "s_vn", layer, n + 1)
                            wait(pe, "d_kd", layer, g + 1)
                            for h in range(DNH):
                                mm(Z[:, h * P:(h + 1) * P], dn(d, B_KD)[r, h], dn(d, B_VN)[r, h], start=True, stop=True)
                            for h in range(DNH):
                                hs = slice(h * P, (h + 1) * P)
                                mm(Y[r, hs], dn(d, B_QEG)[:, h, r], state[:, d, h], start=True, stop=False)
                                last = mm(Y[r, hs], dn(d, B_QK)[r, h, r], dn(d, B_VN)[r, h], start=False, stop=True)
                            last.then_inc(S["s_o"], 1)
                assert nfill[0] == 24
                wait(pe, "s_or", layer, 6)
                token_tiles(layer, T_Z, u0 + 13)
                for t in range(NT):
                    if t == 0:
                        wait(pe, "oc_v", layer, 1)
                    for h in range(DNH):
                        last = tr(B[2 + t][:, h * P:(h + 1) * P], osum[:, t, h * P:(h + 1) * P])
                    last.then_inc(S["oc_mm"], 1)
                wait(pe, "oc_ev", layer, 3)
                for m in range(8):
                    if m % 2 == 0:
                        arrived(u0 + 14 + m // 2)
                    if m >= 2:
                        wait(pe, "br_ev", layer, m - 1)
                    w = wslot(u0 + 14 + m // 2, 12, 256)
                    for b in range(3):
                        for k in range(4):
                            last = mm(B[2 + 3 * (m % 2) + b][:, 0:TOK], w[:, 4 * b + k, (m % 2) * P:(m % 2 + 1) * P], oT[:, b, k],
                                      start=k == 0, stop=k == 3)
                    last.then_inc(S["br_mm"], 1)
                wait(pe, "br_ev", layer, 8)
                for m in range(8):
                    if m % 4 == 0:
                        arrived(u0 + 18 + m // 4)
                    if m >= 2:
                        wait(pe, "wo_ev", layer, m - 1)
                    w = wslot(u0 + 18 + m // 4, KT, 512)
                    for k in range(KT):
                        last = mm(B[m % 2][:, 0:TOK], w[:, k, (m % 4) * P:(m % 4 + 1) * P], merged[:, k], start=k == 0, stop=k == KT - 1)
                    last.then_inc(S["wo_mm"], 1)
                sum_squares(layer, 2, sqP)
                sum_squares(layer, 3, sqT)
                wait(pe, "h_a", layer, 8)
                wait(pe, "h_v", layer, 8)

                def gate_up(i, r, n, slot_unit, w0):
                    k0 = slot(slot_unit) * SLOT
                    w = ring[:, k0:k0 + 16 * n].rearrange("p (g k n) -> p g k n", g=2, k=KT)
                    for g, (done, used) in enumerate(((gu_g, gu_s), (gu_u, gu_h))):
                        if w0 is not None:
                            pe.wait_ge(used, w0)
                        for k in range(KT):
                            last = mm(B[2 * g + r][:, 0:TOK], w[:, g, k, (r % (n // P)) * P:(r % (n // P) + 1) * P], hT[:, k],
                                      start=k == 0, stop=k == KT - 1)
                        last.then_inc(done, 1)

                if layer == 0:
                    for i in range(3):
                        arrived(U_DENSE + i)
                        for r in range(2):
                            gate_up(2 * i + r, r, 256, U_DENSE + i, 2 * i + r - 1 if i else None)
                    with pe.Fori(0, 2) as it:
                        for j in range(4):
                            u = U_DENSE + 3 + j
                            pe.wait_ge(s_slot[slot(u)], full(u) + (full(u + 4) - full(u)) * it)
                            for r in range(2):
                                gate_up(0, r, 256, u, 8 * it + 6 + 2 * j + r - 1)
                    pe.wait_ge(gu_h, FG)
                    for m in range(8):
                        u = U_DENSE + 11 + m
                        arrived(u)
                        if m >= 2:
                            pe.wait_ge(down_ev, m - 1)
                        w = wslot(u, FG, P)
                        for k in range(FG):
                            last = mm(B[4 + m % 2][:, 0:TOK], w[:, k], hid[:, k], start=k == 0, stop=k == FG - 1)
                        last.then_inc(down_mm, 1)
                else:
                    for t in range(NT):
                        for k in range(KT):
                            last = mm(B[6][:, NE * t:NE * (t + 1)], hT[:, k, t * P:(t + 1) * P], v3(rtw[:, :], KT)[:, k],
                                      start=k == 0, stop=k == KT - 1)
                    last.then_inc(rl_mm, 1)
                    pe.wait_ge(rl_ok, 1)
                    for e in range(NE):
                        for t in range(NT):
                            n = NT * e + t
                            last = mm(B[2 + n // 4][:, (n % 4) * P:(n % 4 + 1) * P], comb[:, t, e:e + 1].to_broadcast([P, P]), ident,
                                      start=True, stop=True)
                            if n % 4 == 3:
                                last.then_inc(rb_mm, 1)
                    pe.wait_ge(rb_ev, 6)
                    with pe.Fori(0, NE // 2) as it:
                        for e2 in range(2):
                            e = 2 * it + e2
                            for i in range(FE):
                                u = U_MOE + MOE_U * e2 + i // 2
                                if i % 2 == 0:
                                    pe.wait_ge(s_slot[slot(u)], full(u) + (full(u + 2 * MOE_U) - full(u)) * it)
                                gate_up(i, i % 2, 256 if i < FE - 1 else P, u, FG + FE * e + i - 1)
                            pe.wait_ge(gu_h, FG + FE * e + FE)
                            for m in range(8):
                                u = U_MOE + MOE_U * e2 + 6 + m // 2
                                if m % 2 == 0:
                                    pe.wait_ge(s_slot[slot(u)], full(u) + (full(u + 2 * MOE_U) - full(u)) * it)
                                pe.wait_ge(down_ev, 8 + 8 * e + m - 1)
                                w = wslot(u, FE, 256)
                                for k in range(FE):
                                    last = mm(B[4 + m % 2][:, 0:TOK], w[:, k, (m % 2) * P:(m % 2 + 1) * P], hid[:, k],
                                              start=k == 0, stop=k == FE - 1)
                                last.then_inc(down_mm, 1)
                sum_squares(layer, 4, sqP)
            wait(pe, "x_new", DEPTH, 0)
            for t in range(NT):
                for half in range(2):
                    for k in range(4):
                        last = tr(B[2 + 2 * t + half][:, k * P:(k + 1) * P], xT[:, 4 * half + k, t * P:(t + 1) * P])
                    last.then_inc(xo_mm, 1)

        @block.scalar
        def _(act):
            go = nc.scalar.activation
            link = linker(act, act_step)

            def copy(out, in_):
                return go(out, in_, ACT.Copy)

            act.wait_ge(rt_ev, 4)
            go(rows[:, 160:176], rows[:, 160:176], ACT.Silu).then_inc(sc_ok, 1)
            for t in range(NT):
                for half in range(2):
                    act.wait_ge(xt_mm, 2 * t + half + 1)
                    copy(xT[:, 4 * half:4 * half + 4, t * P:(t + 1) * P], v3(B[2 + 2 * t + half][:, :], 4)).then_inc(xt_ev, 1)

            def square(src, dst):
                go(dst, src, ACT.Square).then_inc(S["sq"], 1)

            def root(layer, q):
                wait(act, "stat", layer, q)
                go(rs[:, :], B[2][:, 0:TOK], ACT.Sqrt, bias=eps1, scale=1.0 / D).then_inc(S["root"], 1)

            def modulate(layer, q, a):
                wait(act, "xn", layer, q)
                act.wait_ge(mod_ok, layer + 1)
                for k in range(4):
                    for s, lo, hi in SEG:
                        last = go(hT[:, k, lo:hi], hT[:, k, lo:hi], ACT.Identity, bias=mod[:, layer, a, k, s:s + 1],
                                  scale=mod[:, layer, a + 1, k, s:s + 1])
                    last.then_inc(S["h_a"], 1)

            act.wait_ge(xt_ev, 2 * NT)
            for layer in range(DEPTH):
                def evac(n, out, func=ACT.Copy, width=512):
                    wait(act, "proj_mm", layer, n + 1)
                    go(out, B[n % 2][:, 0:width], func).then_inc(S["proj_ev"], 1)

                wait(act, "x_new", layer, 0)
                square(xT, sqT)
                root(layer, 1)
                modulate(layer, 1, 0)
                wait(act, "pads", layer, 1)
                for j in range(12):
                    wait(act, "proj_mm", layer, j + 1)
                    copy(pre[:, j, 2:2 + CTX], B[j % 2][:, 0:CTX])
                    copy(pre[:, j, CTX + 6:CTX + 6 + LAT], B[j % 2][:, CTX:TOK]).then_inc(S["proj_ev"], 1)
                for t in range(NT):
                    evac(T_BA + t, ba[:, t], width=16)
                act.wait_ge(parked, 16 * (layer + 1))
                for t in range(NT):
                    wait(act, "proj_mm", layer, T_A + t + 1)
                    for a in range(2):
                        src = B[(T_A + t) % 2][:, 256 * a:256 * a + 256].rearrange("p (b c d) -> p b c d", b=2, c=2)
                        dst = qkv[:, t, 256 * a:256 * a + 256].rearrange("p (c b d) -> p b c d", b=2, c=2)
                        last = copy(dst, src)
                    last.then_inc(S["proj_ev"], 1)
                for t in range(NT):
                    evac(T_A + 3 + t, qkv[:, t, 512:1024])
                wait(act, "proj_ev", layer, T_A + 6)
                go(asq, qkv[:, :, 0:768], ACT.Square).then_inc(S["a_sq"], 1)
                go(beta, ba[:, :, 0:8], ACT.Sigmoid)
                act.wait_ge(lw_in, 16 * (7 + 6 * layer))
                wait(act, "ba_v", layer, 1)
                link(go(t2, t1, ACT.Abs))
                link(go(t2, t2, ACT.Exp, scale=-1.0))
                go(expa, expa, ACT.Exp)
                go(t2, t2, ACT.Ln, bias=one1).then_inc(S["ba_l"], 1)
                wait(act, "conv", layer, 12)
                for i in range(3):
                    last = go(CV[:, 4 * i * COUT:4 * (i + 1) * COUT], CV[:, 4 * i * COUT:4 * (i + 1) * COUT], ACT.Silu)
                    last.then_inc(S["silu"], 1)
                wait(act, "silu", layer, 3)
                go(GT[:, 12 * CROW:12 * CROW + 8 * COUT], CV[:, 0:8 * COUT], ACT.Square).then_inc(S["dsq"], 1)
                for j in range(8):
                    wait(act, "dst", layer, j + 1)
                    go(dsq[:, j], B[2 + j % 2][:, 0:COUT], ACT.Sqrt, bias=eps128 if j < 4 else eps1,
                       scale=float(DK) if j < 4 else 1.0).then_inc(S["droot"], 1)
                wait(act, "a_ss", layer, 1)
                go(ass, ass, ACT.Sqrt, bias=eps1, scale=1.0 / HD).then_inc(S["a_rt"], 1)
                for i in range(6):
                    evac(T_UV + i, uB[:, i] if i < 3 else vB[:, i - 3], ACT.Gelu_apprx_tanh)
                wait(act, "proj_ev", layer, T_UV + 6)
                wait(act, "qkn", layer, 1)
                for t in range(NT):
                    link(go(gsc, vB[:, t], ACT.Square, accum_out=vss[:, t:t + 1]))
                go(vss, vss, ACT.Sqrt, bias=eps1, scale=1.0 / 512).then_inc(S["v_rt"], 1)
                wait(act, "gc_v", layer, 1)
                go(edec, edec, ACT.Exp)
                go(egl, egl, ACT.Exp)
                go(eg, gcs, ACT.Exp).then_inc(S["gc_e"], 1)
                wait(act, "kvt_mm", layer, 3)
                for i in range(6):
                    wait(act, "kvt_mm", layer, i + 1)
                    dst = vtok[:, i] if i < 3 else ktok[:, i - 3]
                    copy(dst, v3(B[(5, 6, 7, 2, 3, 4)[i]][:, :], 4)).then_inc(S["kvt_ev"], 1)
                for i in range(6):
                    wait(act, "tr_mm", layer, i + 1)
                    if i < 3:
                        copy(qTt[:, :, i * P:(i + 1) * P], v3(B[2 + i][:, :], 4)).then_inc(S["tr_ev"], 1)
                    elif i < 5:
                        copy(kTt[:, :, 256 * (i - 3):256 * (i - 2)], v3(B[2 + i][:, :], 2)).then_inc(S["tr_ev"], 1)
                    else:
                        copy(wsT, B[7][:, :]).then_inc(S["tr_ev"], 1)
                for t in range(NT):
                    wait(act, "b_t", layer, t + 1)
                    copy(oT[:, 1, :, t * P:(t + 1) * P], v3(B[5 + t][:, :], 4)).then_inc(S["b_ev"], 1)
                n_at = NT * HEADS
                for i in range(n_at + 3):
                    if i < n_at:
                        w = P if i < HEADS else TOK
                        wait(act, "at_m", layer, i + 1)
                        if i >= 2:
                            wait(act, "at_t", layer, i - 1)
                        go(Pb[:, i % 2, 0:w], B[2 + i % 2][:, 0:w], ACT.Exp, bias=anm[:, i:i + 1], scale=HD ** -0.5,
                           accum_out=ars[:, i:i + 1]).then_inc(S["at_e"], 1)
                    if 1 <= i <= n_at:
                        j = i - 1
                        w = P if j < HEADS else TOK
                        wait(act, "at_t", layer, j + 1)
                        if j >= 2:
                            wait(act, "at_pv", layer, j - 1)
                        copy(PTb[:, j % 2, 0:w], B[4 + j % 2][:, 0:w]).then_inc(S["at_pt"], 1)
                    if i >= 10 and i % 8 == 2:
                        t = i // 8 - 1
                        wait(act, "at_pv", layer, 8 * (t + 1))
                        copy(oT[:, 0, :, t * P:(t + 1) * P], v3(B[6 + t % 2][:, :], 4)).then_inc(S["at_o"], 1)
                nfill = [0]

                def gate():
                    n = nfill[0]
                    nfill[0] += 1
                    evac(T_G + n, gates[:, n], width=TOK)

                for pair in range(3):
                    gate()
                    for d in range(2):
                        wait(act, "d_d0", layer, 2 * pair + d + 1)
                        go(dn(d, B_QEG), v3(B[2 + 3 * d][:, :], 4), ACT.Exp)
                        go(dn(d, B_M), dn(d, B_M), ACT.Exp, scale=-1.0)
                        go(dn(d, B_QK), dn(d, B_QK), ACT.Exp).then_inc(S["d_e"], 1)
                    gate()
                    for s in range(1, len(LEVELS)):
                        gate()
                        for d in range(2):
                            wait(act, "d_w", layer, 10 * pair + 2 * (s - 1) + d + 1)
                            copy(dn(d, B_W), v3(B[2 + 3 * d][:, :], 4)).then_inc(S["d_we"], 1)
                    for d in range(2):
                        wait(act, "d_uw", layer, 2 * pair + d + 1)
                        copy(dn(d, B_VU), v3(B[2 + 3 * d][:, :], 4))
                        copy(dn(d, B_KW), v3(B[3 + 3 * d][:, :], 4)).then_inc(S["d_uwe"], 1)
                    gate()
                for t in range(NT):
                    evac(T_Z + t, zs[:, t], ACT.Silu)
                go(RX[:, 6144:7680], OT[:, 3072:4608], ACT.Square).then_inc(S["oc_sq"], 1)
                wait(act, "oc_ss", layer, 1)
                go(oss, oss, ACT.Sqrt, bias=eps1, scale=1.0 / DK).then_inc(S["oc_rt"], 1)
                wait(act, "proj_ev", layer, T_Z)
                go(GT[:, :], GT[:, :], ACT.Sigmoid).then_inc(S["gsig"], 1)
                wait(act, "oc_mm", layer, 3)
                for t in range(NT):
                    copy(oT[:, 2, :, t * P:(t + 1) * P], v3(B[2 + t][:, :], 4)).then_inc(S["oc_ev"], 1)
                for m in range(8):
                    wait(act, "wo_mm", layer, m + 1)
                    copy(yT[:, m], B[m % 2][:, 0:TOK]).then_inc(S["wo_ev"], 1)
                wait(act, "wo_ev", layer, 8)
                square(yT, sqP)
                root(layer, 2)
                wait(act, "x_new", layer, 1)
                square(xT, sqT)
                root(layer, 3)
                modulate(layer, 2, 3)

                def silu(idx, r, prev):
                    act.wait_ge(gu_g, idx + 1)
                    if prev is not None:
                        act.wait_ge(gu_h, prev)
                    go(sgb[:, r], B[r][:, 0:TOK], ACT.Silu).then_inc(gu_s, 1)

                if layer == 0:
                    for i in range(6):
                        silu(i, i % 2, i - 1 if i >= 2 else None)
                    with act.Fori(0, 2) as it:
                        for i in range(8):
                            silu(8 * it + 6 + i, i % 2, 8 * it + 5 + i)
                    act.wait_ge(down_ev, 8)
                else:
                    act.wait_ge(rl_c, 1)
                    go(m8[:, 1::8], m8[:, 1::8], ACT.Exp).then_inc(rl_e, 1)
                    for n in range(6):
                        act.wait_ge(rb_mm, n + 1)
                        copy(GT[:, 4224 + 512 * n:4224 + 512 * (n + 1)], B[2 + n][:, :]).then_inc(rb_ev, 1)
                    with act.Fori(0, NE) as e:
                        for i in range(FE):
                            silu(FG + FE * e + i, i % 2, FG + FE * e + (i - 1 if i else 0))
                    act.wait_ge(down_ev, 8 + 8 * NE)
                square(yT, sqP)
                root(layer, 4)
            for t in range(NT):
                for half in range(2):
                    act.wait_ge(xo_mm, 2 * t + half + 1)
                    copy(v3(GT[:, 0:3072], NT)[:, t, 512 * half:512 * (half + 1)], B[2 + 2 * t + half][:, :]).then_inc(xo_ev, 1)

        @block.vector
        def _(dve):
            v = nc.vector
            link = linker(dve, dve_step)

            def note(ins, name, layer, n):
                ins.then_inc(S[name], 1)
                wait(dve, name, layer, n)

            def bc(ap, n):
                return ap.unsqueeze(2).to_broadcast([P, ap.shape[1], n])

            dve.wait_ge(cst_in, 32)
            v.tensor_copy(lmask[:, :], RX[:, 6144:6144 + NCST - NRES]).then_inc(bf_ok, 1)
            for i, (lo, n) in enumerate(((0, 64), (64, 96), (160, 24), (184, 120))):
                dve.wait_ge(rt_mm, 4)
                v.tensor_copy(rows[:, lo:lo + n], B[0][:, i * P:i * P + n]).then_inc(rt_ev, 1)
            dve.wait_ge(rt_ev, 4)
            for layer in range(DEPTH):
                dve.wait_ge(ada_mm, 12 * (layer + 1))
                m = mod[:, layer]
                link(v.tensor_tensor(m.rearrange("p a k s -> p (a k) s"), v3(B[1 + layer][:, 0:96], 48), bc(adab[:, layer], 2), ALU.add))
                for a, n in ((1, 0), (4, 2)):
                    link(v.tensor_scalar(m[:, a], m[:, a], 1.0, None, ALU.add))
                for a, n in ((1, 0), (2, 1), (4, 2), (5, 3)):
                    last = v.tensor_tensor(m[:, a], m[:, a], bc(nrmT[:, layer, n], 2), ALU.mult)
                    if a == 5:
                        last.then_inc(mod_ok, 1)
            dve.wait_ge(mod_ok, DEPTH)
            dve.wait_ge(xt_ev, 2 * NT)

            def rstd(layer, q):
                wait(dve, "root", layer, q)
                note(v.reciprocal(rs[:, :], rs[:, :]), "rinv", layer, q)

            def normed(layer, n, a):
                note(v.tensor_tensor(hT, xT, rs[:, :].unsqueeze(1).to_broadcast([P, KT, TOK]), ALU.mult), "xn", layer, n)
                for k in range(4, 8):
                    for s, lo, hi in SEG:
                        last = v.tensor_scalar(hT[:, k, lo:hi], hT[:, k, lo:hi], mod[:, layer, a + 1, k, s:s + 1],
                                               mod[:, layer, a, k, s:s + 1], ALU.mult, ALU.add)
                    last.then_inc(S["h_v"], 1)

            def add_branch(layer, q, a, n):
                rstd(layer, q)
                link(v.tensor_tensor(yT, yT, rs[:, :].unsqueeze(1).to_broadcast([P, KT, TOK]), ALU.mult))
                for k in range(KT):
                    for s, lo, hi in SEG:
                        last = v.scalar_tensor_tensor(xT[:, k, lo:hi], yT[:, k, lo:hi], mod[:, layer, a, k, s:s + 1], xT[:, k, lo:hi],
                                                      ALU.mult, ALU.add)
                note(last, "x_new", layer, n)

            for layer in range(DEPTH):
                rstd(layer, 1)
                normed(layer, 1, 0)
                v.memset(pre[:, :, 0:2], 0.0)
                v.memset(pre[:, :, CTX + 2:CTX + 6], 0.0)
                note(v.memset(pre[:, :, CROW - 2:CROW], 0.0), "pads", layer, 1)
                for j in range(12):
                    wait(dve, "proj_ev", layer, j + 1)
                    w = cwT[:, layer, :, j]
                    link(v.tensor_scalar(cv[:, j], pre[:, j, 0:COUT], w[:, 0:1], None, ALU.mult))
                    for k in range(1, CONV_K):
                        ins = v.scalar_tensor_tensor(cv[:, j], pre[:, j, k:k + COUT], w[:, k:k + 1], cv[:, j], ALU.mult, ALU.add)
                        if k < CONV_K - 1:
                            link(ins)
                    ins.then_inc(S["conv"], 1)
                wait(dve, "proj_ev", layer, T_BA + 3)
                dve.wait_ge(lw_in, 16 * (7 + 6 * layer))
                note(v.tensor_tensor(t1, ba[:, :, 8:16], dtb.unsqueeze(1).to_broadcast([P, NT, 8]), ALU.add), "ba_v", layer, 1)
                wait(dve, "a_sq", layer, 1)
                v.tensor_reduce(ass, asq.rearrange("p t (h d) -> p (t h) d", d=HD), AX.X, ALU.add).then_inc(S["a_ss"], 1)
                wait(dve, "ba_l", layer, 1)
                link(v.scalar_tensor_tensor(gg, t1, 0.0, t2, ALU.max, ALU.add))
                link(v.scalar_tensor_tensor(gg, gg, -1.0, expa.unsqueeze(1).to_broadcast([P, NT, 8]), ALU.mult, ALU.mult))
                v.tensor_scalar(gm[:, :, 0], gg, chsel[:, 0:1], None, ALU.mult)
                v.tensor_scalar(gm[:, :, 1], gg, chsel[:, 1:2], None, ALU.mult).then_inc(S["g_ok"], 1)
                wait(dve, "droot", layer, 8)
                link(v.reciprocal(dsq, dsq))
                v.tensor_tensor(cv[:, 0:8], cv[:, 0:8], dsq, ALU.mult).then_inc(S["qkn"], 1)
                wait(dve, "a_rt", layer, 1)
                link(v.reciprocal(ass, ass))
                qk = qkv[:, :, 0:768].rearrange("p t (h d) -> p t h d", d=HD)
                link(v.tensor_tensor(qk, qk, v3(ass, NT).unsqueeze(3).to_broadcast([P, NT, 12, HD]), ALU.mult))
                for t in range(NT):
                    q2 = qkv[:, t, 0:768].rearrange("p (h d) -> p h d", d=HD)
                    v.tensor_tensor(q2[:, 0:8], q2[:, 0:8], qkgain[:, 0:64].unsqueeze(1).to_broadcast([P, 8, HD]), ALU.mult)
                    last = v.tensor_tensor(q2[:, 8:12], q2[:, 8:12], qkgain[:, 64:128].unsqueeze(1).to_broadcast([P, 4, HD]), ALU.mult)
                link(last)
                for t in (1, 2):
                    q5 = qkv[:, t, 0:768].rearrange("p (h a f q) -> p h a f q", h=12, a=2, f=2)
                    x1, x2 = q5[:, :, :, 0], q5[:, :, :, 1]
                    cos, sin = (rope[:, t - 1, f].unsqueeze(1).to_broadcast([P, 12, 2, HD // 4]) for f in range(2))
                    for o, x, f in ((rt[0], x1, cos), (rt[1], x2, sin), (rt[2], x1, sin), (rt[3], x2, cos)):
                        last = v.tensor_tensor(o, x, f, ALU.mult)
                    link(last)
                    v.tensor_tensor(x1, rt[0], rt[1], ALU.subtract)
                    last = v.tensor_tensor(x2, rt[2], rt[3], ALU.add)
                    if t == 1:
                        link(last)
                last.then_inc(S["a_ok"], 1)
                wait(dve, "v_rt", layer, 1)
                link(v.reciprocal(vss, vss))
                for t in range(NT):
                    last = v.scalar_tensor_tensor(vB[:, t], vB[:, t], vss[:, t:t + 1], ggain, ALU.mult, ALU.mult)
                last.then_inc(S["v_ok"], 1)
                wait(dve, "gc_mm", layer, 1)
                gps = B[4][:, 0:96].rearrange("p (t n) -> p t n", t=NT)
                link(v.tensor_copy(gcs, gps[:, :, 0:8]))
                v.tensor_tensor(edec, gps[:, :, 8:16], gcs, ALU.subtract)
                v.tensor_copy(egl.rearrange("p t c n -> p t (c n)"), gps[:, :, 16:32]).then_inc(S["gc_v"], 1)
                wait(dve, "gc_e", layer, 1)
                v.tensor_tensor(beg, beta, eg, ALU.mult).then_inc(S["beg"], 1)
                for t in range(NT):
                    wait(dve, "b_mm", layer, t + 1)
                    for g in range(4):
                        gs = slice(g * P, (g + 1) * P)
                        last = v.scalar_tensor_tensor(uB[:, t, gs], B[2 + t][:, gs], bsT[:, layer, g:g + 1], uB[:, t, gs],
                                                      ALU.add, ALU.mult)
                    last.then_inc(S["b_v"], 1)
                n_at = NT * HEADS
                for i in range(n_at + 1):
                    if i < n_at:
                        w = P if i < HEADS else TOK
                        wait(dve, "at_s", layer, i + 1)
                        link(v.tensor_reduce(amx[:, i:i + 1], B[2 + i % 2][:, 0:w], AX.X, ALU.max))
                        v.tensor_scalar(anm[:, i:i + 1], amx[:, i:i + 1], -(HD ** -0.5), None, ALU.mult).then_inc(S["at_m"], 1)
                    if i:
                        j = i - 1
                        w = P if j < HEADS else TOK
                        wait(dve, "at_e", layer, j + 1)
                        link(v.reciprocal(ars[:, j:j + 1], ars[:, j:j + 1]))
                        v.tensor_scalar(Pb[:, j % 2, 0:w], Pb[:, j % 2, 0:w], ars[:, j:j + 1], None, ALU.mult).then_inc(S["at_p"], 1)
                dve.wait_ge(kv_out, 32 * (layer + 1))
                wait(dve, "at_o", layer, 3)
                dve.wait_ge(bf_ok, 1)
                for pair in range(3):
                    for d in range(2):
                        t = TILE[pair][d]
                        wait(dve, "d_in", layer, 2 * pair + d + 1)
                        link(v.tensor_tensor(dn(d, B_W), v3(B[2 + 3 * d][:, :], 4), bc(gcs[:, t, 4 * d:4 * d + 4], P), ALU.subtract))
                        v.tensor_scalar(dn(d, B_M), dn(d, B_W), 0.0, None, ALU.max)
                        v.tensor_scalar(dn(d, B_QK), dn(d, B_W), 0.0, None, ALU.min).then_inc(S["d_d0"], 1)
                    for d in range(2):
                        wait(dve, "d_pool", layer, 2 * pair + d + 1)
                        v.tensor_tensor(dn(d, B_QK), v3(B[4 + 3 * d][:, :], 4), dn(d, B_QK), ALU.mult)
                        v.tensor_tensor(dn(d, B_M), v3(B[3 + 3 * d][:, :], 4), dn(d, B_M), ALU.mult).then_inc(S["d_m"], 1)
                    for d in range(2):
                        g = 2 * pair + d
                        m0, m1 = (lm[:, 0, i].unsqueeze(1).to_broadcast([P, DNH, P]) for i in (d, 1 - d))
                        eye = ident.unsqueeze(1).to_broadcast([P, DNH, P])
                        wait(dve, "d_mt", layer, g + 1)
                        note(v.tensor_copy(dn(d, B_MT), v3(B[2 + 3 * d][:, :], 4)), "d_mtc", layer, g + 1)
                        v.tensor_tensor(dn(d, B_T), dn(d, B_M), m0, ALU.mult)
                        link(v.tensor_tensor(dn(d, B_U), dn(d, B_MT), m1, ALU.mult))
                        v.tensor_tensor(dn(d, B_T), dn(d, B_T), eye, ALU.add)
                        v.tensor_tensor(dn(d, B_U), dn(d, B_U), eye, ALU.add).then_inc(S["d_t1"], 1)
                    dve.wait_ge(S["d_t1"], PER["d_t1"] * layer + 2 * pair + 2)
                    for s in range(1, len(LEVELS)):
                        for d in range(2):
                            n = 10 * pair + 2 * (s - 1) + d + 1
                            wait(dve, "d_du", layer, n)
                            if s < len(LEVELS) - 1:
                                v.tensor_tensor(dn(d, B_T), dn(d, B_T), v3(B[3 + 3 * d][:, :], 4), ALU.add)
                            note(v.tensor_tensor(dn(d, B_U), dn(d, B_U), v3(B[4 + 3 * d][:, :], 4), ALU.add), "d_up", layer, n)
                    for step in range(2):
                        for d in range(2):
                            n = 4 * pair + 2 * step + d
                            ch = step if d == 0 else 1 - step
                            r = slice(CHUNK * ch, CHUNK * (ch + 1))
                            wait(dve, "s_ws", layer, n + 1)
                            v.tensor_tensor(dn(d, B_VN)[r], dn(d, B_VU)[r], v3(B[2 + 3 * d][r, :], 4), ALU.subtract).then_inc(S["s_vn"], 1)
                        for d in range(2):
                            n = 4 * pair + 2 * step + d
                            t = TILE[pair][d]
                            ch = step if d == 0 else 1 - step
                            wait(dve, "s_o", layer, n + 1)
                            for h in range(DNH):
                                last = v.scalar_tensor_tensor(state[:, d, h], state[:, d, h], egl[:, t, ch, 4 * d + h:4 * d + h + 1],
                                                              B[4 + 3 * d][:, h * P:(h + 1) * P], ALU.mult, ALU.add)
                            note(last, "s_st", layer, n + 1)
                    for d in range(2):
                        t = TILE[pair][d]
                        if pair == 1 or (pair == 0 and d == 0):
                            ins = v.tensor_copy(osum[:, t], B[3 + 3 * d][:, :])
                        else:
                            ins = v.tensor_tensor(osum[:, t], B[3 + 3 * d][:, :], osum[:, t], ALU.add)
                        note(ins, "s_or", layer, 2 * pair + d + 1)
                wait(dve, "oc_sq", layer, 1)
                v.tensor_reduce(oss, RX[:, 6144:7680].rearrange("p (n e) -> p n e", e=DK), AX.X, ALU.add).then_inc(S["oc_ss"], 1)
                wait(dve, "oc_rt", layer, 1)
                link(v.reciprocal(oss, oss))
                o12 = OT[:, 3072:4608].rearrange("p (n e) -> p n e", e=DK)
                link(v.tensor_tensor(o12, o12, bc(oss, DK), ALU.mult))
                link(v.tensor_tensor(o12, o12, dngain[:, :].unsqueeze(1).to_broadcast([P, 12, DK]), ALU.mult))
                wait(dve, "proj_ev", layer, T_Z + 3)
                v.tensor_tensor(osum, osum, zs, ALU.mult).then_inc(S["oc_v"], 1)
                wait(dve, "gsig", layer, 1)
                for m in range(8):
                    wait(dve, "br_mm", layer, m + 1)
                    for b in range(3):
                        last = v.tensor_tensor(btmp[b], B[2 + 3 * (m % 2) + b][:, 0:TOK], gates[:, 8 * b + m], ALU.mult)
                    link(last)
                    link(v.tensor_tensor(btmp[0], btmp[0], btmp[1], ALU.add))
                    note(v.tensor_tensor(merged[:, m], btmp[0], btmp[2], ALU.add), "br_ev", layer, m + 1)
                dve.wait_ge(unparked, 16 * (layer + 1))
                add_branch(layer, 2, 2, 1)
                rstd(layer, 3)
                normed(layer, 2, 3)

                def hidden(idx, i, r, e):
                    dve.wait_ge(gu_s, idx + 1)
                    dve.wait_ge(gu_u, idx + 1)
                    dst = hid[:, i] if e is not None else hid[:, bass.ds(i, 1)].rearrange("p a n -> p (a n)")
                    if e is None:
                        v.tensor_tensor(dst, B[2 + r][:, 0:TOK], sgb[:, r], ALU.mult).then_inc(gu_h, 1)
                    else:
                        link_h(v.tensor_tensor(sgb[:, r], B[2 + r][:, 0:TOK], sgb[:, r], ALU.mult), idx)
                        v.tensor_tensor(dst, sgb[:, r], combB[:, bass.ds(e, 1)].rearrange("p a n -> p (a n)"), ALU.mult).then_inc(gu_h, 1)

                def link_h(ins, idx):
                    ins.then_inc(gu_m, 1)
                    dve.wait_ge(gu_m, idx - FG + 1)

                if layer == 0:
                    for i in range(6):
                        hidden(i, i, i % 2, None)
                    with dve.Fori(0, 2) as it:
                        for i in range(8):
                            hidden(8 * it + 6 + i, 8 * it + 6 + i, i % 2, None)
                    for m in range(8):
                        dve.wait_ge(down_mm, m + 1)
                        v.tensor_copy(yT[:, m], B[4 + m % 2][:, 0:TOK]).then_inc(down_ev, 1)
                    dve.wait_ge(down_ev, 8)
                else:
                    link(v.memset(RX[:, 3072:6144], 0.0))
                    dve.wait_ge(rl_mm, 1)
                    lg = v3(t1.rearrange("p t n -> p (t n)"), NT)
                    link(v.tensor_copy(lg, v3(B[6][:, 0:24], NT)))
                    idx = i8.bitcast(U32)
                    for t in range(NT):
                        link(v.max(m8[:, 8 * t:8 * t + 8], lg[:, t]))
                        link(v.max_index(idx[:, 8 * t:8 * t + 8], m8[:, 8 * t:8 * t + 8], lg[:, t]))
                    v.tensor_copy(i8f, idx)
                    v.tensor_tensor(m8[:, 1::8], m8[:, 1::8], m8[:, 0::8], ALU.subtract).then_inc(rl_c, 1)
                    dve.wait_ge(rl_e, 1)
                    link(v.tensor_scalar(m8[:, 0::8], m8[:, 1::8], 1.0, None, ALU.add))
                    link(v.reciprocal(m8[:, 0::8], m8[:, 0::8]))
                    link(v.tensor_tensor(m8[:, 1::8], m8[:, 1::8], m8[:, 0::8], ALU.mult))
                    for t in range(NT):
                        v.tensor_scalar(oh0[:, t], iota8, i8f[:, 8 * t:8 * t + 1], m8[:, 8 * t:8 * t + 1], ALU.is_equal, ALU.mult)
                        last = v.tensor_scalar(oh1[:, t], iota8, i8f[:, 8 * t + 1:8 * t + 2], m8[:, 8 * t + 1:8 * t + 2], ALU.is_equal, ALU.mult)
                    link(last)
                    v.tensor_tensor(comb, oh0, oh1, ALU.add).then_inc(rl_ok, 1)
                    dve.wait_ge(rb_ev, 6)
                    with dve.Fori(0, NE) as e:
                        for i in range(FE):
                            hidden(FG + FE * e + i, i, i % 2, e)
                        for m in range(8):
                            dve.wait_ge(down_mm, 8 + 8 * e + m + 1)
                            v.tensor_tensor(yT[:, m], B[4 + m % 2][:, 0:TOK], yT[:, m], ALU.add).then_inc(down_ev, 1)
                    dve.wait_ge(down_ev, 8 + 8 * NE)
                add_branch(layer, 4, 5, 2)


_INS = ["x_prompt", "x_sample", "cache_attn_k", "cache_attn_v", "state_delta", "c", "c_ctx", "ada_w", "ada_b", "norms", "w_in",
        "qk_norm", "gmlp_norm", "gmlp_ws", "gmlp_bs", "dn_conv", "dn_a_log", "dn_dt_bias", "dn_norm", "w_branch", "w_out",
        "ffn_w_gate", "ffn_w_up", "ffn_w_down", "moe_router", "moe_w_gate", "moe_w_up", "moe_w_down"]
_OUTS = [(1, CTX, D), (1, LAT, D), (1, DEPTH, CTX, KVH, HD), (1, DEPTH, CTX, KVH, HD), (1, DEPTH, 2, DNH, DK, DK)]


def kernel(**inputs):
    import concourse.bacc as _bacc
    from concourse.bass_utils import run_bass_kernel_spmd as _run

    nc = _bacc.Bacc("TRN2", target_bir_lowering=False, num_devices=1)
    arrays = {"constants": constants()}
    args = [nc.dram_tensor("constants", (P, NCST), F32, kind="ExternalInput").ap()]
    for name in _INS:
        a = np.ascontiguousarray(inputs[name])
        arrays[f"in_{name}"] = a
        args.append(nc.dram_tensor(f"in_{name}", a.shape, mybir.dt.from_np(a.dtype), kind="ExternalInput").ap())
    args.append(nc.dram_tensor("xpark", (P, KT * TOK), F32, kind="Internal").ap())
    for i, shape in enumerate(_OUTS):
        args.append(nc.dram_tensor(f"out_{i}", shape, F32, kind="ExternalOutput").ap())
    build(nc, *args)
    r = _run(nc, [arrays], core_ids=[0])
    return tuple(r.results[0][f"out_{i}"] for i in range(len(_OUTS)))
```

```python
import math
from contextlib import ExitStack

import numpy as np

import concourse.bass as bass
from concourse import mybir

F32 = mybir.dt.float32
BF16 = mybir.dt.bfloat16
U32 = mybir.dt.uint32
I32 = mybir.dt.int32
ALU = mybir.AluOpType
ACT = mybir.ActivationFunctionType
AX = mybir.AxisListType

P = 128
D = 1024
KT = D // P
DEPTH = 2
CTX, LAT = 128, 256
TOK = CTX + LAT
NT = TOK // P
HEADS, KVH, HD = 8, 4, 64
ROPE_THETA, GRID_W = 10000.0, 64
DNH, DK = 4, 128
CHUNK = 64
CONV_K = 5
FFN = 2816
NE, ED = 8, 1408
EPS = 1e-6
TOP_K, SLOTS = 2, P
NI = 1 + (TOP_K * TOK + (NE - 1) * (SLOTS - 1)) // SLOTS + 1
MIN_ITEMS = TOP_K * TOK // SLOTS
FG, FE = FFN // P, ED // P

C_QA, C_KA, C_U, C_V, C_DN, C_BA, C_Z, C_GATE = 0, 512, 1024, 1536, 2048, 3584, 3600, 4112

NSLOT = 4
SLOT = 4096
CROW = CTX + LAT + 4 * (CONV_K // 2)
COUT = CROW - (CONV_K - 1)
LAT0 = CTX + 4
SEG = ((0, 0, CTX), (1, CTX, TOK))

T_QKV, T_BA, T_A, T_UV, T_G, T_Z = 0, 12, 15, 21, 27, 51
N_PROJ = 54
LEVELS = (1, 2, 4, 8, 16, 32)

ADA_FIRST = (0, 1, 2, 3)
ADA_AT = (dict(n1=(), at=(4, 5, 6), z=(7, 8), oc=(9,), n3=(10, 11), h3=(12, 13), n4=(14, 15)),
          dict(n1=(16,), at=(17, 18, 19), z=(20, 21), oc=(22,), n3=(23,), h3=(), n4=()))
ADA_U = 12
ADA_DONE = {3: (1, 0), 5: (2, 1), 9: (4, 2), 11: (5, 3)}

PER = dict(proj_mm=N_PROJ, proj_ev=N_PROJ, sq=4, stat=4, root=4, rinv=4, xn=2, h_a=8, h_v=8, x_new=2,
           pads=1, conv=12, silu=3, dsq=1, dst=8, droot=8, qkn=1, kvt_mm=6, kvt_ev=6,
           ba_v=1, ba_l=1, g_ok=1, gc_mm=1, gc_v=1, gc_e=1, beg=1,
           a_sq=1, a_ss=1, a_rt=1, a_ok=1, tr_mm=6, tr_ev=6, v_ss=1, v_rt=1, v_ok=1,
           at_s=24, at_m=24, at_e=24, at_p=24, at_t=24, at_pt=24, at_pv=24, at_o=3,
           b_mm=3, b_v=3, b_t=3, b_ev=3,
           d_in=6, d_d0=6, d_e=6, d_pool=6, d_m=6, d_mt=6, d_mtc=6, d_t1=6, d_ct=30, d_w=30, d_we=30,
           d_du=30, d_up=30, d_uw=6, d_uwe=6, d_kd=6, s_ws=12, s_vn=12, s_o=12, s_st=12, s_or=6,
           oc_sq=1, oc_ss=1, oc_rt=1, oc_v=1, oc_mm=3, oc_ev=3, gsig=1,
           br_mm=8, br_ev=8, wo_mm=8, wo_ev=8)


TILE = ((0, 0), (1, 2), (2, 1))
TCOL = (0, LAT0, LAT0 + P)


def constants():
    i, j = np.arange(P)[:, None], np.arange(P)[None, :]
    same = (i // CHUNK) == (j // CHUNK)
    parts = [np.eye(P), (i >= j) & same, (i <= j) & same, same, np.ones((P, P))]
    quarter = HD // 4
    freqs = (1.0 / (np.float32(ROPE_THETA) ** (np.arange(quarter, dtype=np.float32) / quarter))).astype(np.float32)
    rope = np.zeros((P, 2, 2, 2, quarter), np.float32)
    for t in range(LAT // P):
        pos = t * P + np.arange(P)
        for a, x in enumerate((pos // GRID_W, pos % GRID_W)):
            ang = x[:, None].astype(np.float32) * freqs[None]
            rope[:, t, 0, a], rope[:, t, 1, a] = np.cos(ang), np.sin(ang)
    parts.append(rope.reshape(P, -1))
    parts.append(np.stack([np.arange(P) < CHUNK, np.arange(P) >= CHUNK], 1))
    parts.append(np.tile([EPS, DK * EPS, 1.0], (P, 1)))
    parts.append(np.tile(np.arange(NE), (P, 1)))
    for s in LEVELS:
        low = (i // (2 * s) == j // (2 * s)) & (i % (2 * s) >= s) & (j % (2 * s) < s)
        parts += [-1.0 * low, -1.0 * low.T]
    e = np.arange(NE)
    parts += [i <= j, np.tile(np.arange(P) + 1.0, (P, 1)), np.tile((e[None] < e[:, None]).reshape(1, -1), (P, 1)),
              np.tile(np.arange(NI), (P, 1))]
    return np.ascontiguousarray(np.concatenate([np.asarray(x, np.float32) for x in parts], 1))


NRES = 5 * P + 128 + 2 + 3 + NE
NMASK = 2 * len(LEVELS) * P
NROUTE = 2 * P + NE * NE + NI
NCST = NRES + NMASK + NROUTE


def build(nc, cst_d, x_prompt, x_sample, cache_k, cache_v, state_in, c, c_ctx, ada_w, ada_b, norms, w_in, qk_norm,
          gmlp_norm, gmlp_ws, gmlp_bs, dn_conv, dn_a_log, dn_dt_bias, dn_norm, w_branch, w_out, ffn_g, ffn_u, ffn_d,
          router, moe_g, moe_u, moe_d, xpark, y_prompt, y_sample, new_k, new_v, new_s):
    ctx = ExitStack()
    with ctx:
        def sb(name, n, dt=F32):
            return ctx.enter_context(nc.sbuf_tensor(name, [P, n], dt))

        def sem(name):
            return ctx.enter_context(nc.semaphore(name))

        ring = sb("ring", NSLOT * SLOT)
        H = sb("hT", KT * TOK)
        GT = sb("gates", 24 * TOK)
        CV = sb("conv", 12 * COUT)
        KK_ = sb("ktok", NT * 512)
        OT = sb("oT", 12 * TOK)
        RX = sb("work", 10240)
        cst = sb("cst", NRES)
        lmask = sb("lmask", 2 * len(LEVELS) * P, BF16)
        rows = sb("rowsT", 64 + 96 + 24 + 120)
        modv = sb("modv", DEPTH * 96)
        sm = sb("small", 768)

        def v3(ap, a):
            return ap.rearrange("p (a b) -> p a b", a=a)

        hT, xT = v3(H[:, :], KT), v3(RX[:, 0:KT * TOK], KT)
        yT = v3(RX[:, 3072:6144], KT)
        sqT, sqP = v3(GT[:, 0:3072], KT), v3(CV[:, 0:3072], KT)
        gates = v3(GT[:, :], 24)
        pre = v3(GT[:, 0:12 * CROW], 12)
        dsq = v3(GT[:, 12 * CROW:12 * CROW + 8 * COUT], 8)
        cv = v3(CV[:, :], 12)
        vtok = CV[:, 8 * COUT:8 * COUT + 1536].rearrange("p (t h e) -> p t h e", t=NT, h=DNH)
        ktok = KK_[:, :].rearrange("p (t h e) -> p t h e", t=NT, h=DNH)
        oT = OT[:, :].rearrange("p (b k n) -> p b k n", b=3, k=4)
        ident, inclL, inclU, same, ones = (cst[:, i * P:(i + 1) * P] for i in range(5))
        rope = cst[:, 640:768].rearrange("p (t f a q) -> p t f a q", t=2, f=2, a=2)
        chsel = cst[:, 768:770]
        eps1, eps128, one1 = (cst[:, 770 + i:771 + i] for i in range(3))
        iota8 = cst[:, 773:773 + NE]
        lm = lmask[:, :].rearrange("p (s f n) -> p s f n", s=len(LEVELS), f=2)
        nrmT = rows[:, 0:64].rearrange("p (l a k) -> p l a k", l=DEPTH, a=4)
        adab = rows[:, 64:160].rearrange("p (l m) -> p l m", l=DEPTH)
        scT = rows[:, 160:176].rearrange("p (s k) -> p s k", s=2)
        bsT = rows[:, 176:184].rearrange("p (l g) -> p l g", l=DEPTH)
        cwT = rows[:, 184:304].rearrange("p (l j n) -> p l j n", l=DEPTH, j=CONV_K)
        mod = modv[:, :].rearrange("p (l a k s) -> p l a k s", l=DEPTH, a=6, k=KT)

        qkv = v3(RX[:, 0:3072], NT)
        qTt = v3(RX[:, 3072:4608], 4)
        kTt = v3(RX[:, 4608:5632], 2)
        Pb = v3(RX[:, 5632:6400], 2)
        PTb = v3(RX[:, 6400:7168], 2)
        uB, vB = v3(RX[:, 7168:8704], NT), v3(RX[:, 8704:10240], NT)
        wsT = OT[:, 3072:3584]
        ggain = OT[:, 3584:4096]
        qkgain = OT[:, 4096:4224]
        asq = v3(OT[:, 0:2304], NT)
        kcache, vcache = GT[:, 8192:8448], GT[:, 8448:8704]
        wsraw = v3(GT[:, 8704:9216], 4)
        gsc = GT[:, 7168:7680]
        rt = [GT[:, 384 * i:384 * (i + 1)].rearrange("p (h a q) -> p h a q", h=12, a=2) for i in range(4)]

        def dn(d, i):
            return v3(RX[:, (9 * d + i) * 512:(9 * d + i + 1) * 512], DNH)
        B_M, B_QK, B_QEG, B_MT, B_T, B_U, B_W, B_VU, B_KW = range(9)
        B_CT, B_KD, B_VN = B_M, B_MT, B_T
        state = RX[:, 9216:10240].rearrange("p (d h e) -> p d h e", d=2, h=DNH)
        osum = v3(OT[:, 3072:4608], NT)
        zs = v3(CV[:, 0:1536], NT)
        merged = v3(CV[:, 1536:4608], KT)
        btmp = [RX[:, 6144 + 384 * i:6528 + 384 * i] for i in range(3)]
        sgb = v3(RX[:, 6144:6912], 2)
        hid = v3(GT[:, 0:FG * TOK], FG)

        m_off = [0]

        def gt(n):
            m_off[0] += n
            assert m_off[0] <= 9216
            return GT[:, m_off[0] - n:m_off[0]]
        ehid, xg = v3(gt(FE * SLOTS), FE), v3(gt(KT * SLOTS), KT)
        ytok, scatT = gt(D), gt(TOK)
        esel, wsel = v3(gt(NT * SLOTS), NT), v3(gt(NT * SLOTS), NT)
        esg = v3(gt(4 * P), 2)
        route = gt(NROUTE)
        tri, slot1 = route[:, 0:P], route[:, P:2 * P]
        before, item = v3(route[:, 2 * P:2 * P + NE * NE], NE), route[:, 2 * P + NE * NE:NROUTE]
        sel2 = gt(NT * NE).rearrange("p (t e) -> p t e", t=NT), gt(NT * NE).rearrange("p (t e) -> p t e", t=NT)
        rank = v3(gt(NT * NE), NT)
        cnt, nit, e_lo, e_hi = (gt(NE) for _ in range(4))
        tri8 = v3(gt(NE * NE), NE)
        own, own2 = v3(gt(NI * NE), NI), v3(gt(NI * NE), NI)
        it_e, it_lo = gt(NI), gt(NI)
        oprod = gt(NI * NT * NE).rearrange("p (i t e) -> p i t e", i=NI, t=NT)
        it_rank, it_comb = v3(gt(NI * NT), NI), v3(gt(NI * NT), NI)
        h2tok = v3(CV[:, 0:3072], NT)

        def ada_rows(n, buf):
            return buf[0:2, 512 * (n % 2):512 * (n % 2 + 1)]

        off = [0]

        def small(n):
            off[0] += n
            assert off[0] <= 768
            return sm[:, off[0] - n:off[0]]
        ba = v3(small(48), NT)
        beta, gg, t1, t2, beg, edec, eg = (v3(small(24), NT) for _ in range(7))
        gcs = v3(small(24), NT)
        table = small(NI + 1).bitcast(I32)
        gm = small(48).rearrange("p (t c n) -> p t c n", t=NT, c=2)
        egl = small(48).rearrange("p (t c n) -> p t c n", t=NT, c=2)
        expa, dtb = small(8), small(8)
        ass, amx, anm, ars = small(36), small(24), small(24), small(24)
        vss, oss = small(3), small(12)
        m8, i8, i8f = small(24), small(24), small(24)
        oh0, oh1, comb = (v3(small(24), NT) for _ in range(3))
        baw = OT[:, 4224:4352]
        dngain = sb("dngain", DK)
        rs = sb("rstd", TOK)
        rtw = sb("routerw", KT * NE)

        B = [ctx.enter_context(nc.psum_tensor(f"bank{i}", [P, 512], F32)) for i in range(8)]

        s_slot = [sem(f"slot{i}_full") for i in range(NSLOT)]
        S = {n: sem(n) for n in PER}
        (cst_in, rows_in, x_in, bf_ok, rt_mm, rt_ev, sc_ok, xt_mm, xt_ev, ada_mm, ada_ev, ada_t, ada_cp, mod_ok, lw_in, cache_in, dn_in, parked,
         unparked, kv_out, st_out, st_in, y_out, gu_g, gu_u, gu_s, gu_h, down_mm, down_ev, rl_mm, rl_c, rl_e, rl_ok, rk_mm, tbl_ok, ht_mm, ht_ev, route_in,
         ots_full, mg_mm, msg_ok, mh_ok, wsel_ok, sel_ok, ga_mm, ga_ev, wt_mm, wt_ev, dn_mm, yt_ok, sc_mm, sc_ad,
         xo_mm, xo_ev, sp_turn, act_step, dve_step, pool_step) = (sem(n) for n in (
            "cst_in rows_in x_in bf_ok rt_mm rt_ev sc_ok xt_mm xt_ev ada_mm ada_ev ada_t ada_cp mod_ok lw_in cache_in dn_in parked "
            "unparked kv_out st_out st_in y_out gu_g gu_u gu_s gu_h down_mm down_ev rl_mm rl_c rl_e rl_ok rk_mm tbl_ok ht_mm ht_ev route_in "
            "ots_full mg_mm msg_ok mh_ok wsel_ok sel_ok ga_mm ga_ev wt_mm wt_ev dn_mm yt_ok sc_mm sc_ad "
            "xo_mm xo_ev sp_turn act_step dve_step pool_step").split())

        H_BANK = (0, 1, 3, 4, 5, 7)

        def wait(eng, name, layer, n):
            if PER[name] * layer + n > 0:
                eng.wait_ge(S[name], PER[name] * layer + n)

        def linker(eng, step):
            n = [0]

            def link(ins):
                n[0] += 1
                ins.then_inc(step, 1)
                eng.wait_ge(step, n[0])
            return link

        WIN = [C_DN, C_DN + 512, C_DN + 1024, C_QA, C_KA, C_U, C_V] + [C_GATE + 512 * i for i in range(6)] + [C_Z]
        WIN_END = [4, 8, 12, T_A + 3, T_A + 6, T_UV + 3, T_UV + 6] + [T_G + 4 * (i + 1) for i in range(6)] + [T_Z + 3]
        FF_GU, FF_DN = 11, 8
        order = [("ada", n) for n in ADA_FIRST]
        for layer, at in enumerate(ADA_AT):
            for ada, first, last in (("n1", 0, 7), ("at", 7, 13), ("z", 13, 14), ("oc", 14, 20), ("n3", 0, 0), ("h3", 0, 0)):
                order += [("ada", n) for n in at[ada]] + [("w", layer, i) for i in range(first, last)]
            if layer == 0:
                order += [("ff", i) for i in range(FF_GU + FF_DN)]
            order += [("ada", n) for n in at["n4"]]
        U_MOE = len(order)
        M_GU, M_DN, M_SLOT = 6, 4, 5
        WIN = [C_DN, C_DN + 512, C_DN + 1024, C_QA, C_KA, C_U, C_V] + [C_GATE + 512 * i for i in range(6)] + [C_Z]
        WIN_END = [4, 8, 12, T_A + 3, T_A + 6, T_UV + 3, T_UV + 6] + [T_G + 4 * (i + 1) for i in range(6)] + [T_Z + 3]

        def at_ring(*key):
            return order.index(key)

        def slot(unit):
            return unit % NSLOT

        def wslot(unit, k, n):
            s = slot(unit)
            return ring[:, s * SLOT:s * SLOT + k * n].rearrange("p (k n) -> p k n", k=k)

        def dmas(unit):
            return 2 if unit < U_MOE and order[unit][0] == "ff" and order[unit][1] < FF_GU else 1

        def full(unit):
            return 16 * sum(dmas(u) for u in range(unit % NSLOT, unit + 1, NSLOT))

        def m_place(j):
            if j % M_SLOT == M_SLOT - 1:
                return OT[:, 0:SLOT]
            k = slot(U_MOE + j % M_SLOT)
            return ring[:, k * SLOT:(k + 1) * SLOT]

        def m_dmas(j):
            return 2 if j < M_GU else 1

        def m_sem(j):
            return ots_full if j % M_SLOT == M_SLOT - 1 else s_slot[slot(U_MOE + j % M_SLOT)]

        def m_full(j, i):
            s = j % M_SLOT
            at_start = 0 if s == M_SLOT - 1 else full(U_MOE + s - NSLOT)
            here = m_dmas(s) + (m_dmas(s + M_SLOT) if j >= M_SLOT else 0)
            return 16 * (m_dmas(s) + m_dmas(s + M_SLOT)) * i + at_start + 16 * here

        block = ctx.enter_context(nc.Block())

        @block.sync
        def _(sp):
            def load(unit, dst, src):
                sp.dma_start(dst, src).then_inc(s_slot[slot(unit)], 16)

            def freed(unit):
                if unit < NSLOT:
                    return
                kind, *at = order[unit - NSLOT]
                if kind == "ada":
                    sp.wait_ge(ada_mm, at[0] + 1)
                elif kind == "w":
                    layer, i = at
                    if i < 14:
                        wait(sp, "proj_mm", layer, WIN_END[i])
                    elif i < 18:
                        wait(sp, "br_mm", layer, 2 * (i - 13))
                    else:
                        wait(sp, "wo_mm", layer, 4 * (i - 17))
                elif at[0] < FF_GU:
                    sp.wait_ge(gu_u, 2 * (at[0] + 1))
                else:
                    sp.wait_ge(down_mm, at[0] - FF_GU + 1)

            for u, (kind, *at) in enumerate(order):
                if kind == "w" and at[1] == 4:
                    wait(sp, "xn", at[0], 1)
                    wait(sp, "sq", at[0], 1)
                    sp.dma_start(xpark.rearrange("p (k n) -> p k n", k=KT), xT).then_inc(parked, 16)
                freed(u)
                if kind == "ada":
                    layer, i = divmod(at[0], ADA_U)
                    load(u, wslot(u, KT, 512), ada_w[layer, :, 512 * i:512 * (i + 1)].rearrange("(k p) n -> p k n", p=P))
                elif kind == "w":
                    layer, i = at
                    if i < 14:
                        load(u, wslot(u, KT, 512), w_in[layer, :, WIN[i]:WIN[i] + 512].rearrange("(k p) n -> p k n", p=P))
                    elif i < 18:
                        n0 = 256 * (i - 14)
                        src = w_branch[layer, :, :, n0:n0 + 256].rearrange("b (k p) n -> p (b k) n", p=P)
                        load(u, wslot(u, 12, 256), src)
                    else:
                        n0 = 512 * (i - 18)
                        load(u, wslot(u, KT, 512), w_out[layer, :, n0:n0 + 512].rearrange("(k p) n -> p k n", p=P))
                elif at[0] < FF_GU:
                    d = ring[:, slot(u) * SLOT:(slot(u) + 1) * SLOT].rearrange("p (g k n) -> p g k n", g=2, k=KT)
                    n0 = 256 * at[0]
                    load(u, d[:, 0], ffn_g[0, :, n0:n0 + 256].rearrange("(k p) n -> p k n", p=P))
                    load(u, d[:, 1], ffn_u[0, :, n0:n0 + 256].rearrange("(k p) n -> p k n", p=P))
                else:
                    n0 = P * (at[0] - FF_GU)
                    load(u, wslot(u, FG, P), ffn_d[0, :, n0:n0 + P].rearrange("(k p) n -> p k n", p=P))

            def moe_load(e, j):
                ex = slice(0, 1) if e is None else bass.ds(e, 1)
                if j < M_GU:
                    n = 256 if j < M_GU - 1 else P
                    d = m_place(j)[:, 0:16 * n].rearrange("p (g k n) -> p g k n", g=2, k=KT)
                    for g, w in enumerate((moe_g, moe_u)):
                        src = w[0, ex, :, 256 * j:256 * j + n].rearrange("a (k p) n -> p (a k) n", p=P)
                        sp.dma_start(d[:, g], src).then_inc(m_sem(j), 16)
                else:
                    n0 = 256 * (j - M_GU)
                    src = moe_d[0, ex, :, n0:n0 + 256].rearrange("a (k p) n -> p (a k) n", p=P)
                    sp.dma_start(m_place(j)[:, 0:FE * 256].rearrange("p (k n) -> p k n", k=FE), src).then_inc(m_sem(j), 16)

            for j in range(4):
                freed(U_MOE + j)
                moe_load(None, j)
            wait(sp, "br_mm", 1, 8)
            moe_load(None, 4)
            for j in range(M_SLOT, M_GU + M_DN):
                sp.wait_ge(mg_mm, j - M_SLOT + 1)
                moe_load(None, j)
            sp.wait_ge(tbl_ok, 1)
            n_items = sp.value_load(table[0:1, NI:NI + 1], min_val=MIN_ITEMS, max_val=NI - 1)
            with sp.Fori(1, n_items) as i:
                e = sp.value_load(table[0:1, bass.ds(i, 1)], min_val=0, max_val=NE - 1)
                for j in range(M_GU + M_DN):
                    if j == 0:
                        sp.wait_ge(mg_mm, M_GU * i)
                    elif j < M_SLOT:
                        sp.wait_ge(dn_mm, M_DN * i + (j - M_DN))
                    else:
                        sp.wait_ge(mg_mm, M_GU * i + (j - M_SLOT + 1))
                    sp.sem_inc(sp_turn, 1)
                    moe_load(e, j)
            for t in range(NT):
                sp.wait_ge(xo_ev, 2 * t + 2)
                dst = y_prompt[0] if t == 0 else y_sample[0, (t - 1) * P:t * P, :]
                sp.dma_start(dst, v3(GT[:, 0:3072], NT)[:, t]).then_inc(y_out, 16)
            sp.wait_ge(y_out, 16 * NT)

        @block.gpsimd
        def _(pool):
            link = linker(pool, pool_step)

            def bc(ap, n):
                return ap.unsqueeze(2).to_broadcast([P, ap.shape[1], n])

            pool.dma_start(cst[:, :], cst_d[:, 0:NRES]).then_inc(cst_in, 16)
            pool.dma_start(RX[:, 6144:6144 + NMASK], cst_d[:, NRES:NRES + NMASK]).then_inc(cst_in, 16)
            st = v3(RX[:, 8192:8704], 4)
            link(nc.gpsimd.memset(st, 0.0))
            pool.dma_start(st[0:64, 0], norms.rearrange("l a (k p) -> (l a k) p", p=P)).then_inc(rows_in, 16)
            pool.dma_start(st[0:96, 1], ada_b.rearrange("l (m p) -> (l m) p", p=P)).then_inc(rows_in, 16)
            pool.dma_start(st[0:8, 2], c_ctx.rearrange("(k p) -> k p", p=P)).then_inc(rows_in, 16)
            pool.dma_start(st[8:16, 2], c.rearrange("s (k p) -> (s k) p", p=P)).then_inc(rows_in, 16)
            pool.dma_start(st[16:24, 2], gmlp_bs.rearrange("l g p -> (l g) p")).then_inc(rows_in, 16)
            pool.dma_start(st[0:120, 3], dn_conv.rearrange("l j (n p) -> (l j n) p", p=P)).then_inc(rows_in, 16)
            xtok = v3(RX[:, 3072:6144], NT)
            pool.dma_start(xtok[:, 0], x_prompt[0]).then_inc(x_in, 16)
            for t in (1, 2):
                pool.dma_start(xtok[:, t], x_sample[0, (t - 1) * P:t * P, :]).then_inc(x_in, 16)

            for layer in range(DEPTH):
                wait(pool, "x_new", layer, 0)
                for dst, src in ((v3(baw, KT), w_in[layer, :, C_BA:C_BA + 16].rearrange("(k p) n -> p k n", p=P)),
                                 (ggain, gmlp_norm[layer].partition_broadcast(P)),
                                 (qkgain, qk_norm[layer].rearrange("a d -> (a d)").partition_broadcast(P)),
                                 (expa, dn_a_log[layer].rearrange("a d -> (a d)").partition_broadcast(P)),
                                 (dtb, dn_dt_bias[layer].rearrange("a d -> (a d)").partition_broadcast(P)),
                                 (dngain[:, :], dn_norm[layer].partition_broadcast(P))):
                    pool.dma_start(dst, src).then_inc(lw_in, 16)
                if layer == 0:
                    pool.dma_start(v3(rtw[:, :], KT), router[0].rearrange("(k p) n -> p k n", p=P)).then_inc(lw_in, 16)
                pool.dma_start(wsraw, gmlp_ws[layer].rearrange("g q r -> q g r")).then_inc(cache_in, 16)
                pool.dma_start(kcache, cache_k[0, layer].rearrange("t h d -> t (h d)")).then_inc(cache_in, 16)
                pool.dma_start(vcache, cache_v[0, layer].rearrange("t h d -> t (h d)")).then_inc(cache_in, 16)
                wait(pool, "a_ok", layer, 1)
                pool.dma_start(new_k[0, layer].rearrange("t h d -> t (h d)"), qkv[:, 0, 512:768]).then_inc(kv_out, 16)
                pool.dma_start(new_v[0, layer].rearrange("t h d -> t (h d)"), qkv[:, 0, 768:1024]).then_inc(kv_out, 16)
                pool.wait_ge(kv_out, 32 * (layer + 1))
                wait(pool, "b_ev", layer, 3)
                wait(pool, "at_pv", layer, 24)
                wait(pool, "at_pt", layer, 24)
                link(nc.gpsimd.memset(state, 0.0))
                wait(pool, "kvt_ev", layer, 6)
                wait(pool, "beg", layer, 1)
                for pair in range(3):
                    for d in range(2):
                        g = 2 * pair + d
                        t = TILE[pair][d]
                        h4 = slice(4 * d, 4 * d + 4)
                        if pair:
                            wait(pool, "s_or", layer, g - 1)
                        nc.gpsimd.tensor_tensor(dn(d, B_VU), vtok[:, t], bc(beta[:, t, h4], DK), ALU.mult)
                        link(nc.gpsimd.tensor_tensor(dn(d, B_KW), ktok[:, t], bc(beg[:, t, h4], DK), ALU.mult))
                        wait(pool, "d_e", layer, g + 1)
                        nc.gpsimd.tensor_tensor(dn(d, B_M), dn(d, B_M), bc(beta[:, t, h4], P), ALU.mult)
                        incl = inclU if d == 0 else inclL
                        nc.gpsimd.tensor_tensor(dn(d, B_QK), dn(d, B_QK), incl.unsqueeze(1).to_broadcast([P, DNH, P]), ALU.mult)
                        nc.gpsimd.tensor_tensor(dn(d, B_QEG), dn(d, B_QEG), cv[:, 0:4, TCOL[t]:TCOL[t] + P],
                                                ALU.mult).then_inc(S["d_pool"], 1)
                    for s in range(1, len(LEVELS)):
                        for d in range(2):
                            g = 2 * pair + d
                            if s == 1:
                                wait(pool, "d_mtc", layer, g + 1)
                                wait(pool, "d_t1", layer, g + 1)
                            else:
                                wait(pool, "d_w", layer, 10 * pair + 2 * (s - 2) + d + 1)
                            nc.gpsimd.tensor_tensor(dn(d, B_CT), dn(d, B_MT),
                                                    lm[:, s, 1 - d].unsqueeze(1).to_broadcast([P, DNH, P]),
                                                    ALU.mult).then_inc(S["d_ct"], 1)
                    for d in range(2):
                        t = TILE[pair][d]
                        wait(pool, "d_ct", layer, 10 * pair + 8 + d + 1)
                        nc.gpsimd.tensor_tensor(dn(d, B_KD), ktok[:, t], bc(edec[:, t, 4 * d:4 * d + 4], DK),
                                                ALU.mult).then_inc(S["d_kd"], 1)
                    if pair == 0:
                        wait(pool, "s_st", layer, 4)
                        for d in range(2):
                            pool.dma_start(new_s[0, layer, d].rearrange("h k e -> k h e"), state[:, d]).then_inc(st_out, 16)
                        pool.wait_ge(st_out, 32 * (layer + 1))
                        for d in range(2):
                            pool.dma_start(state[:, d], state_in[0, layer, d].rearrange("h k e -> k h e")).then_inc(st_in, 16)
                wait(pool, "s_or", layer, 6)
                wait(pool, "s_st", layer, 12)
                wait(pool, "oc_mm", layer, 3)
                pool.dma_start(xT, xpark.rearrange("p (k n) -> p k n", k=KT)).then_inc(unparked, 16)
            wait(pool, "br_ev", 1, 8)
            pool.dma_start(route, cst_d[:, NRES + NMASK:NCST]).then_inc(route_in, 16)
            pool.wait_ge(unparked, 16 * DEPTH)
            pool.wait_ge(kv_out, 32 * DEPTH)
            pool.wait_ge(st_out, 32 * DEPTH)

        @block.tensor
        def _(pe):
            mm = nc.tensor.matmul

            def tr(out, in_):
                return nc.tensor.transpose(out, in_, ident)

            def arrived(unit):
                pe.wait_ge(s_slot[slot(unit)], full(unit))

            pe.wait_ge(cst_in, 32)
            pe.wait_ge(rows_in, 96)
            st = v3(RX[:, 8192:8704], 4)
            for i in range(4):
                tr(B[0][:, i * P:(i + 1) * P], st[:, i]).then_inc(rt_mm, 1)
            pe.wait_ge(x_in, 16 * NT)
            xtok = v3(RX[:, 3072:6144], NT)
            for t in range(NT):
                for half in range(2):
                    for k in range(4):
                        last = tr(B[2 + 2 * t + half][:, k * P:(k + 1) * P], xtok[:, t, (4 * half + k) * P:(4 * half + k + 1) * P])
                    last.then_inc(xt_mm, 1)

            def ada_row(n, k, b):
                u = at_ring("ada", n)
                if k == 0:
                    arrived(u)
                    if n >= 2:
                        pe.wait_ge(ada_cp, n - 1)
                last = mm(B[b + n % 2][0:2, :], scT[:, :, k], wslot(u, KT, 512)[:, k], start=k == 0, stop=k == KT - 1)
                if k == KT - 1:
                    last.then_inc(ada_mm, 1)

            def ada_turn(n, b, buf):
                pe.wait_ge(ada_ev, n + 1)
                for m in range(4):
                    last = nc.tensor.transpose(B[b + n % 2][:, 2 * m:2 * m + 2], ada_rows(n, buf)[:, m * P:(m + 1) * P], ident[0:2, 0:2])
                last.then_inc(ada_t, 1)

            def ada_units(units, b):
                for j, n in enumerate(units):
                    for k in range(KT):
                        ada_row(n, k, b)
                    if j:
                        ada_turn(n - 1, b, KK_)
                if units:
                    ada_turn(units[-1], b, KK_)

            def sum_squares(layer, q, sq):
                wait(pe, "sq", layer, q)
                for k in range(KT):
                    last = mm(B[2][:, 0:TOK], ones, sq[:, k], start=k == 0, stop=k == KT - 1)
                last.then_inc(S["stat"], 1)

            def bank_free(layer, n):
                wait(pe, "proj_ev", layer, n - 1)

            def feature_tile(layer, n, unit, m):
                bank_free(layer, n)
                w = wslot(unit, KT, 512)
                for k in range(KT):
                    last = mm(B[n % 2][:, 0:TOK], w[:, k, m * P:(m + 1) * P], hT[:, k], start=k == 0, stop=k == KT - 1)
                last.then_inc(S["proj_mm"], 1)

            def token_tiles(layer, n, unit):
                arrived(unit)
                w = wslot(unit, KT, 512)
                for t in range(NT):
                    bank_free(layer, n + t)
                    for k in range(KT):
                        last = mm(B[(n + t) % 2][:, :], hT[:, k, t * P:(t + 1) * P], w[:, k], start=k == 0, stop=k == KT - 1)
                    last.then_inc(S["proj_mm"], 1)

            for layer in range(DEPTH):
                at = ADA_AT[layer]

                def unit(i):
                    return at_ring("w", layer, i)

                wait(pe, "x_new", layer, 0)
                sum_squares(layer, 1, sqT)
                if layer == 0:
                    pe.wait_ge(sc_ok, 1)
                    ada_units(ADA_FIRST, 0)
                    pe.wait_ge(ada_cp, len(ADA_FIRST))
                ada_units(at["n1"], 6)
                wait(pe, "h_a", layer, 4)
                wait(pe, "h_v", layer, 4)
                for i in range(3):
                    arrived(unit(i))
                    for m in range(4):
                        feature_tile(layer, 4 * i + m, unit(i), m)
                pe.wait_ge(lw_in, 16 * (7 + 6 * layer))
                for t in range(NT):
                    n = T_BA + t
                    bank_free(layer, n)
                    for k in range(KT):
                        last = mm(B[n % 2][:, 0:16], hT[:, k, t * P:(t + 1) * P], v3(baw, KT)[:, k], start=k == 0, stop=k == KT - 1)
                    last.then_inc(S["proj_mm"], 1)
                token_tiles(layer, T_A, unit(3))
                token_tiles(layer, T_A + 3, unit(4))
                wait(pe, "dsq", layer, 1)
                for j in range(8):
                    if j >= 2:
                        wait(pe, "droot", layer, j - 1)
                    mm(B[2 + j % 2][:, 0:COUT], ones, dsq[:, j], start=True, stop=True).then_inc(S["dst"], 1)
                token_tiles(layer, T_UV, unit(5))
                token_tiles(layer, T_UV + 3, unit(6))
                wait(pe, "g_ok", layer, 1)
                for t in range(NT):
                    c0 = 32 * t
                    mm(B[4][:, c0:c0 + 4], inclU, gg[:, t, 0:4], start=True, stop=True)
                    mm(B[4][:, c0 + 4:c0 + 8], inclL, gg[:, t, 4:8], start=True, stop=True)
                    mm(B[4][:, c0 + 8:c0 + 16], same, gg[:, t], start=True, stop=True)
                    last = mm(B[4][:, c0 + 16:c0 + 32], ones, gm[:, t].rearrange("p c n -> p (c n)"), start=True, stop=True)
                last.then_inc(S["gc_mm"], 1)
                if at["n1"]:
                    pe.wait_ge(ada_cp, at["n1"][-1] + 1)
                wait(pe, "qkn", layer, 1)
                wait(pe, "droot", layer, 8)
                for i, j0 in ((0, 8), (1, 4)):
                    for t in range(NT):
                        b = (5, 6, 7, 2, 3, 4)[3 * i + t]
                        if b == 4:
                            wait(pe, "gc_v", layer, 1)
                        for h in range(DNH):
                            last = tr(B[b][:, h * P:(h + 1) * P], cv[:, j0 + h, TCOL[t]:TCOL[t] + P])
                        last.then_inc(S["kvt_mm"], 1)
                wait(pe, "a_ok", layer, 1)
                pe.wait_ge(cache_in, 48 * (layer + 1))
                wait(pe, "kvt_ev", layer, 6)
                for t in range(NT):
                    for j in range(4):
                        last = tr(B[2 + t][:, j * P:(j + 1) * P], qkv[:, t, j * P:(j + 1) * P])
                    last.then_inc(S["tr_mm"], 1)
                for half in range(2):
                    for a in range(2):
                        for n in range(2):
                            src = (kcache if n else qkv[:, 0, 512:768]) if half == 0 else qkv[:, 1 + n, 512:768]
                            j = 2 * a + n
                            last = tr(B[5 + half][:, j * P:(j + 1) * P], src[:, a * P:(a + 1) * P])
                    last.then_inc(S["tr_mm"], 1)
                for g in range(4):
                    last = tr(B[7][:, g * P:(g + 1) * P], wsraw[:, g])
                last.then_inc(S["tr_mm"], 1)
                wait(pe, "tr_ev", layer, 6)
                wait(pe, "v_ok", layer, 1)
                for t in range(NT):
                    for g in range(4):
                        last = mm(B[2 + t][:, g * P:(g + 1) * P], v3(wsT, 4)[:, g], vB[:, t, g * P:(g + 1) * P], start=True, stop=True)
                    last.then_inc(S["b_mm"], 1)
                for t in range(NT):
                    wait(pe, "b_v", layer, t + 1)
                    for g in range(4):
                        last = tr(B[5 + t][:, g * P:(g + 1) * P], uB[:, t, g * P:(g + 1) * P])
                    last.then_inc(S["b_t"], 1)
                wait(pe, "b_ev", layer, 3)

                def scores(i):
                    t, h = divmod(i, HEADS)
                    a, b, cc = h // 4, h // 2 % 2, h % 2
                    if i >= 2:
                        wait(pe, "at_e", layer, i - 1)
                    keys = kTt[64 * b:64 * b + 64, a, 0:P] if t == 0 else kTt[64 * b:64 * b + 64, a, P:512]
                    q = qTt[64 * b:64 * b + 64, 2 * a + cc, t * P:(t + 1) * P]
                    mm(B[2 + i % 2][:, 0:P if t == 0 else TOK], q, keys, start=True, stop=True).then_inc(S["at_s"], 1)

                def flip(i):
                    wait(pe, "at_p", layer, i + 1)
                    if i >= 2:
                        wait(pe, "at_pt", layer, i - 1)
                    n = 1 if i < HEADS else 3
                    for kt in range(n):
                        last = tr(B[4 + i % 2][:, kt * P:(kt + 1) * P], Pb[:, i % 2, kt * P:(kt + 1) * P])
                    last.then_inc(S["at_t"], 1)

                def weigh(i):
                    t, h = divmod(i, HEADS)
                    wait(pe, "at_pt", layer, i + 1)
                    if h == 0 and t == 2:
                        wait(pe, "at_o", layer, 1)
                    g = h // 2
                    vs = [qkv[:, 0, 768:1024]] if t == 0 else [vcache, qkv[:, 1, 768:1024], qkv[:, 2, 768:1024]]
                    out = B[6 + t % 2][64 * (h % 2):64 * (h % 2) + 64, (h // 2) * P:(h // 2 + 1) * P]
                    for kt, v in enumerate(vs):
                        last = mm(out, v[:, HD * g:HD * (g + 1)], PTb[:, i % 2, kt * P:(kt + 1) * P],
                                  start=kt == 0, stop=kt == len(vs) - 1)
                    last.then_inc(S["at_pv"], 1)

                wait(pe, "proj_ev", layer, T_UV + 6)
                for i in range(NT * HEADS + 2):
                    if i < NT * HEADS:
                        scores(i)
                        ada_row(at["at"][i // KT], i % KT, 0)
                    if 1 <= i <= NT * HEADS:
                        flip(i - 1)
                    if i >= KT and i % KT == 2 and i < NT * HEADS:
                        ada_turn(at["at"][i // KT - 1], 0, GT)
                    if i >= 2:
                        weigh(i - 2)
                ada_turn(at["at"][-1], 0, GT)

                nfill = [0]

                def fill():
                    n = nfill[0]
                    nfill[0] += 1
                    if n % 4 == 0:
                        arrived(unit(7 + n // 4))
                    feature_tile(layer, T_G + n, unit(7 + n // 4), n % 4)

                wait(pe, "at_o", layer, 3)
                pe.wait_ge(ada_cp, at["at"][-1] + 1)
                for pair in range(3):
                    fill()
                    for d in range(2):
                        t = TILE[pair][d]
                        g = 2 * pair + d
                        X, Y, Z = B[2 + 3 * d], B[3 + 3 * d], B[4 + 3 * d]
                        if pair:
                            wait(pe, "s_or", layer, g - 1)
                        cols = slice(TCOL[t], TCOL[t] + P)
                        for h in range(DNH):
                            hs = slice(h * P, (h + 1) * P)
                            mm(X[:, hs], gg[:, t, 4 * d + h:4 * d + h + 1].to_broadcast([P, P]), inclU if d == 0 else inclL, start=True, stop=True)
                        for h in range(DNH):
                            hs = slice(h * P, (h + 1) * P)
                            mm(Y[:, hs], cv[:, 4 + h, cols], cv[:, 4 + h, cols], start=True, stop=True)
                        for h in range(DNH):
                            hs = slice(h * P, (h + 1) * P)
                            last = mm(Z[:, hs], cv[:, 4 + h, cols], cv[:, h, cols], start=True, stop=True)
                        last.then_inc(S["d_in"], 1)
                    fill()
                    for d in range(2):
                        wait(pe, "d_m", layer, 2 * pair + d + 1)
                        for h in range(DNH):
                            last = tr(B[2 + 3 * d][:, h * P:(h + 1) * P], dn(d, B_M)[:, h])
                        last.then_inc(S["d_mt"], 1)
                    for s in range(1, len(LEVELS)):
                        fill()
                        for d in range(2):
                            n = 10 * pair + 2 * (s - 1) + d + 1
                            wait(pe, "d_ct", layer, n)
                            if s == 1:
                                wait(pe, "d_t1", layer, 2 * pair + d + 1)
                            else:
                                wait(pe, "d_up", layer, n - 2)
                            for h in range(DNH):
                                last = mm(B[2 + 3 * d][:, h * P:(h + 1) * P], dn(d, B_CT)[:, h], dn(d, B_T)[:, h], start=True, stop=True)
                            last.then_inc(S["d_w"], 1)
                        for d in range(2):
                            n = 10 * pair + 2 * (s - 1) + d + 1
                            wait(pe, "d_we", layer, n)
                            for h in range(DNH):
                                hs = slice(h * P, (h + 1) * P)
                                if s < len(LEVELS) - 1:
                                    mm(B[3 + 3 * d][:, hs], dn(d, B_U)[:, h], dn(d, B_W)[:, h], start=True, stop=True)
                            for h in range(DNH):
                                hs = slice(h * P, (h + 1) * P)
                                last = mm(B[4 + 3 * d][:, hs], dn(d, B_W)[:, h], dn(d, B_U)[:, h], start=True, stop=True)
                            last.then_inc(S["d_du"], 1)
                    for d in range(2):
                        g = 2 * pair + d
                        wait(pe, "d_up", layer, 10 * pair + 8 + d + 1)
                        for h in range(DNH):
                            mm(B[2 + 3 * d][:, h * P:(h + 1) * P], dn(d, B_U)[:, h], dn(d, B_VU)[:, h], start=True, stop=True)
                        for h in range(DNH):
                            last = mm(B[3 + 3 * d][:, h * P:(h + 1) * P], dn(d, B_KW)[:, h], dn(d, B_U)[:, h], start=True, stop=True)
                        last.then_inc(S["d_uw"], 1)
                    for step in range(2):
                        for d in range(2):
                            g, n = 2 * pair + d, 4 * pair + 2 * step + d
                            X = B[2 + 3 * d]
                            ch = step if d == 0 else 1 - step
                            r = slice(CHUNK * ch, CHUNK * (ch + 1))
                            wait(pe, "d_uwe", layer, g + 1)
                            if step:
                                wait(pe, "s_st", layer, n - 1)
                            elif pair == 1:
                                pe.wait_ge(st_in, 32 * (layer + 1))
                            for h in range(DNH):
                                last = mm(X[r, h * P:(h + 1) * P], dn(d, B_KW)[:, h, r], state[:, d, h], start=True, stop=True)
                            last.then_inc(S["s_ws"], 1)
                        if step == 0:
                            fill()
                        for d in range(2):
                            g, n = 2 * pair + d, 4 * pair + 2 * step + d
                            Y, Z = B[3 + 3 * d], B[4 + 3 * d]
                            ch = step if d == 0 else 1 - step
                            r = slice(CHUNK * ch, CHUNK * (ch + 1))
                            wait(pe, "s_vn", layer, n + 1)
                            wait(pe, "d_kd", layer, g + 1)
                            for h in range(DNH):
                                mm(Z[:, h * P:(h + 1) * P], dn(d, B_KD)[r, h], dn(d, B_VN)[r, h], start=True, stop=True)
                            for h in range(DNH):
                                hs = slice(h * P, (h + 1) * P)
                                mm(Y[r, hs], dn(d, B_QEG)[:, h, r], state[:, d, h], start=True, stop=False)
                                last = mm(Y[r, hs], dn(d, B_QK)[r, h, r], dn(d, B_VN)[r, h], start=False, stop=True)
                            last.then_inc(S["s_o"], 1)
                assert nfill[0] == 24
                wait(pe, "proj_ev", layer, T_Z)
                ada_units(at["z"], 0)
                pe.wait_ge(ada_cp, at["z"][-1] + 1)
                wait(pe, "s_or", layer, 6)
                token_tiles(layer, T_Z, unit(13))
                oc_unit, = at["oc"]
                for k in range(KT):
                    ada_row(oc_unit, k, 6)
                for t in range(NT):
                    if t == 0:
                        wait(pe, "oc_v", layer, 1)
                    for h in range(DNH):
                        last = tr(B[2 + t][:, h * P:(h + 1) * P], osum[:, t, h * P:(h + 1) * P])
                    last.then_inc(S["oc_mm"], 1)
                wait(pe, "oc_ev", layer, 3)
                ada_turn(oc_unit, 6, KK_)
                for m in range(8):
                    if m == 1:
                        pe.wait_ge(ada_cp, oc_unit + 1)
                    if m % 2 == 0:
                        arrived(unit(14 + m // 2))
                    if m >= 2:
                        wait(pe, "br_ev", layer, m - 1)
                    w = wslot(unit(14 + m // 2), 12, 256)
                    for b in range(3):
                        for k in range(4):
                            last = mm(B[2 + 3 * (m % 2) + b][:, 0:TOK], w[:, 4 * b + k, (m % 2) * P:(m % 2 + 1) * P], oT[:, b, k],
                                      start=k == 0, stop=k == 3)
                    last.then_inc(S["br_mm"], 1)
                wait(pe, "br_ev", layer, 8)
                for m in range(8):
                    if m % 4 == 0:
                        arrived(unit(18 + m // 4))
                    if m >= 2:
                        wait(pe, "wo_ev", layer, m - 1)
                    w = wslot(unit(18 + m // 4), KT, 512)
                    for k in range(KT):
                        last = mm(B[m % 2][:, 0:TOK], w[:, k, (m % 4) * P:(m % 4 + 1) * P], merged[:, k], start=k == 0, stop=k == KT - 1)
                    last.then_inc(S["wo_mm"], 1)
                sum_squares(layer, 2, sqP)
                ada_units(at["n3"], 6)
                sum_squares(layer, 3, sqT)
                ada_units(at["h3"], 6)
                wait(pe, "h_a", layer, 8)
                wait(pe, "h_v", layer, 8)

                def gate_up(i, r, n, slot_unit, w0):
                    k0 = slot(slot_unit) * SLOT
                    w = ring[:, k0:k0 + 16 * n].rearrange("p (g k n) -> p g k n", g=2, k=KT)
                    for g, (done, used) in enumerate(((gu_g, gu_s), (gu_u, gu_h))):
                        if w0 is not None:
                            pe.wait_ge(used, w0)
                        for k in range(KT):
                            last = mm(B[2 * g + r][:, 0:TOK], w[:, g, k, (r % (n // P)) * P:(r % (n // P) + 1) * P], hT[:, k],
                                      start=k == 0, stop=k == KT - 1)
                        last.then_inc(done, 1)

                if layer == 0:
                    for i in range(3):
                        arrived(at_ring("ff", i))
                        for r in range(2):
                            gate_up(2 * i + r, r, 256, at_ring("ff", i), 2 * i + r - 1 if i else None)
                    with pe.Fori(0, 2) as it:
                        for j in range(4):
                            u = at_ring("ff", 3 + j)
                            pe.wait_ge(s_slot[slot(u)], full(u) + (full(u + 4) - full(u)) * it)
                            for r in range(2):
                                gate_up(0, r, 256, u, 8 * it + 6 + 2 * j + r - 1)
                    pe.wait_ge(gu_h, FG)
                    for m in range(8):
                        u = at_ring("ff", FF_GU + m)
                        arrived(u)
                        if m >= 2:
                            pe.wait_ge(down_ev, m - 1)
                        w = wslot(u, FG, P)
                        for k in range(FG):
                            last = mm(B[4 + m % 2][:, 0:TOK], w[:, k], hid[:, k], start=k == 0, stop=k == FG - 1)
                        last.then_inc(down_mm, 1)
                else:
                    pe.wait_ge(ada_cp, 2 * ADA_U)
                    for t in range(NT):
                        for k in range(KT):
                            last = mm(B[6][:, NE * t:NE * (t + 1)], hT[:, k, t * P:(t + 1) * P], v3(rtw[:, :], KT)[:, k],
                                      start=k == 0, stop=k == KT - 1)
                    last.then_inc(rl_mm, 1)
                    for n in range(2 * NT):
                        t, half = divmod(n, 2)
                        for k in range(4):
                            last = tr(B[H_BANK[n]][:, k * P:(k + 1) * P], hT[:, 4 * half + k, t * P:(t + 1) * P])
                        last.then_inc(ht_mm, 1)
                    pe.wait_ge(rl_ok, 1)
                    pe.wait_ge(route_in, 16)
                    for t in range(NT + 1):
                        c0 = 32 + NE * t
                        for a in range(min(t + 1, NT)):
                            last = mm(B[6][:, c0:c0 + NE], tri if a == t else ones, sel2[0][:, a], start=a == 0,
                                      stop=a == min(t, NT - 1))
                    last.then_inc(rk_mm, 1)

                    def gather():
                        for m in range(KT):
                            for t in range(NT):
                                last = mm(B[4 + m // 4][:, (m % 4) * P:(m % 4 + 1) * P], h2tok[:, t, m * P:(m + 1) * P], esel[:, t],
                                          start=t == 0, stop=t == NT - 1)
                            if m % 4 == 3:
                                last.then_inc(ga_mm, 1)

                    def scatter(i):
                        pe.wait_ge(yt_ok, 2 * i + 2)
                        pe.wait_ge(wt_ev, i + 1)
                        for m in range(KT):
                            pe.wait_ge(sc_ad, KT * i + (m if m else 1))
                            mm(B[6 + m % 2][:, 0:TOK], ytok[:, m * P:(m + 1) * P], scatT, start=True, stop=True).then_inc(sc_mm, 1)

                    pe.wait_ge(ht_ev, 2 * NT)
                    pe.wait_ge(sel_ok, 1)
                    gather()
                    n_items = pe.value_load(table[0:1, NI:NI + 1], min_val=MIN_ITEMS, max_val=NI - 1)
                    with pe.Fori(0, n_items) as i:
                        pe.wait_ge(ga_ev, 2 * i + 2)
                        for j in range(M_GU):
                            n = 256 if j < M_GU - 1 else P
                            pe.wait_ge(m_sem(j), m_full(j, i))
                            if j >= 2:
                                pe.wait_ge(mh_ok, M_GU * i + j - 1)
                            w = m_place(j)[:, 0:16 * n].rearrange("p (g k n) -> p g k n", g=2, k=KT)
                            for g in range(2):
                                for m in range(n // P):
                                    for k in range(KT):
                                        c0 = g * n + m * P
                                        last = mm(B[j % 2][:, c0:c0 + SLOTS], w[:, g, k, m * P:(m + 1) * P], xg[:, k],
                                                  start=k == 0, stop=k == KT - 1)
                            last.then_inc(mg_mm, 1)
                            if j == 0:
                                scatter(i)
                        pe.wait_ge(sel_ok, i + 2)
                        pe.wait_ge(sc_ad, KT * i + KT)
                        for t in range(NT):
                            last = tr(B[6][:, t * P:(t + 1) * P], wsel[:, t])
                        last.then_inc(wt_mm, 1)
                        gather()
                        pe.wait_ge(mh_ok, M_GU * i + M_GU)
                        for j in range(M_DN):
                            pe.wait_ge(m_sem(M_GU + j), m_full(M_GU + j, i))
                            w = m_place(M_GU + j)[:, 0:FE * 256].rearrange("p (k n) -> p k n", k=FE)
                            for k in range(FE):
                                last = mm(B[2 + j // 2][:, 256 * (j % 2):256 * (j % 2 + 1)], ehid[:, k], w[:, k], start=k == 0,
                                          stop=k == FE - 1)
                            last.then_inc(dn_mm, 1)
                    scatter(n_items)
                sum_squares(layer, 4, sqP)
                ada_units(at["n4"], 6)
            wait(pe, "x_new", DEPTH, 0)
            for t in range(NT):
                for half in range(2):
                    for k in range(4):
                        last = tr(B[2 + 2 * t + half][:, k * P:(k + 1) * P], xT[:, 4 * half + k, t * P:(t + 1) * P])
                    last.then_inc(xo_mm, 1)

        @block.scalar
        def _(act):
            go = nc.scalar.activation
            link = linker(act, act_step)

            def copy(out, in_):
                return go(out, in_, ACT.Copy)

            act.wait_ge(rt_ev, 4)
            go(rows[:, 160:176], rows[:, 160:176], ACT.Silu).then_inc(sc_ok, 1)
            for t in range(NT):
                for half in range(2):
                    act.wait_ge(xt_mm, 2 * t + half + 1)
                    copy(xT[:, 4 * half:4 * half + 4, t * P:(t + 1) * P], v3(B[2 + 2 * t + half][:, :], 4)).then_inc(xt_ev, 1)

            def square(src, dst):
                go(dst, src, ACT.Square).then_inc(S["sq"], 1)

            def root(layer, q):
                wait(act, "stat", layer, q)
                go(rs[:, :], B[2][:, 0:TOK], ACT.Sqrt, bias=eps1, scale=1.0 / D).then_inc(S["root"], 1)

            def modulate(layer, q, a):
                wait(act, "xn", layer, q)
                act.wait_ge(mod_ok, 4 * layer + (1 if a == 0 else 3))
                for k in range(4):
                    for s, lo, hi in SEG:
                        last = go(hT[:, k, lo:hi], hT[:, k, lo:hi], ACT.Identity, bias=mod[:, layer, a, k, s:s + 1],
                                  scale=mod[:, layer, a + 1, k, s:s + 1])
                    last.then_inc(S["h_a"], 1)

            def ada_copy(n, b, buf):
                act.wait_ge(ada_mm, n + 1)
                copy(ada_rows(n, buf), B[b + n % 2][0:2, :]).then_inc(ada_ev, 1)

            act.wait_ge(xt_ev, 2 * NT)
            for layer in range(DEPTH):
                at = ADA_AT[layer]

                def evac(n, out, func=ACT.Copy, width=512):
                    wait(act, "proj_mm", layer, n + 1)
                    go(out, B[n % 2][:, 0:width], func).then_inc(S["proj_ev"], 1)

                wait(act, "x_new", layer, 0)
                square(xT, sqT)
                root(layer, 1)
                if layer == 0:
                    for n in ADA_FIRST:
                        ada_copy(n, 0, KK_)
                modulate(layer, 1, 0)
                for n in at["n1"]:
                    ada_copy(n, 6, KK_)
                wait(act, "pads", layer, 1)
                for j in range(12):
                    wait(act, "proj_mm", layer, j + 1)
                    copy(pre[:, j, 2:2 + CTX], B[j % 2][:, 0:CTX])
                    copy(pre[:, j, CTX + 6:CTX + 6 + LAT], B[j % 2][:, CTX:TOK]).then_inc(S["proj_ev"], 1)
                for t in range(NT):
                    evac(T_BA + t, ba[:, t], width=16)
                act.wait_ge(parked, 16 * (layer + 1))
                for t in range(NT):
                    wait(act, "proj_mm", layer, T_A + t + 1)
                    for a in range(2):
                        src = B[(T_A + t) % 2][:, 256 * a:256 * a + 256].rearrange("p (b c d) -> p b c d", b=2, c=2)
                        dst = qkv[:, t, 256 * a:256 * a + 256].rearrange("p (c b d) -> p b c d", b=2, c=2)
                        last = copy(dst, src)
                    last.then_inc(S["proj_ev"], 1)
                for t in range(NT):
                    evac(T_A + 3 + t, qkv[:, t, 512:1024])
                wait(act, "proj_ev", layer, T_A + 6)
                go(asq, qkv[:, :, 0:768], ACT.Square).then_inc(S["a_sq"], 1)
                go(beta, ba[:, :, 0:8], ACT.Sigmoid)
                act.wait_ge(lw_in, 16 * (7 + 6 * layer))
                wait(act, "ba_v", layer, 1)
                link(go(t2, t1, ACT.Abs))
                link(go(t2, t2, ACT.Exp, scale=-1.0))
                go(expa, expa, ACT.Exp)
                go(t2, t2, ACT.Ln, bias=one1).then_inc(S["ba_l"], 1)
                wait(act, "conv", layer, 12)
                for i in range(3):
                    last = go(CV[:, 4 * i * COUT:4 * (i + 1) * COUT], CV[:, 4 * i * COUT:4 * (i + 1) * COUT], ACT.Silu)
                    last.then_inc(S["silu"], 1)
                wait(act, "silu", layer, 3)
                go(GT[:, 12 * CROW:12 * CROW + 8 * COUT], CV[:, 0:8 * COUT], ACT.Square).then_inc(S["dsq"], 1)
                for j in range(8):
                    wait(act, "dst", layer, j + 1)
                    go(dsq[:, j], B[2 + j % 2][:, 0:COUT], ACT.Sqrt, bias=eps128 if j < 4 else eps1,
                       scale=float(DK) if j < 4 else 1.0).then_inc(S["droot"], 1)
                wait(act, "a_ss", layer, 1)
                go(ass, ass, ACT.Sqrt, bias=eps1, scale=1.0 / HD).then_inc(S["a_rt"], 1)
                for i in range(6):
                    evac(T_UV + i, uB[:, i] if i < 3 else vB[:, i - 3], ACT.Gelu_apprx_tanh)
                wait(act, "proj_ev", layer, T_UV + 6)
                wait(act, "qkn", layer, 1)
                for t in range(NT):
                    link(go(gsc, vB[:, t], ACT.Square, accum_out=vss[:, t:t + 1]))
                go(vss, vss, ACT.Sqrt, bias=eps1, scale=1.0 / 512).then_inc(S["v_rt"], 1)
                wait(act, "gc_v", layer, 1)
                go(edec, edec, ACT.Exp)
                go(egl, egl, ACT.Exp)
                go(eg, gcs, ACT.Exp).then_inc(S["gc_e"], 1)
                wait(act, "kvt_mm", layer, 3)
                for i in range(6):
                    wait(act, "kvt_mm", layer, i + 1)
                    dst = vtok[:, i] if i < 3 else ktok[:, i - 3]
                    copy(dst, v3(B[(5, 6, 7, 2, 3, 4)[i]][:, :], 4)).then_inc(S["kvt_ev"], 1)
                for i in range(6):
                    wait(act, "tr_mm", layer, i + 1)
                    if i < 3:
                        copy(qTt[:, :, i * P:(i + 1) * P], v3(B[2 + i][:, :], 4)).then_inc(S["tr_ev"], 1)
                    elif i < 5:
                        copy(kTt[:, :, 256 * (i - 3):256 * (i - 2)], v3(B[2 + i][:, :], 2)).then_inc(S["tr_ev"], 1)
                    else:
                        copy(wsT, B[7][:, :]).then_inc(S["tr_ev"], 1)
                for t in range(NT):
                    wait(act, "b_t", layer, t + 1)
                    copy(oT[:, 1, :, t * P:(t + 1) * P], v3(B[5 + t][:, :], 4)).then_inc(S["b_ev"], 1)
                n_at = NT * HEADS
                for i in range(n_at + 3):
                    if i < n_at:
                        w = P if i < HEADS else TOK
                        wait(act, "at_m", layer, i + 1)
                        if i >= 2:
                            wait(act, "at_t", layer, i - 1)
                        go(Pb[:, i % 2, 0:w], B[2 + i % 2][:, 0:w], ACT.Exp, bias=anm[:, i:i + 1], scale=HD ** -0.5,
                           accum_out=ars[:, i:i + 1]).then_inc(S["at_e"], 1)
                    if i >= KT and i % KT == 1 and i < n_at:
                        ada_copy(at["at"][i // KT - 1], 0, GT)
                    if 1 <= i <= n_at:
                        j = i - 1
                        w = P if j < HEADS else TOK
                        wait(act, "at_t", layer, j + 1)
                        if j >= 2:
                            wait(act, "at_pv", layer, j - 1)
                        copy(PTb[:, j % 2, 0:w], B[4 + j % 2][:, 0:w]).then_inc(S["at_pt"], 1)
                    if i >= 10 and i % 8 == 2:
                        t = i // 8 - 1
                        wait(act, "at_pv", layer, 8 * (t + 1))
                        copy(oT[:, 0, :, t * P:(t + 1) * P], v3(B[6 + t % 2][:, :], 4)).then_inc(S["at_o"], 1)
                ada_copy(at["at"][-1], 0, GT)
                nfill = [0]

                def gate():
                    n = nfill[0]
                    nfill[0] += 1
                    evac(T_G + n, gates[:, n], width=TOK)

                for pair in range(3):
                    gate()
                    for d in range(2):
                        wait(act, "d_d0", layer, 2 * pair + d + 1)
                        go(dn(d, B_QEG), v3(B[2 + 3 * d][:, :], 4), ACT.Exp)
                        go(dn(d, B_M), dn(d, B_M), ACT.Exp, scale=-1.0)
                        go(dn(d, B_QK), dn(d, B_QK), ACT.Exp).then_inc(S["d_e"], 1)
                    gate()
                    for s in range(1, len(LEVELS)):
                        gate()
                        for d in range(2):
                            wait(act, "d_w", layer, 10 * pair + 2 * (s - 1) + d + 1)
                            copy(dn(d, B_W), v3(B[2 + 3 * d][:, :], 4)).then_inc(S["d_we"], 1)
                    for d in range(2):
                        wait(act, "d_uw", layer, 2 * pair + d + 1)
                        copy(dn(d, B_VU), v3(B[2 + 3 * d][:, :], 4))
                        copy(dn(d, B_KW), v3(B[3 + 3 * d][:, :], 4)).then_inc(S["d_uwe"], 1)
                    gate()
                for n in at["z"]:
                    ada_copy(n, 0, KK_)
                for t in range(NT):
                    evac(T_Z + t, zs[:, t], ACT.Silu)
                go(RX[:, 6144:7680], OT[:, 3072:4608], ACT.Square).then_inc(S["oc_sq"], 1)
                wait(act, "oc_ss", layer, 1)
                go(oss, oss, ACT.Sqrt, bias=eps1, scale=1.0 / DK).then_inc(S["oc_rt"], 1)
                wait(act, "proj_ev", layer, T_Z)
                go(GT[:, :], GT[:, :], ACT.Sigmoid).then_inc(S["gsig"], 1)
                wait(act, "oc_mm", layer, 3)
                for t in range(NT):
                    copy(oT[:, 2, :, t * P:(t + 1) * P], v3(B[2 + t][:, :], 4)).then_inc(S["oc_ev"], 1)
                ada_copy(at["oc"][0], 6, KK_)
                for m in range(8):
                    wait(act, "wo_mm", layer, m + 1)
                    copy(yT[:, m], B[m % 2][:, 0:TOK]).then_inc(S["wo_ev"], 1)
                wait(act, "wo_ev", layer, 8)
                square(yT, sqP)
                root(layer, 2)
                for n in at["n3"]:
                    ada_copy(n, 6, KK_)
                wait(act, "x_new", layer, 1)
                square(xT, sqT)
                root(layer, 3)
                modulate(layer, 2, 3)
                for n in at["h3"]:
                    ada_copy(n, 6, KK_)

                def silu(idx, r, prev):
                    act.wait_ge(gu_g, idx + 1)
                    if prev is not None:
                        act.wait_ge(gu_h, prev)
                    go(sgb[:, r], B[r][:, 0:TOK], ACT.Silu).then_inc(gu_s, 1)

                if layer == 0:
                    for i in range(6):
                        silu(i, i % 2, i - 1 if i >= 2 else None)
                    with act.Fori(0, 2) as it:
                        for i in range(8):
                            silu(8 * it + 6 + i, i % 2, 8 * it + 5 + i)
                    act.wait_ge(down_ev, 8)
                else:
                    for n in range(2 * NT):
                        act.wait_ge(ht_mm, n + 1)
                        copy(h2tok[:, n // 2, 512 * (n % 2):512 * (n % 2 + 1)], B[H_BANK[n]][:, :]).then_inc(ht_ev, 1)
                    act.wait_ge(rl_c, 1)
                    go(m8[:, 1::8], m8[:, 1::8], ACT.Exp).then_inc(rl_e, 1)

                    def gathered(i):
                        for half in range(2):
                            act.wait_ge(ga_mm, 2 * i + half + 1)
                            copy(xg[:, 4 * half:4 * half + 4], v3(B[4 + half][:, :], 4)).then_inc(ga_ev, 1)

                    gathered(0)
                    n_items = act.value_load(table[0:1, NI:NI + 1], min_val=MIN_ITEMS, max_val=NI - 1)
                    with act.Fori(0, n_items) as i:
                        for j in range(M_GU):
                            n = 256 if j < M_GU - 1 else P
                            act.wait_ge(mg_mm, M_GU * i + j + 1)
                            if j >= 2:
                                act.wait_ge(mh_ok, M_GU * i + j - 1)
                            go(esg[:, j % 2, 0:n], B[j % 2][:, 0:n], ACT.Silu).then_inc(msg_ok, 1)
                        act.wait_ge(wt_mm, i + 1)
                        copy(scatT, B[6][:, 0:TOK]).then_inc(wt_ev, 1)
                        gathered(i + 1)
                        for half in range(2):
                            act.wait_ge(dn_mm, M_DN * i + 2 * half + 2)
                            copy(ytok[:, 512 * half:512 * (half + 1)], B[2 + half][:, :]).then_inc(yt_ok, 1)
                    act.wait_ge(sc_ad, KT * n_items + KT + 1)
                square(yT, sqP)
                root(layer, 4)
                for n in at["n4"]:
                    ada_copy(n, 6, KK_)
            for t in range(NT):
                for half in range(2):
                    act.wait_ge(xo_mm, 2 * t + half + 1)
                    copy(v3(GT[:, 0:3072], NT)[:, t, 512 * half:512 * (half + 1)], B[2 + 2 * t + half][:, :]).then_inc(xo_ev, 1)

        @block.vector
        def _(dve):
            v = nc.vector
            link = linker(dve, dve_step)

            def note(ins, name, layer, n):
                ins.then_inc(S[name], 1)
                wait(dve, name, layer, n)

            def note1(ins, signal):
                ins.then_inc(signal, 1)
                dve.wait_ge(signal, 1)

            def bc(ap, n):
                return ap.unsqueeze(2).to_broadcast([P, ap.shape[1], n])

            dve.wait_ge(cst_in, 32)
            v.tensor_copy(lmask[:, :], RX[:, 6144:6144 + NMASK]).then_inc(bf_ok, 1)
            for i, (lo, n) in enumerate(((0, 64), (64, 96), (160, 24), (184, 120))):
                dve.wait_ge(rt_mm, 4)
                v.tensor_copy(rows[:, lo:lo + n], B[0][:, i * P:i * P + n]).then_inc(rt_ev, 1)
            dve.wait_ge(rt_ev, 4)
            dve.wait_ge(xt_ev, 2 * NT)

            def ada_take(n, b):
                layer, i = divmod(n, ADA_U)
                dve.wait_ge(ada_t, n + 1)
                dst = mod[:, layer].rearrange("p a k s -> p (a k) s")[:, 4 * i:4 * i + 4]
                v.tensor_tensor(dst, v3(B[b + n % 2][:, 0:8], 4), bc(adab[:, layer, 4 * i:4 * i + 4], 2), ALU.add).then_inc(ada_cp, 1)
                if i in ADA_DONE:
                    dve.wait_ge(ada_cp, n + 1)
                    a, g = ADA_DONE[i]
                    m = mod[:, layer, a]
                    if a in (1, 4):
                        link(v.tensor_scalar(m, m, 1.0, None, ALU.add))
                    v.tensor_tensor(m, m, bc(nrmT[:, layer, g], 2), ALU.mult).then_inc(mod_ok, 1)

            def rstd(layer, q):
                wait(dve, "root", layer, q)
                note(v.reciprocal(rs[:, :], rs[:, :]), "rinv", layer, q)

            def normed(layer, n, a, units=()):
                note(v.tensor_tensor(hT, xT, rs[:, :].unsqueeze(1).to_broadcast([P, KT, TOK]), ALU.mult), "xn", layer, n)
                for u in units:
                    ada_take(u, 0)
                dve.wait_ge(mod_ok, 4 * layer + (1 if a == 0 else 3))
                for k in range(4, 8):
                    for s, lo, hi in SEG:
                        last = v.tensor_scalar(hT[:, k, lo:hi], hT[:, k, lo:hi], mod[:, layer, a + 1, k, s:s + 1],
                                               mod[:, layer, a, k, s:s + 1], ALU.mult, ALU.add)
                    last.then_inc(S["h_v"], 1)

            def add_branch(layer, q, a, n):
                rstd(layer, q)
                link(v.tensor_tensor(yT, yT, rs[:, :].unsqueeze(1).to_broadcast([P, KT, TOK]), ALU.mult))
                dve.wait_ge(mod_ok, 4 * layer + (2 if a == 2 else 4))
                for k in range(KT):
                    for s, lo, hi in SEG:
                        last = v.scalar_tensor_tensor(xT[:, k, lo:hi], yT[:, k, lo:hi], mod[:, layer, a, k, s:s + 1], xT[:, k, lo:hi],
                                                      ALU.mult, ALU.add)
                note(last, "x_new", layer, n)

            for layer in range(DEPTH):
                at = ADA_AT[layer]
                rstd(layer, 1)
                normed(layer, 1, 0, ADA_FIRST if layer == 0 else ())
                for n in at["n1"]:
                    ada_take(n, 6)
                v.memset(pre[:, :, 0:2], 0.0)
                v.memset(pre[:, :, CTX + 2:CTX + 6], 0.0)
                note(v.memset(pre[:, :, CROW - 2:CROW], 0.0), "pads", layer, 1)
                for j in range(12):
                    wait(dve, "proj_ev", layer, j + 1)
                    w = cwT[:, layer, :, j]
                    link(v.tensor_scalar(cv[:, j], pre[:, j, 0:COUT], w[:, 0:1], None, ALU.mult))
                    for k in range(1, CONV_K):
                        ins = v.scalar_tensor_tensor(cv[:, j], pre[:, j, k:k + COUT], w[:, k:k + 1], cv[:, j], ALU.mult, ALU.add)
                        if k < CONV_K - 1:
                            link(ins)
                    ins.then_inc(S["conv"], 1)
                wait(dve, "proj_ev", layer, T_BA + 3)
                dve.wait_ge(lw_in, 16 * (7 + 6 * layer))
                note(v.tensor_tensor(t1, ba[:, :, 8:16], dtb.unsqueeze(1).to_broadcast([P, NT, 8]), ALU.add), "ba_v", layer, 1)
                wait(dve, "a_sq", layer, 1)
                v.tensor_reduce(ass, asq.rearrange("p t (h d) -> p (t h) d", d=HD), AX.X, ALU.add).then_inc(S["a_ss"], 1)
                wait(dve, "ba_l", layer, 1)
                link(v.scalar_tensor_tensor(gg, t1, 0.0, t2, ALU.max, ALU.add))
                link(v.scalar_tensor_tensor(gg, gg, -1.0, expa.unsqueeze(1).to_broadcast([P, NT, 8]), ALU.mult, ALU.mult))
                v.tensor_scalar(gm[:, :, 0], gg, chsel[:, 0:1], None, ALU.mult)
                v.tensor_scalar(gm[:, :, 1], gg, chsel[:, 1:2], None, ALU.mult).then_inc(S["g_ok"], 1)
                wait(dve, "droot", layer, 8)
                link(v.reciprocal(dsq, dsq))
                v.tensor_tensor(cv[:, 0:8], cv[:, 0:8], dsq, ALU.mult).then_inc(S["qkn"], 1)
                wait(dve, "a_rt", layer, 1)
                link(v.reciprocal(ass, ass))
                qk = qkv[:, :, 0:768].rearrange("p t (h d) -> p t h d", d=HD)
                link(v.tensor_tensor(qk, qk, v3(ass, NT).unsqueeze(3).to_broadcast([P, NT, 12, HD]), ALU.mult))
                for t in range(NT):
                    q2 = qkv[:, t, 0:768].rearrange("p (h d) -> p h d", d=HD)
                    v.tensor_tensor(q2[:, 0:8], q2[:, 0:8], qkgain[:, 0:64].unsqueeze(1).to_broadcast([P, 8, HD]), ALU.mult)
                    last = v.tensor_tensor(q2[:, 8:12], q2[:, 8:12], qkgain[:, 64:128].unsqueeze(1).to_broadcast([P, 4, HD]), ALU.mult)
                link(last)
                for t in (1, 2):
                    q5 = qkv[:, t, 0:768].rearrange("p (h a f q) -> p h a f q", h=12, a=2, f=2)
                    x1, x2 = q5[:, :, :, 0], q5[:, :, :, 1]
                    cos, sin = (rope[:, t - 1, f].unsqueeze(1).to_broadcast([P, 12, 2, HD // 4]) for f in range(2))
                    for o, x, f in ((rt[0], x1, cos), (rt[1], x2, sin), (rt[2], x1, sin), (rt[3], x2, cos)):
                        last = v.tensor_tensor(o, x, f, ALU.mult)
                    link(last)
                    v.tensor_tensor(x1, rt[0], rt[1], ALU.subtract)
                    last = v.tensor_tensor(x2, rt[2], rt[3], ALU.add)
                    if t == 1:
                        link(last)
                last.then_inc(S["a_ok"], 1)
                wait(dve, "v_rt", layer, 1)
                link(v.reciprocal(vss, vss))
                for t in range(NT):
                    last = v.scalar_tensor_tensor(vB[:, t], vB[:, t], vss[:, t:t + 1], ggain, ALU.mult, ALU.mult)
                last.then_inc(S["v_ok"], 1)
                wait(dve, "gc_mm", layer, 1)
                gps = B[4][:, 0:96].rearrange("p (t n) -> p t n", t=NT)
                link(v.tensor_copy(gcs, gps[:, :, 0:8]))
                v.tensor_tensor(edec, gps[:, :, 8:16], gcs, ALU.subtract)
                v.tensor_copy(egl.rearrange("p t c n -> p t (c n)"), gps[:, :, 16:32]).then_inc(S["gc_v"], 1)
                wait(dve, "gc_e", layer, 1)
                v.tensor_tensor(beg, beta, eg, ALU.mult).then_inc(S["beg"], 1)
                for t in range(NT):
                    wait(dve, "b_mm", layer, t + 1)
                    for g in range(4):
                        gs = slice(g * P, (g + 1) * P)
                        last = v.scalar_tensor_tensor(uB[:, t, gs], B[2 + t][:, gs], bsT[:, layer, g:g + 1], uB[:, t, gs],
                                                      ALU.add, ALU.mult)
                    last.then_inc(S["b_v"], 1)
                n_at = NT * HEADS
                for i in range(n_at + 1):
                    if i >= KT and i % KT == 3:
                        ada_take(at["at"][i // KT - 1], 0)
                    if i < n_at:
                        w = P if i < HEADS else TOK
                        wait(dve, "at_s", layer, i + 1)
                        link(v.tensor_reduce(amx[:, i:i + 1], B[2 + i % 2][:, 0:w], AX.X, ALU.max))
                        v.tensor_scalar(anm[:, i:i + 1], amx[:, i:i + 1], -(HD ** -0.5), None, ALU.mult).then_inc(S["at_m"], 1)
                    if i:
                        j = i - 1
                        w = P if j < HEADS else TOK
                        wait(dve, "at_e", layer, j + 1)
                        link(v.reciprocal(ars[:, j:j + 1], ars[:, j:j + 1]))
                        v.tensor_scalar(Pb[:, j % 2, 0:w], Pb[:, j % 2, 0:w], ars[:, j:j + 1], None, ALU.mult).then_inc(S["at_p"], 1)
                ada_take(at["at"][-1], 0)
                dve.wait_ge(kv_out, 32 * (layer + 1))
                wait(dve, "at_o", layer, 3)
                dve.wait_ge(bf_ok, 1)
                for pair in range(3):
                    for d in range(2):
                        t = TILE[pair][d]
                        wait(dve, "d_in", layer, 2 * pair + d + 1)
                        link(v.tensor_tensor(dn(d, B_W), v3(B[2 + 3 * d][:, :], 4), bc(gcs[:, t, 4 * d:4 * d + 4], P), ALU.subtract))
                        v.tensor_scalar(dn(d, B_M), dn(d, B_W), 0.0, None, ALU.max)
                        v.tensor_scalar(dn(d, B_QK), dn(d, B_W), 0.0, None, ALU.min).then_inc(S["d_d0"], 1)
                    for d in range(2):
                        wait(dve, "d_pool", layer, 2 * pair + d + 1)
                        v.tensor_tensor(dn(d, B_QK), v3(B[4 + 3 * d][:, :], 4), dn(d, B_QK), ALU.mult)
                        v.tensor_tensor(dn(d, B_M), v3(B[3 + 3 * d][:, :], 4), dn(d, B_M), ALU.mult).then_inc(S["d_m"], 1)
                    for d in range(2):
                        g = 2 * pair + d
                        m0, m1 = (lm[:, 0, i].unsqueeze(1).to_broadcast([P, DNH, P]) for i in (d, 1 - d))
                        eye = ident.unsqueeze(1).to_broadcast([P, DNH, P])
                        wait(dve, "d_mt", layer, g + 1)
                        note(v.tensor_copy(dn(d, B_MT), v3(B[2 + 3 * d][:, :], 4)), "d_mtc", layer, g + 1)
                        v.tensor_tensor(dn(d, B_T), dn(d, B_M), m0, ALU.mult)
                        link(v.tensor_tensor(dn(d, B_U), dn(d, B_MT), m1, ALU.mult))
                        v.tensor_tensor(dn(d, B_T), dn(d, B_T), eye, ALU.add)
                        v.tensor_tensor(dn(d, B_U), dn(d, B_U), eye, ALU.add).then_inc(S["d_t1"], 1)
                    dve.wait_ge(S["d_t1"], PER["d_t1"] * layer + 2 * pair + 2)
                    for s in range(1, len(LEVELS)):
                        for d in range(2):
                            n = 10 * pair + 2 * (s - 1) + d + 1
                            wait(dve, "d_du", layer, n)
                            if s < len(LEVELS) - 1:
                                v.tensor_tensor(dn(d, B_T), dn(d, B_T), v3(B[3 + 3 * d][:, :], 4), ALU.add)
                            note(v.tensor_tensor(dn(d, B_U), dn(d, B_U), v3(B[4 + 3 * d][:, :], 4), ALU.add), "d_up", layer, n)
                    for step in range(2):
                        for d in range(2):
                            n = 4 * pair + 2 * step + d
                            ch = step if d == 0 else 1 - step
                            r = slice(CHUNK * ch, CHUNK * (ch + 1))
                            wait(dve, "s_ws", layer, n + 1)
                            v.tensor_tensor(dn(d, B_VN)[r], dn(d, B_VU)[r], v3(B[2 + 3 * d][r, :], 4), ALU.subtract).then_inc(S["s_vn"], 1)
                        for d in range(2):
                            n = 4 * pair + 2 * step + d
                            t = TILE[pair][d]
                            ch = step if d == 0 else 1 - step
                            wait(dve, "s_o", layer, n + 1)
                            for h in range(DNH):
                                last = v.scalar_tensor_tensor(state[:, d, h], state[:, d, h], egl[:, t, ch, 4 * d + h:4 * d + h + 1],
                                                              B[4 + 3 * d][:, h * P:(h + 1) * P], ALU.mult, ALU.add)
                            note(last, "s_st", layer, n + 1)
                    for d in range(2):
                        t = TILE[pair][d]
                        if pair == 1 or (pair == 0 and d == 0):
                            ins = v.tensor_copy(osum[:, t], B[3 + 3 * d][:, :])
                        else:
                            ins = v.tensor_tensor(osum[:, t], B[3 + 3 * d][:, :], osum[:, t], ALU.add)
                        note(ins, "s_or", layer, 2 * pair + d + 1)
                for n in at["z"]:
                    ada_take(n, 0)
                wait(dve, "oc_sq", layer, 1)
                v.tensor_reduce(oss, RX[:, 6144:7680].rearrange("p (n e) -> p n e", e=DK), AX.X, ALU.add).then_inc(S["oc_ss"], 1)
                wait(dve, "oc_rt", layer, 1)
                link(v.reciprocal(oss, oss))
                o12 = OT[:, 3072:4608].rearrange("p (n e) -> p n e", e=DK)
                link(v.tensor_tensor(o12, o12, bc(oss, DK), ALU.mult))
                link(v.tensor_tensor(o12, o12, dngain[:, :].unsqueeze(1).to_broadcast([P, 12, DK]), ALU.mult))
                wait(dve, "proj_ev", layer, T_Z + 3)
                v.tensor_tensor(osum, osum, zs, ALU.mult).then_inc(S["oc_v"], 1)
                ada_take(at["oc"][0], 6)
                wait(dve, "gsig", layer, 1)
                for m in range(8):
                    wait(dve, "br_mm", layer, m + 1)
                    for b in range(3):
                        last = v.tensor_tensor(btmp[b], B[2 + 3 * (m % 2) + b][:, 0:TOK], gates[:, 8 * b + m], ALU.mult)
                    link(last)
                    link(v.tensor_tensor(btmp[0], btmp[0], btmp[1], ALU.add))
                    note(v.tensor_tensor(merged[:, m], btmp[0], btmp[2], ALU.add), "br_ev", layer, m + 1)
                dve.wait_ge(unparked, 16 * (layer + 1))
                add_branch(layer, 2, 2, 1)
                for n in at["n3"]:
                    ada_take(n, 6)
                rstd(layer, 3)
                normed(layer, 2, 3)
                for n in at["h3"]:
                    ada_take(n, 6)

                def hidden(idx, r):
                    dve.wait_ge(gu_s, idx + 1)
                    dve.wait_ge(gu_u, idx + 1)
                    dst = hid[:, bass.ds(idx, 1)].rearrange("p a n -> p (a n)")
                    v.tensor_tensor(dst, B[2 + r][:, 0:TOK], sgb[:, r], ALU.mult).then_inc(gu_h, 1)

                if layer == 0:
                    for i in range(6):
                        hidden(i, i % 2)
                    with dve.Fori(0, 2) as it:
                        for i in range(8):
                            hidden(8 * it + 6 + i, i % 2)
                    for m in range(8):
                        dve.wait_ge(down_mm, m + 1)
                        v.tensor_copy(yT[:, m], B[4 + m % 2][:, 0:TOK]).then_inc(down_ev, 1)
                    dve.wait_ge(down_ev, 8)
                else:
                    note1(v.memset(RX[:, 3072:6144], 0.0), sc_ad)
                    dve.wait_ge(rl_mm, 1)
                    lg = v3(t1.rearrange("p t n -> p (t n)"), NT)
                    link(v.tensor_copy(lg, v3(B[6][:, 0:24], NT)))
                    idx = i8.bitcast(U32)
                    for t in range(NT):
                        link(v.max(m8[:, 8 * t:8 * t + 8], lg[:, t]))
                        link(v.max_index(idx[:, 8 * t:8 * t + 8], m8[:, 8 * t:8 * t + 8], lg[:, t]))
                    v.tensor_copy(i8f, idx)
                    v.tensor_tensor(m8[:, 1::8], m8[:, 1::8], m8[:, 0::8], ALU.subtract).then_inc(rl_c, 1)
                    dve.wait_ge(rl_e, 1)
                    link(v.tensor_scalar(m8[:, 0::8], m8[:, 1::8], 1.0, None, ALU.add))
                    link(v.reciprocal(m8[:, 0::8], m8[:, 0::8]))
                    link(v.tensor_tensor(m8[:, 1::8], m8[:, 1::8], m8[:, 0::8], ALU.mult))
                    sel, picked = sel2
                    for t in range(NT):
                        for j, (oh, pk) in enumerate(((oh0, sel), (oh1, picked))):
                            c0 = 8 * t + j
                            v.tensor_scalar(oh[:, t], iota8, i8f[:, c0:c0 + 1], m8[:, c0:c0 + 1], ALU.is_equal, ALU.mult)
                            last = v.tensor_scalar(pk[:, t], iota8, i8f[:, c0:c0 + 1], None, ALU.is_equal)
                    link(last)
                    v.tensor_tensor(comb, oh0, oh1, ALU.add)
                    note1(v.tensor_tensor(sel, sel, picked, ALU.add), rl_ok)
                    for half in range(2):
                        v.memset(ytok[:, 512 * half:512 * (half + 1)], 0.0).then_inc(yt_ok, 1)
                    v.memset(scatT, 0.0).then_inc(wt_ev, 1)
                    dve.wait_ge(rk_mm, 1)
                    v.tensor_tensor(rank, v3(B[6][:, 32:56], NT), sel, ALU.mult)
                    link(v.tensor_copy(cnt, B[6][:, 56:64]))
                    link(v.tensor_scalar(nit, cnt, 0.0, None, ALU.is_gt))
                    for n in range(1, NT):
                        link(v.scalar_tensor_tensor(nit, cnt, float(SLOTS * n), nit, ALU.is_gt, ALU.add))
                    link(v.tensor_scalar(nit[:, 0:1], nit[:, 0:1], 1.0, None, ALU.max))
                    link(v.tensor_tensor(tri8, before, nit.unsqueeze(1).to_broadcast([P, NE, NE]), ALU.mult))
                    link(v.tensor_reduce(e_lo, tri8, AX.X, ALU.add))
                    link(v.tensor_tensor(e_hi, e_lo, nit, ALU.add))
                    lo, hi = (x.unsqueeze(1).to_broadcast([P, NI, NE]) for x in (e_lo, e_hi))
                    v.tensor_tensor(own, lo, bc(item, NE), ALU.is_le)
                    link(v.tensor_tensor(own2, hi, bc(item, NE), ALU.is_gt))
                    link(v.tensor_tensor(own, own, own2, ALU.mult))
                    link(v.tensor_tensor(own2, own, iota8.unsqueeze(1).to_broadcast([P, NI, NE]), ALU.mult))
                    link(v.tensor_reduce(it_e, own2, AX.X, ALU.add))
                    v.tensor_copy(table[:, 0:NI], it_e)
                    v.tensor_copy(table[:, NI:NI + 1], e_hi[:, NE - 1:NE]).then_inc(tbl_ok, 1)
                    link(v.tensor_tensor(own2, own, lo, ALU.mult))
                    link(v.tensor_reduce(it_lo, own2, AX.X, ALU.add))
                    link(v.tensor_tensor(it_lo, item, it_lo, ALU.subtract))
                    link(v.tensor_scalar(it_lo, it_lo, float(SLOTS), None, ALU.mult))
                    own4 = own.unsqueeze(2).to_broadcast([P, NI, NT, NE])
                    link(v.tensor_tensor(oprod, own4, rank.unsqueeze(1).to_broadcast([P, NI, NT, NE]), ALU.mult))
                    link(v.tensor_reduce(it_rank, oprod, AX.X, ALU.add))
                    v.tensor_tensor(it_rank, it_rank, bc(it_lo, NT), ALU.subtract)
                    link(v.tensor_tensor(oprod, own4, comb.unsqueeze(1).to_broadcast([P, NI, NT, NE]), ALU.mult))
                    link(v.tensor_reduce(it_comb, oprod, AX.X, ALU.add))

                    def of_item(x, i):
                        ap = x[:, bass.ds(i, 1)].rearrange("p a t -> p (a t)")
                        return ap.unsqueeze(2).to_broadcast([P, NT, SLOTS])

                    def choose(i):
                        v.tensor_tensor(esel, slot1.unsqueeze(1).to_broadcast([P, NT, SLOTS]), of_item(it_rank, i),
                                        ALU.is_equal).then_inc(sel_ok, 1)

                    def add_up(i):
                        dve.wait_ge(sc_ad, KT * i + 1)
                        for m in range(KT):
                            dve.wait_ge(sc_mm, KT * i + m + 1)
                            v.tensor_tensor(yT[:, m], B[6 + m % 2][:, 0:TOK], yT[:, m], ALU.add).then_inc(sc_ad, 1)

                    choose(0)
                    n_items = dve.value_load(table[0:1, NI:NI + 1], min_val=MIN_ITEMS, max_val=NI - 1)
                    with dve.Fori(0, n_items) as i:
                        dve.wait_ge(sel_ok, i + 1)
                        dve.wait_ge(ga_mm, 2 * i + 2)
                        v.tensor_tensor(wsel, esel, of_item(it_comb, i), ALU.mult).then_inc(wsel_ok, 1)
                        dve.wait_ge(wsel_ok, i + 1)
                        choose(i + 1)
                        for j in range(M_GU):
                            n = 256 if j < M_GU - 1 else P
                            dve.wait_ge(msg_ok, M_GU * i + j + 1)
                            dst = GT[:, 2 * j * SLOTS:2 * j * SLOTS + n]
                            v.tensor_tensor(dst, B[j % 2][:, n:2 * n], esg[:, j % 2, 0:n], ALU.mult).then_inc(mh_ok, 1)
                            if j == 0:
                                add_up(i)
                    add_up(n_items)
                    dve.wait_ge(sc_ad, KT * n_items + KT + 1)
                add_branch(layer, 4, 5, 2)
                for n in at["n4"]:
                    ada_take(n, 6)


_INS = ["x_prompt", "x_sample", "cache_attn_k", "cache_attn_v", "state_delta", "c", "c_ctx", "ada_w", "ada_b", "norms", "w_in",
        "qk_norm", "gmlp_norm", "gmlp_ws", "gmlp_bs", "dn_conv", "dn_a_log", "dn_dt_bias", "dn_norm", "w_branch", "w_out",
        "ffn_w_gate", "ffn_w_up", "ffn_w_down", "moe_router", "moe_w_gate", "moe_w_up", "moe_w_down"]
_OUTS = [(1, CTX, D), (1, LAT, D), (1, DEPTH, CTX, KVH, HD), (1, DEPTH, CTX, KVH, HD), (1, DEPTH, 2, DNH, DK, DK)]


def kernel(**inputs):
    import concourse.bacc as _bacc
    from concourse.bass_utils import run_bass_kernel_spmd as _run

    nc = _bacc.Bacc("TRN2", target_bir_lowering=False, num_devices=1)
    arrays = {"constants": constants()}
    args = [nc.dram_tensor("constants", (P, NCST), F32, kind="ExternalInput").ap()]
    for name in _INS:
        a = np.ascontiguousarray(inputs[name])
        arrays[f"in_{name}"] = a
        args.append(nc.dram_tensor(f"in_{name}", a.shape, mybir.dt.from_np(a.dtype), kind="ExternalInput").ap())
    args.append(nc.dram_tensor("xpark", (P, KT * TOK), F32, kind="Internal").ap())
    for i, shape in enumerate(_OUTS):
        args.append(nc.dram_tensor(f"out_{i}", shape, F32, kind="ExternalOutput").ap())
    build(nc, *args)
    r = _run(nc, [arrays], core_ids=[0])
    return tuple(r.results[0][f"out_{i}"] for i in range(len(_OUTS)))
```

```python
import math
from contextlib import ExitStack

import numpy as np

import concourse.bass as bass
from concourse import mybir

F32 = mybir.dt.float32
F32R = mybir.dt.float32r
BF16 = mybir.dt.bfloat16
U32 = mybir.dt.uint32
I32 = mybir.dt.int32
ALU = mybir.AluOpType
ACT = mybir.ActivationFunctionType
AX = mybir.AxisListType

P = 128
D = 1024
KT = D // P
DEPTH = 2
CTX, LAT = 128, 256
TOK = CTX + LAT
NT = TOK // P
HEADS, KVH, HD = 8, 4, 64
ROPE_THETA, GRID_W = 10000.0, 64
DNH, DK = 4, 128
CHUNK = 64
CONV_K = 5
FFN = 2816
NE, ED = 8, 1408
EPS = 1e-6
TOP_K, SLOTS = 2, P
NI = 1 + (TOP_K * TOK + (NE - 1) * (SLOTS - 1)) // SLOTS + 1
MIN_ITEMS = TOP_K * TOK // SLOTS
FG, FE = FFN // P, ED // P

C_QA, C_KA, C_U, C_V, C_DN, C_BA, C_Z, C_GATE = 0, 512, 1024, 1536, 2048, 3584, 3600, 4112

NSLOT = 4
SLOT = 4096
CROW = CTX + LAT + 4 * (CONV_K // 2)
COUT = CROW - (CONV_K - 1)
LAT0 = CTX + 4
SEG = ((0, 0, CTX), (1, CTX, TOK))

T_QKV, T_BA, T_A, T_UV, T_G, T_Z = 0, 12, 15, 21, 27, 51
N_PROJ = 54
LEVELS = (1, 2, 4, 8, 16, 32)

ADA_FIRST = (0, 1, 2, 3)
ADA_AT = (dict(n1=(), at=(4, 5, 6), z=(7, 8), oc=(9,), n3=(10, 11), h3=(12, 13), n4=(14, 15)),
          dict(n1=(16,), at=(17, 18, 19), z=(20, 21), oc=(22,), n3=(23,), h3=(), n4=()))
ADA_U = 12
ADA_DONE = {3: (1, 0), 5: (2, 1), 9: (4, 2), 11: (5, 3)}

PER = dict(proj_mm=N_PROJ, proj_ev=N_PROJ, sq=4, stat=4, root=4, rinv=4, xn=2, h_a=8, h_v=8, x_new=2,
           pads=1, conv=12, silu=3, dsq=1, dst=8, droot=8, qkn=1, kvt_mm=6, kvt_ev=6,
           ba_v=1, ba_l=1, g_ok=1, gc_mm=1, gc_v=1, gc_e=1, beg=1,
           a_sq=1, a_ss=1, a_rt=1, a_ok=1, tr_mm=6, tr_ev=6, v_ss=1, v_rt=1, v_ok=1,
           at_s=24, at_m=24, at_e=24, at_p=24, at_t=24, at_pt=24, at_pv=24, at_o=3,
           b_mm=3, b_v=3, b_t=3, b_ev=3,
           d_in=6, d_d0=6, d_e=6, d_pool=6, d_m=6, d_mt=6, d_mtc=6, d_t1=6, d_ct=30, d_w=30, d_we=30,
           d_du=30, d_up=30, d_uw=6, d_uwe=6, d_kd=6, s_ws=12, s_vn=12, s_o=12, s_st=12, s_or=6,
           oc_sq=1, oc_ss=1, oc_rt=1, oc_v=1, oc_mm=3, oc_ev=3, gsig=1,
           br_mm=8, br_ev=8, wo_mm=8, wo_ev=8)


TILE = ((0, 0), (1, 2), (2, 1))
TCOL = (0, LAT0, LAT0 + P)


def constants():
    i, j = np.arange(P)[:, None], np.arange(P)[None, :]
    same = (i // CHUNK) == (j // CHUNK)
    parts = [np.eye(P), (i >= j) & same, (i <= j) & same, same, np.ones((P, P))]
    quarter = HD // 4
    freqs = (1.0 / (np.float32(ROPE_THETA) ** (np.arange(quarter, dtype=np.float32) / quarter))).astype(np.float32)
    rope = np.zeros((P, 2, 2, 2, quarter), np.float32)
    for t in range(LAT // P):
        pos = t * P + np.arange(P)
        for a, x in enumerate((pos // GRID_W, pos % GRID_W)):
            ang = x[:, None].astype(np.float32) * freqs[None]
            rope[:, t, 0, a], rope[:, t, 1, a] = np.cos(ang), np.sin(ang)
    parts.append(rope.reshape(P, -1))
    parts.append(np.stack([np.arange(P) < CHUNK, np.arange(P) >= CHUNK], 1))
    parts.append(np.tile([EPS, DK * EPS, 1.0], (P, 1)))
    parts.append(np.tile(np.arange(NE), (P, 1)))
    for s in LEVELS:
        low = (i // (2 * s) == j // (2 * s)) & (i % (2 * s) >= s) & (j % (2 * s) < s)
        parts += [-1.0 * low, -1.0 * low.T]
    e = np.arange(NE)
    parts += [i <= j, np.tile(np.arange(P) + 1.0, (P, 1)), np.tile((e[None] < e[:, None]).reshape(1, -1), (P, 1)),
              np.tile(np.arange(NI), (P, 1))]
    return np.ascontiguousarray(np.concatenate([np.asarray(x, np.float32) for x in parts], 1))


NRES = 5 * P + 128 + 2 + 3 + NE
NMASK = 2 * len(LEVELS) * P
NROUTE = 2 * P + NE * NE + NI
NCST = NRES + NMASK + NROUTE


def build(nc, cst_d, x_prompt, x_sample, cache_k, cache_v, state_in, c, c_ctx, ada_w, ada_b, norms, w_in, qk_norm,
          gmlp_norm, gmlp_ws, gmlp_bs, dn_conv, dn_a_log, dn_dt_bias, dn_norm, w_branch, w_out, ffn_g, ffn_u, ffn_d,
          router, moe_g, moe_u, moe_d, xpark, y_prompt, y_sample, new_k, new_v, new_s):
    ctx = ExitStack()
    with ctx:
        def sb(name, n, dt=F32):
            return ctx.enter_context(nc.sbuf_tensor(name, [P, n], dt))

        def sem(name):
            return ctx.enter_context(nc.semaphore(name))

        place = {}

        def sb_at(name, n):
            t = sb(name, n)
            place[name] = nc.sbuf_base - 4 * n
            return t

        def upper(name, where, first, n):
            return nc.alloc_sbuf_tensor_at(name, [P, n], F32R, offset=place[where] + 4 * first)

        ring = sb_at("ring", NSLOT * SLOT)
        H = sb_at("hT", KT * TOK)
        GT = sb_at("gates", 24 * TOK)
        CV = sb_at("conv", 12 * COUT)
        KK_ = sb("ktok", NT * 512)
        OT = sb_at("oT", 12 * TOK)
        RX = sb_at("work", 10240)
        cst = sb("cst", NRES)
        lmask = sb("lmask", 2 * len(LEVELS) * P, BF16)
        rows = sb("rowsT", 64 + 96 + 24 + 120)
        modv = sb("modv", DEPTH * 96)
        sm = sb("small", 768)

        def v3(ap, a):
            return ap.rearrange("p (a b) -> p a b", a=a)

        hT, xT = v3(H[:, :], KT), v3(RX[:, 0:KT * TOK], KT)
        yT = v3(RX[:, 3072:6144], KT)
        sqT, sqP = v3(GT[:, 0:3072], KT), v3(CV[:, 0:3072], KT)
        gates = v3(GT[:, :], 24)
        pre = v3(GT[:, 0:12 * CROW], 12)
        dsq = v3(GT[:, 12 * CROW:12 * CROW + 8 * COUT], 8)
        cv = v3(CV[:, :], 12)
        vtok = CV[:, 8 * COUT:8 * COUT + 1536].rearrange("p (t h e) -> p t h e", t=NT, h=DNH)
        ktok = KK_[:, :].rearrange("p (t h e) -> p t h e", t=NT, h=DNH)
        oT = OT[:, :].rearrange("p (b k n) -> p b k n", b=3, k=4)
        ident, inclL, inclU, same, ones = (cst[:, i * P:(i + 1) * P] for i in range(5))
        rope = cst[:, 640:768].rearrange("p (t f a q) -> p t f a q", t=2, f=2, a=2)
        chsel = cst[:, 768:770]
        eps1, eps128, one1 = (cst[:, 770 + i:771 + i] for i in range(3))
        iota8 = cst[:, 773:773 + NE]
        lm = lmask[:, :].rearrange("p (s f n) -> p s f n", s=len(LEVELS), f=2)
        nrmT = rows[:, 0:64].rearrange("p (l a k) -> p l a k", l=DEPTH, a=4)
        adab = rows[:, 64:160].rearrange("p (l m) -> p l m", l=DEPTH)
        scT = rows[:, 160:176].rearrange("p (s k) -> p s k", s=2)
        bsT = rows[:, 176:184].rearrange("p (l g) -> p l g", l=DEPTH)
        cwT = rows[:, 184:304].rearrange("p (l j n) -> p l j n", l=DEPTH, j=CONV_K)
        mod = modv[:, :].rearrange("p (l a k s) -> p l a k s", l=DEPTH, a=6, k=KT)

        qkv = v3(RX[:, 0:3072], NT)
        qTt = v3(RX[:, 3072:4608], 4)
        kTt = v3(RX[:, 4608:5632], 2)
        Pb = v3(RX[:, 5632:6400], 2)
        PTb = v3(RX[:, 6400:7168], 2)
        uB, vB = v3(RX[:, 7168:8704], NT), v3(RX[:, 8704:10240], NT)
        wsT = OT[:, 3072:3584]
        ggain = OT[:, 3584:4096]
        qkgain = OT[:, 4096:4224]
        asq = v3(OT[:, 0:2304], NT)
        kcache, vcache = GT[:, 8192:8448], GT[:, 8448:8704]
        wsraw = v3(GT[:, 8704:9216], 4)
        gsc = GT[:, 7168:7680]
        rt = [GT[:, 384 * i:384 * (i + 1)].rearrange("p (h a q) -> p h a q", h=12, a=2) for i in range(4)]

        def dn(d, i):
            return v3(RX[:, (9 * d + i) * 512:(9 * d + i + 1) * 512], DNH)
        B_M, B_QK, B_QEG, B_MT, B_T, B_U, B_W, B_VU, B_KW = range(9)
        B_CT, B_KD, B_VN = B_M, B_MT, B_T
        state = RX[:, 9216:10240].rearrange("p (d h e) -> p d h e", d=2, h=DNH)
        osum = v3(OT[:, 3072:4608], NT)
        zs = v3(CV[:, 0:1536], NT)
        merged = v3(CV[:, 1536:4608], KT)
        btmp = [RX[:, 6144 + 384 * i:6528 + 384 * i] for i in range(3)]
        sgb = v3(RX[:, 6144:6912], 2)
        ringS = upper("ring_split", "ring", 0, NSLOT * SLOT)
        hT_hi = v3(upper("hT_hi", "work", 7168, KT * TOK)[:, :], KT)
        hT_lo = v3(upper("hT_lo", "hT", 0, KT * TOK)[:, :], KT)
        hid_hi = v3(upper("hid_hi", "gates", 0, FG * TOK)[:, :], FG)
        hid_lo = v3(upper("hid_lo", "conv", 0, FG * TOK)[:, :], FG)
        hidf = v3(GT[:, FG * TOK:FG * TOK + 2 * TOK], 2)
        ada_buf = RX[:, 6144:7168]

        m_off = [0, 0]

        def gt(n):
            m_off[0] += n
            assert m_off[0] <= 9216
            return GT[:, m_off[0] - n:m_off[0]]

        def gt_split(name, n):
            m_off[0] += n
            assert m_off[0] <= 9216
            return upper(name, "gates", m_off[0] - n, n)[:, :]

        def kk(n):
            m_off[1] += n
            assert m_off[1] <= NT * 512
            return KK_[:, m_off[1] - n:m_off[1]]
        xg_hi, xg_lo = (v3(gt_split(f"xg_{p}", KT * SLOTS), KT) for p in ("hi", "lo"))
        ehid_hi, ehid_lo = (v3(gt_split(f"ehid_{p}", FE * SLOTS), FE) for p in ("hi", "lo"))
        ehid = v3(gt(2 * 256), 2)
        ytok, scatT = gt(D), gt(TOK)
        esel, wsel = v3(gt(NT * SLOTS), NT), v3(gt(NT * SLOTS), NT)
        esg = v3(gt(2 * 256), 2)
        route = gt(NROUTE)
        it_rank, it_comb = v3(gt(NI * NT), NI), v3(gt(NI * NT), NI)
        tri, slot1 = route[:, 0:P], route[:, P:2 * P]
        before, item = v3(route[:, 2 * P:2 * P + NE * NE], NE), route[:, 2 * P + NE * NE:NROUTE]
        sel2 = tuple(kk(NT * NE).rearrange("p (t e) -> p t e", t=NT) for _ in range(2))
        rank = v3(kk(NT * NE), NT)
        cnt, nit, e_lo, e_hi = (kk(NE) for _ in range(4))
        tri8 = v3(kk(NE * NE), NE)
        own, own2 = v3(kk(NI * NE), NI), v3(kk(NI * NE), NI)
        it_e, it_lo = kk(NI), kk(NI)
        oprod = kk(NI * NT * NE).rearrange("p (i t e) -> p i t e", i=NI, t=NT)
        w_upper = upper("w_upper_a", "work", 6144, SLOT), upper("w_upper_b", "conv", 0, SLOT)
        otS = upper("oT_split", "oT", 0, SLOT)
        h2tok = v3(H[:, :], NT)

        def ada_rows(n, buf):
            return buf[0:2, 512 * (n % 2):512 * (n % 2 + 1)]

        off = [0]

        def small(n):
            off[0] += n
            assert off[0] <= 768
            return sm[:, off[0] - n:off[0]]
        ba = v3(small(48), NT)
        beta, gg, t1, t2, beg, edec, eg = (v3(small(24), NT) for _ in range(7))
        gcs = v3(small(24), NT)
        table = small(NI + 2).bitcast(I32)
        gm = small(48).rearrange("p (t c n) -> p t c n", t=NT, c=2)
        egl = small(48).rearrange("p (t c n) -> p t c n", t=NT, c=2)
        expa, dtb = small(8), small(8)
        ass, amx, anm, ars = small(36), small(24), small(24), small(24)
        vss, oss = small(3), small(12)
        m8, i8, i8f = small(24), small(24), small(24)
        oh0, oh1, comb = (v3(small(24), NT) for _ in range(3))
        baw = OT[:, 4224:4352]
        dngain = sb("dngain", DK)
        rs = sb("rstd", TOK)
        rtw = sb("routerw", KT * NE)

        B = [ctx.enter_context(nc.psum_tensor(f"bank{i}", [P, 512], F32)) for i in range(8)]

        s_slot = [sem(f"slot{i}_full") for i in range(NSLOT)]
        S = {n: sem(n) for n in PER}
        (cst_in, mask_in, rows_in, x_in, bf_ok, rt_mm, rt_ev, sc_ok, xt_mm, xt_ev, ada_mm, ada_ev, ada_t, ada_cp, mod_ok, lw_in, cache_in, dn_in, parked,
         unparked, kv_out, st_out, st_in, y_out, gu_g, gu_u, gu_s, gu_f, gu_hi, gu_h, hs_a, hs_ok, w_hi, w_lo, down_mm, down_ev, rl_mm, rl_c, rl_e, rl_ok, rk_mm, tbl_ok, ht_mm, ht_ev, route_in,
         ots_full, mw_hi, mv_lo, mp_lo, th_mm, hh_ok, hl_ok, ga_lo, mg_mm, msg_ok, mh_ok, wsel_ok, sel_ok, ga_mm, ga_ev, wt_mm, wt_ev, dn_mm, yt_ok, sc_mm, sc_ad,
         xo_mm, xo_ev, sp_turn, act_step, dve_step, pool_step) = (sem(n) for n in (
            "cst_in mask_in rows_in x_in bf_ok rt_mm rt_ev sc_ok xt_mm xt_ev ada_mm ada_ev ada_t ada_cp mod_ok lw_in cache_in dn_in parked "
            "unparked kv_out st_out st_in y_out gu_g gu_u gu_s gu_f gu_hi gu_h hs_a hs_ok w_hi w_lo down_mm down_ev rl_mm rl_c rl_e rl_ok rk_mm tbl_ok ht_mm ht_ev route_in "
            "ots_full mw_hi mv_lo mp_lo th_mm hh_ok hl_ok ga_lo mg_mm msg_ok mh_ok wsel_ok sel_ok ga_mm ga_ev wt_mm wt_ev dn_mm yt_ok sc_mm sc_ad "
            "xo_mm xo_ev sp_turn act_step dve_step pool_step").split())

        H_BANK = (0, 1, 3, 4, 5, 7)

        def wait(eng, name, layer, n):
            if PER[name] * layer + n > 0:
                eng.wait_ge(S[name], PER[name] * layer + n)

        def linker(eng, step):
            n = [0]

            def link(ins):
                n[0] += 1
                ins.then_inc(step, 1)
                eng.wait_ge(step, n[0])
            return link

        WIN = [C_DN, C_DN + 512, C_DN + 1024, C_QA, C_KA, C_U, C_V] + [C_GATE + 512 * i for i in range(6)] + [C_Z]
        WIN_END = [4, 8, 12, T_A + 3, T_A + 6, T_UV + 3, T_UV + 6] + [T_G + 4 * (i + 1) for i in range(6)] + [T_Z + 3]
        FF_GU, FF_DN = 11, 8
        order = [("ada", n) for n in ADA_FIRST]
        for layer, at in enumerate(ADA_AT):
            for ada, first, last in (("n1", 0, 7), ("at", 7, 13), ("z", 13, 14), ("oc", 14, 20), ("n3", 0, 0), ("h3", 0, 0)):
                order += [("ada", n) for n in at[ada]] + [("w", layer, i) for i in range(first, last)]
            if layer == 0:
                order += [(kind, i) for i in range(FF_GU + FF_DN) for kind in ("ff", "ff_hi")]
            order += [("ada", n) for n in at["n4"]]
        U_MOE = len(order)
        M_GU, M_DN, M_SLOT = 6, 4, 5
        WIN = [C_DN, C_DN + 512, C_DN + 1024, C_QA, C_KA, C_U, C_V] + [C_GATE + 512 * i for i in range(6)] + [C_Z]
        WIN_END = [4, 8, 12, T_A + 3, T_A + 6, T_UV + 3, T_UV + 6] + [T_G + 4 * (i + 1) for i in range(6)] + [T_Z + 3]

        def at_ring(*key):
            return order.index(key)

        def slot(unit):
            return unit % NSLOT

        def wslot(unit, k, n):
            s = slot(unit)
            return ring[:, s * SLOT:s * SLOT + k * n].rearrange("p (k n) -> p k n", k=k)

        def dmas(unit):
            if unit < U_MOE and order[unit][0] == "ff_hi":
                return 0
            return 2 if unit < U_MOE and order[unit][0] == "ff" and order[unit][1] < FF_GU else 1

        def full(unit):
            return 16 * sum(dmas(u) for u in range(unit % NSLOT, unit + 1, NSLOT))

        def freed(eng, unit):
            if unit < NSLOT:
                return
            kind, *at = order[unit - NSLOT]
            if kind == "ada":
                eng.wait_ge(ada_mm, at[0] + 1)
            elif kind == "w":
                layer, i = at
                if i < 14:
                    wait(eng, "proj_mm", layer, WIN_END[i])
                elif i < 18:
                    wait(eng, "br_mm", layer, 2 * (i - 13))
                else:
                    wait(eng, "wo_mm", layer, 4 * (i - 17))
            elif at[0] < FF_GU:
                eng.wait_ge(gu_u, 2 * (at[0] + 1))
            else:
                eng.wait_ge(down_mm, at[0] - FF_GU + 1)

        FF_LOOP = 4

        def ff_arrived(eng, j, it):
            u = at_ring("ff", j)
            eng.wait_ge(s_slot[slot(u)], full(u) + ((full(u + 2 * FF_LOOP) - full(u)) * it if it is not None else 0))

        def ff_parts(j):
            u = at_ring("ff", j)
            r0, h0 = slot(u) * SLOT, slot(u + 1) * SLOT
            n, parts = (KT * 256, 2) if j < FF_GU else (FG * P, 1)
            return [(ring[:, r0 + g * n:r0 + (g + 1) * n], ringS[:, h0 + g * n:h0 + (g + 1) * n],
                     ringS[:, r0 + g * n:r0 + (g + 1) * n]) for g in range(parts)]

        def ff_part(j, it, g):
            return 2 * FF_LOOP * it + 2 * j + g + 1 if it is not None else 2 * min(j, FF_GU) + max(j - FF_GU, 0) + g + 1

        def m_place(j, split=False):
            if j % M_SLOT == M_SLOT - 1:
                return (otS if split else OT)[:, 0:SLOT]
            k = slot(U_MOE + j % M_SLOT)
            return (ringS if split else ring)[:, k * SLOT:(k + 1) * SLOT]

        M_HALF = 2
        G_IT, D_IT = M_HALF * M_GU, M_HALF * M_DN

        def m_shape(j):
            return (2, KT, 256 if j < M_GU - 1 else P) if j < M_GU else (1, FE, 256)

        def m_tiles(j, h):
            k = m_shape(j)[1]
            return range(0, (k + 1) // 2) if h == 0 else range((k + 1) // 2, k)

        def m_view(ap, j):
            g, k, n = m_shape(j)
            return ap[:, 0:g * k * n].rearrange("p (g k n) -> p g k n", g=g, k=k)

        def m_half(ap, j, h):
            ks = m_tiles(j, h)
            return m_view(ap, j)[:, :, ks.start:ks.stop].rearrange("p g k n -> p g (k n)")

        def m_used(eng, j, h, i):
            if j < M_GU:
                eng.wait_ge(mg_mm, G_IT * i + M_HALF * j + h + 1)
            else:
                eng.wait_ge(dn_mm, D_IT * i + M_HALF * (j - M_GU) + h + 1)

        def m_upper(act, j, h, i):
            if h == 0:
                act.wait_ge(m_sem(j), m_full(j, i))
            nc.scalar.activation(m_half(w_upper[j % 2], j, h), m_half(m_place(j), j, h), ACT.Copy).then_inc(mw_hi, 1)

        def m_lower(eng, op, j, h, i, done):
            eng.wait_ge(mw_hi, M_HALF * (M_GU + M_DN) * i + M_HALF * j + h + 1)
            op.tensor_tensor(m_half(m_place(j, True), j, h), m_half(m_place(j), j, h), m_half(w_upper[j % 2], j, h).bitcast(F32),
                             ALU.subtract).then_inc(done, 1)

        V_IT, POOL_U = M_HALF * 8, (M_GU, M_GU + 1)

        def m_split(pe, j, h, i):
            if j in POOL_U:
                pe.wait_ge(mp_lo, M_HALF * (len(POOL_U) * i + (j - M_GU)) + h + 1)
            else:
                pe.wait_ge(mv_lo, V_IT * i + M_HALF * (j if j < M_GU else j - len(POOL_U)) + h + 1)

        def m_dmas(j):
            return 2 if j < M_GU else 1

        def m_sem(j):
            return ots_full if j % M_SLOT == M_SLOT - 1 else s_slot[slot(U_MOE + j % M_SLOT)]

        def m_full(j, i):
            s = j % M_SLOT
            at_start = 0 if s == M_SLOT - 1 else full(U_MOE + s - NSLOT)
            here = m_dmas(s) + (m_dmas(s + M_SLOT) if j >= M_SLOT else 0)
            return 16 * (m_dmas(s) + m_dmas(s + M_SLOT)) * i + at_start + 16 * here

        block = ctx.enter_context(nc.Block())

        @block.sync
        def _(sp):
            def load(unit, dst, src):
                sp.dma_start(dst, src).then_inc(s_slot[slot(unit)], 16)

            sp.dma_start(cst[:, :], cst_d[:, 0:NRES]).then_inc(cst_in, 16)
            xtok = v3(RX[:, 3072:6144], NT)
            sp.dma_start(xtok[:, 0], x_prompt[0]).then_inc(x_in, 16)
            sp.dma_start(xtok[:, 1:3], x_sample[0].rearrange("(t p) n -> p t n", p=P)).then_inc(x_in, 16)
            for u, (kind, *at) in enumerate(order):
                if u == 1:
                    sp.wait_ge(rows_in, 96)
                if kind == "w" and at[1] == 4:
                    wait(sp, "xn", at[0], 1)
                    wait(sp, "sq", at[0], 1)
                    sp.dma_start(xpark.rearrange("p (k n) -> p k n", k=KT), xT).then_inc(parked, 16)
                if kind != "ff_hi":
                    freed(sp, u)
                if kind == "ada":
                    layer, i = divmod(at[0], ADA_U)
                    load(u, wslot(u, KT, 512), ada_w[layer, :, 512 * i:512 * (i + 1)].rearrange("(k p) n -> p k n", p=P))
                elif kind == "w":
                    layer, i = at
                    if i < 14:
                        load(u, wslot(u, KT, 512), w_in[layer, :, WIN[i]:WIN[i] + 512].rearrange("(k p) n -> p k n", p=P))
                    elif i < 18:
                        n0 = 256 * (i - 14)
                        src = w_branch[layer, :, :, n0:n0 + 256].rearrange("b (k p) n -> p (b k) n", p=P)
                        load(u, wslot(u, 12, 256), src)
                    else:
                        n0 = 512 * (i - 18)
                        load(u, wslot(u, KT, 512), w_out[layer, :, n0:n0 + 512].rearrange("(k p) n -> p k n", p=P))
                elif kind == "ff_hi":
                    continue
                elif at[0] < FF_GU:
                    d = ring[:, slot(u) * SLOT:(slot(u) + 1) * SLOT].rearrange("p (g k n) -> p g k n", g=2, k=KT)
                    n0 = 256 * at[0]
                    load(u, d[:, 0], ffn_g[0, :, n0:n0 + 256].rearrange("(k p) n -> p k n", p=P))
                    load(u, d[:, 1], ffn_u[0, :, n0:n0 + 256].rearrange("(k p) n -> p k n", p=P))
                else:
                    n0 = P * (at[0] - FF_GU)
                    load(u, wslot(u, FG, P), ffn_d[0, :, n0:n0 + P].rearrange("(k p) n -> p k n", p=P))

            def moe_load(e, j):
                ex = slice(0, 1) if e is None else bass.ds(e, 1)
                if j < M_GU:
                    n = 256 if j < M_GU - 1 else P
                    d = m_place(j)[:, 0:16 * n].rearrange("p (g k n) -> p g k n", g=2, k=KT)
                    for g, w in enumerate((moe_g, moe_u)):
                        src = w[0, ex, :, 256 * j:256 * j + n].rearrange("a (k p) n -> p (a k) n", p=P)
                        sp.dma_start(d[:, g], src).then_inc(m_sem(j), 16)
                else:
                    n0 = 256 * (j - M_GU)
                    src = moe_d[0, ex, :, n0:n0 + 256].rearrange("a (k p) n -> p (a k) n", p=P)
                    sp.dma_start(m_place(j)[:, 0:FE * 256].rearrange("p (k n) -> p k n", k=FE), src).then_inc(m_sem(j), 16)

            for j in range(4):
                freed(sp, U_MOE + j)
                moe_load(None, j)
            wait(sp, "br_mm", 1, 8)
            moe_load(None, 4)
            for j in range(M_SLOT, M_GU + M_DN):
                m_used(sp, j - M_SLOT, 1, 0)
                moe_load(None, j)
            sp.wait_ge(tbl_ok, 1)
            n_items = sp.value_load(table[0:1, NI:NI + 1], min_val=MIN_ITEMS, max_val=NI - 1)
            with sp.Fori(1, n_items) as i:
                e = sp.value_load(table[0:1, bass.ds(i, 1)], min_val=0, max_val=NE - 1)
                for j in range(M_GU + M_DN):
                    if j < M_SLOT:
                        m_used(sp, j + M_SLOT, 1, i - 1)
                    else:
                        m_used(sp, j - M_SLOT, 1, i)
                    sp.sem_inc(sp_turn, 1)
                    moe_load(e, j)
            for t in range(NT):
                sp.wait_ge(xo_ev, 2 * t + 2)
                dst = y_prompt[0] if t == 0 else y_sample[0, (t - 1) * P:t * P, :]
                sp.dma_start(dst, v3(GT[:, 0:3072], NT)[:, t]).then_inc(y_out, 16)
            sp.wait_ge(y_out, 16 * NT)

        @block.gpsimd
        def _(pool):
            link = linker(pool, pool_step)

            def bc(ap, n):
                return ap.unsqueeze(2).to_broadcast([P, ap.shape[1], n])

            st = v3(RX[:, 8192:8704], 4)
            link(nc.gpsimd.memset(st, 0.0))
            pool.dma_start(st[0:8, 2], c_ctx.rearrange("(k p) -> k p", p=P)).then_inc(rows_in, 16)
            pool.dma_start(st[8:16, 2], c.rearrange("s (k p) -> (s k) p", p=P)).then_inc(rows_in, 16)
            pool.dma_start(st[0:64, 0], norms.rearrange("l a (k p) -> (l a k) p", p=P)).then_inc(rows_in, 16)
            pool.dma_start(st[0:96, 1], ada_b.rearrange("l (m p) -> (l m) p", p=P)).then_inc(rows_in, 16)
            pool.dma_start(st[16:24, 2], gmlp_bs.rearrange("l g p -> (l g) p")).then_inc(rows_in, 16)
            pool.dma_start(st[0:120, 3], dn_conv.rearrange("l j (n p) -> (l j n) p", p=P)).then_inc(rows_in, 16)
            pool.dma_start(RX[:, 6144:6144 + NMASK], cst_d[:, NRES:NRES + NMASK]).then_inc(mask_in, 16)

            for layer in range(DEPTH):
                wait(pool, "x_new", layer, 0)
                for dst, src in ((v3(baw, KT), w_in[layer, :, C_BA:C_BA + 16].rearrange("(k p) n -> p k n", p=P)),
                                 (ggain, gmlp_norm[layer].partition_broadcast(P)),
                                 (qkgain, qk_norm[layer].rearrange("a d -> (a d)").partition_broadcast(P)),
                                 (expa, dn_a_log[layer].rearrange("a d -> (a d)").partition_broadcast(P)),
                                 (dtb, dn_dt_bias[layer].rearrange("a d -> (a d)").partition_broadcast(P)),
                                 (dngain[:, :], dn_norm[layer].partition_broadcast(P))):
                    pool.dma_start(dst, src).then_inc(lw_in, 16)
                if layer == 0:
                    pool.dma_start(v3(rtw[:, :], KT), router[0].rearrange("(k p) n -> p k n", p=P)).then_inc(lw_in, 16)
                pool.dma_start(wsraw, gmlp_ws[layer].rearrange("g q r -> q g r")).then_inc(cache_in, 16)
                pool.dma_start(kcache, cache_k[0, layer].rearrange("t h d -> t (h d)")).then_inc(cache_in, 16)
                pool.dma_start(vcache, cache_v[0, layer].rearrange("t h d -> t (h d)")).then_inc(cache_in, 16)
                wait(pool, "a_ok", layer, 1)
                pool.dma_start(new_k[0, layer].rearrange("t h d -> t (h d)"), qkv[:, 0, 512:768]).then_inc(kv_out, 16)
                pool.dma_start(new_v[0, layer].rearrange("t h d -> t (h d)"), qkv[:, 0, 768:1024]).then_inc(kv_out, 16)
                pool.wait_ge(kv_out, 32 * (layer + 1))
                wait(pool, "b_ev", layer, 3)
                wait(pool, "at_pv", layer, 24)
                wait(pool, "at_pt", layer, 24)
                link(nc.gpsimd.memset(state, 0.0))
                wait(pool, "kvt_ev", layer, 6)
                wait(pool, "beg", layer, 1)
                for pair in range(3):
                    for d in range(2):
                        g = 2 * pair + d
                        t = TILE[pair][d]
                        h4 = slice(4 * d, 4 * d + 4)
                        if pair:
                            wait(pool, "s_or", layer, g - 1)
                        nc.gpsimd.tensor_tensor(dn(d, B_VU), vtok[:, t], bc(beta[:, t, h4], DK), ALU.mult)
                        link(nc.gpsimd.tensor_tensor(dn(d, B_KW), ktok[:, t], bc(beg[:, t, h4], DK), ALU.mult))
                        wait(pool, "d_e", layer, g + 1)
                        nc.gpsimd.tensor_tensor(dn(d, B_M), dn(d, B_M), bc(beta[:, t, h4], P), ALU.mult)
                        incl = inclU if d == 0 else inclL
                        nc.gpsimd.tensor_tensor(dn(d, B_QK), dn(d, B_QK), incl.unsqueeze(1).to_broadcast([P, DNH, P]),
                                                ALU.mult).then_inc(S["d_pool"], 1)
                        nc.gpsimd.tensor_tensor(dn(d, B_QEG), dn(d, B_QEG), cv[:, 0:4, TCOL[t]:TCOL[t] + P], ALU.mult)
                    for s in range(1, len(LEVELS)):
                        for d in range(2):
                            g = 2 * pair + d
                            if s == 1:
                                wait(pool, "d_mtc", layer, g + 1)
                                wait(pool, "d_t1", layer, g + 1)
                            else:
                                wait(pool, "d_w", layer, 10 * pair + 2 * (s - 2) + d + 1)
                            nc.gpsimd.tensor_tensor(dn(d, B_CT), dn(d, B_MT),
                                                    lm[:, s, 1 - d].unsqueeze(1).to_broadcast([P, DNH, P]),
                                                    ALU.mult).then_inc(S["d_ct"], 1)
                    for d in range(2):
                        t = TILE[pair][d]
                        wait(pool, "d_ct", layer, 10 * pair + 8 + d + 1)
                        nc.gpsimd.tensor_tensor(dn(d, B_KD), ktok[:, t], bc(edec[:, t, 4 * d:4 * d + 4], DK),
                                                ALU.mult).then_inc(S["d_kd"], 1)
                    if pair == 0:
                        wait(pool, "s_st", layer, 4)
                        for d in range(2):
                            pool.dma_start(new_s[0, layer, d].rearrange("h k e -> k h e"), state[:, d]).then_inc(st_out, 16)
                        pool.wait_ge(st_out, 32 * (layer + 1))
                        for d in range(2):
                            pool.dma_start(state[:, d], state_in[0, layer, d].rearrange("h k e -> k h e")).then_inc(st_in, 16)
                wait(pool, "s_or", layer, 6)
                wait(pool, "s_st", layer, 12)
                wait(pool, "oc_mm", layer, 3)
                pool.dma_start(xT, xpark.rearrange("p (k n) -> p k n", k=KT)).then_inc(unparked, 16)
            wait(pool, "br_ev", 1, 8)
            pool.dma_start(route, cst_d[:, NRES + NMASK:NCST]).then_inc(route_in, 16)
            pool.wait_ge(tbl_ok, 1)
            n_items = pool.value_load(table[0:1, NI:NI + 1], min_val=MIN_ITEMS, max_val=NI - 1)
            with pool.Fori(0, n_items) as i:
                for j in POOL_U:
                    for h in range(M_HALF):
                        m_lower(pool, nc.gpsimd, j, h, i, mp_lo)
            pool.wait_ge(unparked, 16 * DEPTH)
            pool.wait_ge(kv_out, 32 * DEPTH)
            pool.wait_ge(st_out, 32 * DEPTH)

        @block.tensor
        def _(pe):
            mm = nc.tensor.matmul

            def tr(out, in_):
                return nc.tensor.transpose(out, in_, ident)

            def arrived(unit):
                pe.wait_ge(s_slot[slot(unit)], full(unit))

            pe.wait_ge(cst_in, 16)
            pe.wait_ge(rows_in, 96)
            st = v3(RX[:, 8192:8704], 4)
            for i in range(4):
                tr(B[0][:, i * P:(i + 1) * P], st[:, i]).then_inc(rt_mm, 1)
            pe.wait_ge(x_in, 32)
            xtok = v3(RX[:, 3072:6144], NT)
            for t in range(NT):
                for half in range(2):
                    for k in range(4):
                        last = tr(B[2 + 2 * t + half][:, k * P:(k + 1) * P], xtok[:, t, (4 * half + k) * P:(4 * half + k + 1) * P])
                    last.then_inc(xt_mm, 1)

            def ada_row(n, k, b):
                u = at_ring("ada", n)
                if k == 0:
                    arrived(u)
                    if n >= 2:
                        pe.wait_ge(ada_cp, n - 1)
                last = mm(B[b + n % 2][0:2, :], scT[:, :, k], wslot(u, KT, 512)[:, k], start=k == 0, stop=k == KT - 1)
                if k == KT - 1:
                    last.then_inc(ada_mm, 1)

            def ada_turn(n, b, buf):
                pe.wait_ge(ada_ev, n + 1)
                for m in range(4):
                    last = nc.tensor.transpose(B[b + n % 2][:, 2 * m:2 * m + 2], ada_rows(n, buf)[:, m * P:(m + 1) * P], ident[0:2, 0:2])
                last.then_inc(ada_t, 1)

            def ada_units(units, b, buf=KK_):
                for j, n in enumerate(units):
                    for k in range(KT):
                        ada_row(n, k, b)
                    if j:
                        ada_turn(n - 1, b, buf)
                if units:
                    ada_turn(units[-1], b, buf)

            def sum_squares(layer, q, sq):
                wait(pe, "sq", layer, q)
                for k in range(KT):
                    last = mm(B[2][:, 0:TOK], ones, sq[:, k], start=k == 0, stop=k == KT - 1)
                last.then_inc(S["stat"], 1)

            def bank_free(layer, n):
                wait(pe, "proj_ev", layer, n - 1)

            def feature_tile(layer, n, unit, m):
                bank_free(layer, n)
                w = wslot(unit, KT, 512)
                for k in range(KT):
                    last = mm(B[n % 2][:, 0:TOK], w[:, k, m * P:(m + 1) * P], hT[:, k], start=k == 0, stop=k == KT - 1)
                last.then_inc(S["proj_mm"], 1)

            def token_tiles(layer, n, unit):
                arrived(unit)
                w = wslot(unit, KT, 512)
                for t in range(NT):
                    bank_free(layer, n + t)
                    for k in range(KT):
                        last = mm(B[(n + t) % 2][:, :], hT[:, k, t * P:(t + 1) * P], w[:, k], start=k == 0, stop=k == KT - 1)
                    last.then_inc(S["proj_mm"], 1)

            for layer in range(DEPTH):
                at = ADA_AT[layer]

                def unit(i):
                    return at_ring("w", layer, i)

                wait(pe, "x_new", layer, 0)
                if layer == 0:
                    pe.wait_ge(sc_ok, 1)
                    ada_units(ADA_FIRST[:2], 0)
                sum_squares(layer, 1, sqT)
                if layer == 0:
                    ada_units(ADA_FIRST[2:], 0)
                    pe.wait_ge(ada_cp, len(ADA_FIRST))
                ada_units(at["n1"], 6)
                wait(pe, "h_a", layer, 4)
                wait(pe, "h_v", layer, 4)
                for i in range(3):
                    arrived(unit(i))
                    for m in range(4):
                        feature_tile(layer, 4 * i + m, unit(i), m)
                pe.wait_ge(lw_in, 16 * (7 + 6 * layer))
                for t in range(NT):
                    n = T_BA + t
                    bank_free(layer, n)
                    for k in range(KT):
                        last = mm(B[n % 2][:, 0:16], hT[:, k, t * P:(t + 1) * P], v3(baw, KT)[:, k], start=k == 0, stop=k == KT - 1)
                    last.then_inc(S["proj_mm"], 1)
                token_tiles(layer, T_A, unit(3))
                token_tiles(layer, T_A + 3, unit(4))
                token_tiles(layer, T_UV, unit(5))
                wait(pe, "dsq", layer, 1)
                for j in range(8):
                    if j >= 2:
                        wait(pe, "droot", layer, j - 1)
                    mm(B[2 + j % 2][:, 0:COUT], ones, dsq[:, j], start=True, stop=True).then_inc(S["dst"], 1)
                token_tiles(layer, T_UV + 3, unit(6))
                wait(pe, "g_ok", layer, 1)
                for t in range(NT):
                    c0 = 32 * t
                    mm(B[4][:, c0:c0 + 4], inclU, gg[:, t, 0:4], start=True, stop=True)
                    mm(B[4][:, c0 + 4:c0 + 8], inclL, gg[:, t, 4:8], start=True, stop=True)
                    mm(B[4][:, c0 + 8:c0 + 16], same, gg[:, t], start=True, stop=True)
                    last = mm(B[4][:, c0 + 16:c0 + 32], ones, gm[:, t].rearrange("p c n -> p (c n)"), start=True, stop=True)
                last.then_inc(S["gc_mm"], 1)
                if at["n1"]:
                    pe.wait_ge(ada_cp, at["n1"][-1] + 1)
                wait(pe, "qkn", layer, 1)
                wait(pe, "droot", layer, 8)
                for i, j0 in ((0, 8), (1, 4)):
                    for t in range(NT):
                        b = (5, 6, 7, 2, 3, 4)[3 * i + t]
                        if b == 4:
                            wait(pe, "gc_v", layer, 1)
                        for h in range(DNH):
                            last = tr(B[b][:, h * P:(h + 1) * P], cv[:, j0 + h, TCOL[t]:TCOL[t] + P])
                        last.then_inc(S["kvt_mm"], 1)
                wait(pe, "a_ok", layer, 1)
                pe.wait_ge(cache_in, 48 * (layer + 1))
                wait(pe, "kvt_ev", layer, 6)
                for t in range(NT):
                    for j in range(4):
                        last = tr(B[2 + t][:, j * P:(j + 1) * P], qkv[:, t, j * P:(j + 1) * P])
                    last.then_inc(S["tr_mm"], 1)
                for half in range(2):
                    for a in range(2):
                        for n in range(2):
                            src = (kcache if n else qkv[:, 0, 512:768]) if half == 0 else qkv[:, 1 + n, 512:768]
                            j = 2 * a + n
                            last = tr(B[5 + half][:, j * P:(j + 1) * P], src[:, a * P:(a + 1) * P])
                    last.then_inc(S["tr_mm"], 1)
                for g in range(4):
                    last = tr(B[7][:, g * P:(g + 1) * P], wsraw[:, g])
                last.then_inc(S["tr_mm"], 1)
                wait(pe, "tr_ev", layer, 6)
                wait(pe, "v_ok", layer, 1)
                for t in range(NT):
                    for g in range(4):
                        last = mm(B[2 + t][:, g * P:(g + 1) * P], v3(wsT, 4)[:, g], vB[:, t, g * P:(g + 1) * P], start=True, stop=True)
                    last.then_inc(S["b_mm"], 1)
                for t in range(NT):
                    wait(pe, "b_v", layer, t + 1)
                    for g in range(4):
                        last = tr(B[5 + t][:, g * P:(g + 1) * P], uB[:, t, g * P:(g + 1) * P])
                    last.then_inc(S["b_t"], 1)
                wait(pe, "b_ev", layer, 3)

                def scores(i):
                    t, h = divmod(i, HEADS)
                    a, b, cc = h // 4, h // 2 % 2, h % 2
                    if i >= 2:
                        wait(pe, "at_e", layer, i - 1)
                    keys = kTt[64 * b:64 * b + 64, a, 0:P] if t == 0 else kTt[64 * b:64 * b + 64, a, P:512]
                    q = qTt[64 * b:64 * b + 64, 2 * a + cc, t * P:(t + 1) * P]
                    mm(B[2 + i % 2][:, 0:P if t == 0 else TOK], q, keys, start=True, stop=True).then_inc(S["at_s"], 1)

                def flip(i):
                    wait(pe, "at_p", layer, i + 1)
                    if i >= 2:
                        wait(pe, "at_pt", layer, i - 1)
                    n = 1 if i < HEADS else 3
                    for kt in range(n):
                        last = tr(B[4 + i % 2][:, kt * P:(kt + 1) * P], Pb[:, i % 2, kt * P:(kt + 1) * P])
                    last.then_inc(S["at_t"], 1)

                def weigh(i):
                    t, h = divmod(i, HEADS)
                    wait(pe, "at_pt", layer, i + 1)
                    if h == 0 and t == 2:
                        wait(pe, "at_o", layer, 1)
                    g = h // 2
                    vs = [qkv[:, 0, 768:1024]] if t == 0 else [vcache, qkv[:, 1, 768:1024], qkv[:, 2, 768:1024]]
                    out = B[6 + t % 2][64 * (h % 2):64 * (h % 2) + 64, (h // 2) * P:(h // 2 + 1) * P]
                    for kt, v in enumerate(vs):
                        last = mm(out, v[:, HD * g:HD * (g + 1)], PTb[:, i % 2, kt * P:(kt + 1) * P],
                                  start=kt == 0, stop=kt == len(vs) - 1)
                    last.then_inc(S["at_pv"], 1)

                wait(pe, "proj_ev", layer, T_UV + 6)
                for i in range(NT * HEADS + 2):
                    if i < NT * HEADS:
                        scores(i)
                        ada_row(at["at"][i // KT], i % KT, 0)
                    if 1 <= i <= NT * HEADS:
                        flip(i - 1)
                    if i >= KT and i % KT == 2 and i < NT * HEADS:
                        ada_turn(at["at"][i // KT - 1], 0, GT)
                    if i >= 2:
                        weigh(i - 2)
                ada_turn(at["at"][-1], 0, GT)

                nfill = [0]

                def fill():
                    n = nfill[0]
                    nfill[0] += 1
                    if n % 4 == 0:
                        arrived(unit(7 + n // 4))
                    feature_tile(layer, T_G + n, unit(7 + n // 4), n % 4)

                wait(pe, "at_o", layer, 3)
                pe.wait_ge(ada_cp, at["at"][-1] + 1)
                for pair in range(3):
                    fill()
                    for d in range(2):
                        t = TILE[pair][d]
                        g = 2 * pair + d
                        X, Y, Z = B[2 + 3 * d], B[3 + 3 * d], B[4 + 3 * d]
                        if pair:
                            wait(pe, "s_or", layer, g - 1)
                        cols = slice(TCOL[t], TCOL[t] + P)
                        for h in range(DNH):
                            hs = slice(h * P, (h + 1) * P)
                            mm(X[:, hs], gg[:, t, 4 * d + h:4 * d + h + 1].to_broadcast([P, P]), inclU if d == 0 else inclL, start=True, stop=True)
                        for h in range(DNH):
                            hs = slice(h * P, (h + 1) * P)
                            mm(Y[:, hs], cv[:, 4 + h, cols], cv[:, 4 + h, cols], start=True, stop=True)
                        for h in range(DNH):
                            hs = slice(h * P, (h + 1) * P)
                            last = mm(Z[:, hs], cv[:, 4 + h, cols], cv[:, h, cols], start=True, stop=True)
                        last.then_inc(S["d_in"], 1)
                    fill()
                    for d in range(2):
                        wait(pe, "d_m", layer, 2 * pair + d + 1)
                        for h in range(DNH):
                            last = tr(B[2 + 3 * d][:, h * P:(h + 1) * P], dn(d, B_M)[:, h])
                        last.then_inc(S["d_mt"], 1)
                    for s in range(1, len(LEVELS)):
                        fill()
                        for d in range(2):
                            n = 10 * pair + 2 * (s - 1) + d + 1
                            wait(pe, "d_ct", layer, n)
                            if s == 1:
                                wait(pe, "d_t1", layer, 2 * pair + d + 1)
                            else:
                                wait(pe, "d_up", layer, n - 2)
                            for h in range(DNH):
                                last = mm(B[2 + 3 * d][:, h * P:(h + 1) * P], dn(d, B_CT)[:, h], dn(d, B_T)[:, h], start=True, stop=True)
                            last.then_inc(S["d_w"], 1)
                        for d in range(2):
                            n = 10 * pair + 2 * (s - 1) + d + 1
                            wait(pe, "d_we", layer, n)
                            for h in range(DNH):
                                hs = slice(h * P, (h + 1) * P)
                                if s < len(LEVELS) - 1:
                                    mm(B[3 + 3 * d][:, hs], dn(d, B_U)[:, h], dn(d, B_W)[:, h], start=True, stop=True)
                            for h in range(DNH):
                                hs = slice(h * P, (h + 1) * P)
                                last = mm(B[4 + 3 * d][:, hs], dn(d, B_W)[:, h], dn(d, B_U)[:, h], start=True, stop=True)
                            last.then_inc(S["d_du"], 1)
                    for d in range(2):
                        g = 2 * pair + d
                        wait(pe, "d_up", layer, 10 * pair + 8 + d + 1)
                        for h in range(DNH):
                            mm(B[2 + 3 * d][:, h * P:(h + 1) * P], dn(d, B_U)[:, h], dn(d, B_VU)[:, h], start=True, stop=True)
                        for h in range(DNH):
                            last = mm(B[3 + 3 * d][:, h * P:(h + 1) * P], dn(d, B_KW)[:, h], dn(d, B_U)[:, h], start=True, stop=True)
                        last.then_inc(S["d_uw"], 1)
                    for step in range(2):
                        for d in range(2):
                            g, n = 2 * pair + d, 4 * pair + 2 * step + d
                            X = B[2 + 3 * d]
                            ch = step if d == 0 else 1 - step
                            r = slice(CHUNK * ch, CHUNK * (ch + 1))
                            wait(pe, "d_uwe", layer, g + 1)
                            if step:
                                wait(pe, "s_st", layer, n - 1)
                            elif pair == 1:
                                pe.wait_ge(st_in, 32 * (layer + 1))
                            for h in range(DNH):
                                last = mm(X[r, h * P:(h + 1) * P], dn(d, B_KW)[:, h, r], state[:, d, h], start=True, stop=True)
                            last.then_inc(S["s_ws"], 1)
                        if step == 0:
                            fill()
                        for d in range(2):
                            g, n = 2 * pair + d, 4 * pair + 2 * step + d
                            Y, Z = B[3 + 3 * d], B[4 + 3 * d]
                            ch = step if d == 0 else 1 - step
                            r = slice(CHUNK * ch, CHUNK * (ch + 1))
                            wait(pe, "s_vn", layer, n + 1)
                            wait(pe, "d_kd", layer, g + 1)
                            for h in range(DNH):
                                mm(Z[:, h * P:(h + 1) * P], dn(d, B_KD)[r, h], dn(d, B_VN)[r, h], start=True, stop=True)
                            for h in range(DNH):
                                hs = slice(h * P, (h + 1) * P)
                                mm(Y[r, hs], dn(d, B_QEG)[:, h, r], state[:, d, h], start=True, stop=False)
                                last = mm(Y[r, hs], dn(d, B_QK)[r, h, r], dn(d, B_VN)[r, h], start=False, stop=True)
                            last.then_inc(S["s_o"], 1)
                assert nfill[0] == 24
                wait(pe, "proj_ev", layer, T_Z)
                ada_units(at["z"], 0)
                pe.wait_ge(ada_cp, at["z"][-1] + 1)
                wait(pe, "s_or", layer, 6)
                token_tiles(layer, T_Z, unit(13))
                oc_unit, = at["oc"]
                for k in range(KT):
                    ada_row(oc_unit, k, 6)
                for t in range(NT):
                    if t == 0:
                        wait(pe, "oc_v", layer, 1)
                    for h in range(DNH):
                        last = tr(B[2 + t][:, h * P:(h + 1) * P], osum[:, t, h * P:(h + 1) * P])
                    last.then_inc(S["oc_mm"], 1)
                wait(pe, "oc_ev", layer, 3)
                ada_turn(oc_unit, 6, KK_)
                for m in range(8):
                    if m == 1:
                        pe.wait_ge(ada_cp, oc_unit + 1)
                    if m % 2 == 0:
                        arrived(unit(14 + m // 2))
                    if m >= 2:
                        wait(pe, "br_ev", layer, m - 1)
                    w = wslot(unit(14 + m // 2), 12, 256)
                    for b in range(3):
                        for k in range(4):
                            last = mm(B[2 + 3 * (m % 2) + b][:, 0:TOK], w[:, 4 * b + k, (m % 2) * P:(m % 2 + 1) * P], oT[:, b, k],
                                      start=k == 0, stop=k == 3)
                    last.then_inc(S["br_mm"], 1)
                wait(pe, "br_ev", layer, 8)
                for m in range(8):
                    if m % 4 == 0:
                        arrived(unit(18 + m // 4))
                    if m >= 2:
                        wait(pe, "wo_ev", layer, m - 1)
                    w = wslot(unit(18 + m // 4), KT, 512)
                    for k in range(KT):
                        last = mm(B[m % 2][:, 0:TOK], w[:, k, (m % 4) * P:(m % 4 + 1) * P], merged[:, k], start=k == 0, stop=k == KT - 1)
                    last.then_inc(S["wo_mm"], 1)
                sum_squares(layer, 2, sqP)
                ada_units(at["n3"], 6, ada_buf)
                sum_squares(layer, 3, sqT)
                ada_units(at["h3"], 6, ada_buf)
                wait(pe, "h_a", layer, 8)
                wait(pe, "h_v", layer, 8)

                def split_product(out, w_hi, w_lo, x_hi, x_lo, n):
                    for k in range(n):
                        mm(out, w_hi(k), x_hi[:, k], start=k == 0, stop=False)
                        mm(out, w_hi(k), x_lo[:, k], start=False, stop=False)
                        last = mm(out, w_lo(k), x_hi[:, k], start=False, stop=k == n - 1)
                    return last

                def gate_up(j, it=None):
                    first = 2 * j + (2 * FF_LOOP * it if it is not None else 0)
                    parts = [(v3(hi, KT), v3(lo, KT)) for _, hi, lo in ff_parts(j)]
                    for r in range(2):
                        for g, (done, used) in enumerate(((gu_g, gu_s), (gu_u, gu_h))):
                            if r == 0:
                                pe.wait_ge(w_lo, ff_part(j, it, g))
                            if j:
                                pe.wait_ge(used, first + r - 1)
                            hi, lo = parts[g]
                            split_product(B[2 * g + r][:, 0:TOK], lambda k: hi[:, k, r * P:(r + 1) * P],
                                          lambda k: lo[:, k, r * P:(r + 1) * P], hT_hi, hT_lo, KT).then_inc(done, 1)

                if layer == 0:
                    pe.wait_ge(hs_ok, 2)
                    gate_up(0)
                    with pe.Fori(0, 2) as it:
                        for j in range(1, 1 + FF_LOOP):
                            gate_up(j, it)
                    for j in range(1 + 2 * FF_LOOP, FF_GU):
                        gate_up(j)
                    pe.wait_ge(gu_h, FG)
                    for m in range(8):
                        j = FF_GU + m
                        pe.wait_ge(w_lo, ff_part(j, None, 0))
                        if m >= 2:
                            pe.wait_ge(down_ev, m - 1)
                        (_, hi, lo), = ff_parts(j)
                        split_product(B[4 + m % 2][:, 0:TOK], lambda k: v3(hi, FG)[:, k], lambda k: v3(lo, FG)[:, k],
                                      hid_hi, hid_lo, FG).then_inc(down_mm, 1)
                else:
                    pe.wait_ge(ada_cp, 2 * ADA_U)
                    for t in range(NT):
                        for k in range(KT):
                            last = mm(B[6][:, NE * t:NE * (t + 1)], hT[:, k, t * P:(t + 1) * P], v3(rtw[:, :], KT)[:, k],
                                      start=k == 0, stop=k == KT - 1)
                    last.then_inc(rl_mm, 1)
                    for n in range(2 * NT):
                        t, half = divmod(n, 2)
                        for k in range(4):
                            last = tr(B[H_BANK[n]][:, k * P:(k + 1) * P], hT[:, 4 * half + k, t * P:(t + 1) * P])
                        last.then_inc(ht_mm, 1)
                    pe.wait_ge(rl_ok, 1)
                    pe.wait_ge(route_in, 16)
                    for t in range(NT + 1):
                        c0 = 32 + NE * t
                        for a in range(min(t + 1, NT)):
                            last = mm(B[6][:, c0:c0 + NE], tri if a == t else ones, sel2[0][:, a], start=a == 0,
                                      stop=a == min(t, NT - 1))
                    last.then_inc(rk_mm, 1)

                    def gather(half):
                        for m in range(4 * half, 4 * half + 4):
                            for t in range(NT):
                                last = mm(B[4 + half][:, (m % 4) * P:(m % 4 + 1) * P], h2tok[:, t, m * P:(m + 1) * P], esel[:, t],
                                          start=t == 0, stop=t == NT - 1)
                        last.then_inc(ga_mm, 1)

                    def scatter(i):
                        pe.wait_ge(yt_ok, 2 * i + 2)
                        pe.wait_ge(wt_ev, i + 1)
                        for m in range(KT):
                            pe.wait_ge(sc_ad, KT * i + (m if m else 1))
                            mm(B[6 + m % 2][:, 0:TOK], ytok[:, m * P:(m + 1) * P], scatT, start=True, stop=True).then_inc(sc_mm, 1)

                    pe.wait_ge(ht_ev, 2 * NT)
                    pe.wait_ge(sel_ok, 1)
                    gather(0)
                    gather(1)

                    def product(out, j, h, x_hi, x_lo):
                        hi, lo = m_view(w_upper[j % 2], j), m_view(m_place(j, True), j)
                        n_k = m_shape(j)[1]
                        for k in m_tiles(j, h):
                            mm(out, x_hi[:, k], hi[:, :, k], start=k == 0, stop=False)
                            mm(out, x_hi[:, k], lo[:, :, k], start=False, stop=False)
                            last = mm(out, x_lo[:, k], hi[:, :, k], start=False, stop=k == n_k - 1)
                        return last

                    def turn_hidden(j, i):
                        pe.wait_ge(mh_ok, M_GU * i + j + 1)
                        if j >= 2:
                            pe.wait_ge(hl_ok, M_GU * i + j - 1)
                        for m in range(m_shape(j)[2] // P):
                            last = tr(B[2 + j % 2][:, m * P:(m + 1) * P], ehid[:, j % 2, m * P:(m + 1) * P])
                        last.then_inc(th_mm, 1)

                    n_items = pe.value_load(table[0:1, NI:NI + 1], min_val=MIN_ITEMS, max_val=NI - 1)
                    with pe.Fori(0, n_items) as i:
                        pe.wait_ge(ga_lo, 2 * i + 2)
                        for j in range(M_GU):
                            if j >= 2:
                                pe.wait_ge(mh_ok, M_GU * i + j - 1)
                            out = B[j % 2][:, 0:2 * m_shape(j)[2]].rearrange("p (g n) -> p g n", g=2)
                            for h in range(M_HALF):
                                m_split(pe, j, h, i)
                                product(out, j, h, xg_hi, xg_lo).then_inc(mg_mm, 1)
                            if j == 0:
                                scatter(i)
                            else:
                                turn_hidden(j - 1, i)
                        pe.wait_ge(sel_ok, i + 2)
                        pe.wait_ge(sc_ad, KT * i + KT)
                        for t in range(NT):
                            last = tr(B[6][:, t * P:(t + 1) * P], wsel[:, t])
                        last.then_inc(wt_mm, 1)
                        gather(0)
                        turn_hidden(M_GU - 1, i)
                        gather(1)
                        pe.wait_ge(hl_ok, M_GU * i + M_GU)
                        for j in range(M_GU, M_GU + M_DN):
                            c0 = 256 * (j - M_GU)
                            out = B[2 + c0 // 512][:, c0 % 512:c0 % 512 + 256].rearrange("p (g n) -> p g n", g=1)
                            for h in range(M_HALF):
                                m_split(pe, j, h, i)
                                product(out, j, h, ehid_hi, ehid_lo).then_inc(dn_mm, 1)
                    scatter(n_items)
                sum_squares(layer, 4, sqP)
                ada_units(at["n4"], 6, ada_buf)
            wait(pe, "x_new", DEPTH, 0)
            for t in range(NT):
                for half in range(2):
                    for k in range(4):
                        last = tr(B[2 + 2 * t + half][:, k * P:(k + 1) * P], xT[:, 4 * half + k, t * P:(t + 1) * P])
                    last.then_inc(xo_mm, 1)

        @block.scalar
        def _(act):
            go = nc.scalar.activation
            link = linker(act, act_step)

            def copy(out, in_):
                return go(out, in_, ACT.Copy)

            act.wait_ge(rt_ev, 4)
            go(rows[:, 160:176], rows[:, 160:176], ACT.Silu).then_inc(sc_ok, 1)
            for t in range(NT):
                for half in range(2):
                    act.wait_ge(xt_mm, 2 * t + half + 1)
                    copy(xT[:, 4 * half:4 * half + 4, t * P:(t + 1) * P], v3(B[2 + 2 * t + half][:, :], 4)).then_inc(xt_ev, 1)

            def square(src, dst):
                go(dst, src, ACT.Square).then_inc(S["sq"], 1)

            def root(layer, q):
                wait(act, "stat", layer, q)
                go(rs[:, :], B[2][:, 0:TOK], ACT.Sqrt, bias=eps1, scale=1.0 / D).then_inc(S["root"], 1)

            def modulate(layer, q, a):
                wait(act, "xn", layer, q)
                act.wait_ge(mod_ok, 4 * layer + (1 if a == 0 else 3))
                for k in range(4):
                    for s, lo, hi in SEG:
                        last = go(hT[:, k, lo:hi], hT[:, k, lo:hi], ACT.Identity, bias=mod[:, layer, a, k, s:s + 1],
                                  scale=mod[:, layer, a + 1, k, s:s + 1])
                    last.then_inc(S["h_a"], 1)

            def ada_copy(n, b, buf):
                act.wait_ge(ada_mm, n + 1)
                copy(ada_rows(n, buf), B[b + n % 2][0:2, :]).then_inc(ada_ev, 1)

            act.wait_ge(xt_ev, 2 * NT)
            for layer in range(DEPTH):
                at = ADA_AT[layer]

                def evac(n, out, func=ACT.Copy, width=512):
                    wait(act, "proj_mm", layer, n + 1)
                    go(out, B[n % 2][:, 0:width], func).then_inc(S["proj_ev"], 1)

                wait(act, "x_new", layer, 0)
                square(xT, sqT)
                if layer == 0:
                    for n in ADA_FIRST[:2]:
                        ada_copy(n, 0, KK_)
                root(layer, 1)
                if layer == 0:
                    for n in ADA_FIRST[2:]:
                        ada_copy(n, 0, KK_)
                modulate(layer, 1, 0)
                for n in at["n1"]:
                    ada_copy(n, 6, KK_)
                wait(act, "pads", layer, 1)
                for j in range(12):
                    wait(act, "proj_mm", layer, j + 1)
                    copy(pre[:, j, 2:2 + CTX], B[j % 2][:, 0:CTX])
                    copy(pre[:, j, CTX + 6:CTX + 6 + LAT], B[j % 2][:, CTX:TOK]).then_inc(S["proj_ev"], 1)
                for t in range(NT):
                    evac(T_BA + t, ba[:, t], width=16)
                act.wait_ge(parked, 16 * (layer + 1))
                for t in range(NT):
                    wait(act, "proj_mm", layer, T_A + t + 1)
                    for a in range(2):
                        src = B[(T_A + t) % 2][:, 256 * a:256 * a + 256].rearrange("p (b c d) -> p b c d", b=2, c=2)
                        dst = qkv[:, t, 256 * a:256 * a + 256].rearrange("p (c b d) -> p b c d", b=2, c=2)
                        last = copy(dst, src)
                    last.then_inc(S["proj_ev"], 1)
                for t in range(NT):
                    evac(T_A + 3 + t, qkv[:, t, 512:1024])
                wait(act, "proj_ev", layer, T_A + 6)
                go(asq, qkv[:, :, 0:768], ACT.Square).then_inc(S["a_sq"], 1)
                go(beta, ba[:, :, 0:8], ACT.Sigmoid)
                act.wait_ge(lw_in, 16 * (7 + 6 * layer))
                wait(act, "ba_v", layer, 1)
                link(go(t2, t1, ACT.Abs))
                link(go(t2, t2, ACT.Exp, scale=-1.0))
                go(expa, expa, ACT.Exp)
                go(t2, t2, ACT.Ln, bias=one1).then_inc(S["ba_l"], 1)
                for t in range(NT):
                    evac(T_UV + t, uB[:, t], ACT.Gelu_apprx_tanh)
                wait(act, "conv", layer, 12)
                for i in range(3):
                    last = go(CV[:, 4 * i * COUT:4 * (i + 1) * COUT], CV[:, 4 * i * COUT:4 * (i + 1) * COUT], ACT.Silu)
                    last.then_inc(S["silu"], 1)
                wait(act, "silu", layer, 3)
                go(GT[:, 12 * CROW:12 * CROW + 8 * COUT], CV[:, 0:8 * COUT], ACT.Square).then_inc(S["dsq"], 1)
                for j in range(8):
                    wait(act, "dst", layer, j + 1)
                    go(dsq[:, j], B[2 + j % 2][:, 0:COUT], ACT.Sqrt, bias=eps128 if j < 4 else eps1,
                       scale=float(DK) if j < 4 else 1.0).then_inc(S["droot"], 1)
                wait(act, "a_ss", layer, 1)
                go(ass, ass, ACT.Sqrt, bias=eps1, scale=1.0 / HD).then_inc(S["a_rt"], 1)
                for t in range(NT):
                    evac(T_UV + 3 + t, vB[:, t], ACT.Gelu_apprx_tanh)
                wait(act, "proj_ev", layer, T_UV + 6)
                wait(act, "qkn", layer, 1)
                for t in range(NT):
                    link(go(gsc, vB[:, t], ACT.Square, accum_out=vss[:, t:t + 1]))
                go(vss, vss, ACT.Sqrt, bias=eps1, scale=1.0 / 512).then_inc(S["v_rt"], 1)
                wait(act, "gc_v", layer, 1)
                go(edec, edec, ACT.Exp)
                go(egl, egl, ACT.Exp)
                go(eg, gcs, ACT.Exp).then_inc(S["gc_e"], 1)
                wait(act, "kvt_mm", layer, 3)
                for i in range(6):
                    wait(act, "kvt_mm", layer, i + 1)
                    dst = vtok[:, i] if i < 3 else ktok[:, i - 3]
                    copy(dst, v3(B[(5, 6, 7, 2, 3, 4)[i]][:, :], 4)).then_inc(S["kvt_ev"], 1)
                for i in range(6):
                    wait(act, "tr_mm", layer, i + 1)
                    if i < 3:
                        copy(qTt[:, :, i * P:(i + 1) * P], v3(B[2 + i][:, :], 4)).then_inc(S["tr_ev"], 1)
                    elif i < 5:
                        copy(kTt[:, :, 256 * (i - 3):256 * (i - 2)], v3(B[2 + i][:, :], 2)).then_inc(S["tr_ev"], 1)
                    else:
                        copy(wsT, B[7][:, :]).then_inc(S["tr_ev"], 1)
                for t in range(NT):
                    wait(act, "b_t", layer, t + 1)
                    copy(oT[:, 1, :, t * P:(t + 1) * P], v3(B[5 + t][:, :], 4)).then_inc(S["b_ev"], 1)
                n_at = NT * HEADS
                for i in range(n_at + 3):
                    if i < n_at:
                        w = P if i < HEADS else TOK
                        wait(act, "at_m", layer, i + 1)
                        if i >= 2:
                            wait(act, "at_t", layer, i - 1)
                        go(Pb[:, i % 2, 0:w], B[2 + i % 2][:, 0:w], ACT.Exp, bias=anm[:, i:i + 1], scale=HD ** -0.5,
                           accum_out=ars[:, i:i + 1]).then_inc(S["at_e"], 1)
                    if i >= KT and i % KT == 1 and i < n_at:
                        ada_copy(at["at"][i // KT - 1], 0, GT)
                    if 1 <= i <= n_at:
                        j = i - 1
                        w = P if j < HEADS else TOK
                        wait(act, "at_t", layer, j + 1)
                        if j >= 2:
                            wait(act, "at_pv", layer, j - 1)
                        copy(PTb[:, j % 2, 0:w], B[4 + j % 2][:, 0:w]).then_inc(S["at_pt"], 1)
                    if i >= 10 and i % 8 == 2:
                        t = i // 8 - 1
                        wait(act, "at_pv", layer, 8 * (t + 1))
                        copy(oT[:, 0, :, t * P:(t + 1) * P], v3(B[6 + t % 2][:, :], 4)).then_inc(S["at_o"], 1)
                ada_copy(at["at"][-1], 0, GT)
                nfill = [0]

                def gate():
                    n = nfill[0]
                    nfill[0] += 1
                    evac(T_G + n, gates[:, n], width=TOK)

                for pair in range(3):
                    gate()
                    for d in range(2):
                        wait(act, "d_d0", layer, 2 * pair + d + 1)
                        go(dn(d, B_QEG), v3(B[2 + 3 * d][:, :], 4), ACT.Exp)
                        go(dn(d, B_M), dn(d, B_M), ACT.Exp, scale=-1.0)
                        go(dn(d, B_QK), dn(d, B_QK), ACT.Exp).then_inc(S["d_e"], 1)
                    gate()
                    for s in range(1, len(LEVELS)):
                        gate()
                        for d in range(2):
                            wait(act, "d_w", layer, 10 * pair + 2 * (s - 1) + d + 1)
                            copy(dn(d, B_W), v3(B[2 + 3 * d][:, :], 4)).then_inc(S["d_we"], 1)
                    for d in range(2):
                        wait(act, "d_uw", layer, 2 * pair + d + 1)
                        copy(dn(d, B_VU), v3(B[2 + 3 * d][:, :], 4))
                        copy(dn(d, B_KW), v3(B[3 + 3 * d][:, :], 4)).then_inc(S["d_uwe"], 1)
                    gate()
                for n in at["z"]:
                    ada_copy(n, 0, KK_)
                for t in range(NT):
                    evac(T_Z + t, zs[:, t], ACT.Silu)
                go(RX[:, 6144:7680], OT[:, 3072:4608], ACT.Square).then_inc(S["oc_sq"], 1)
                wait(act, "oc_ss", layer, 1)
                go(oss, oss, ACT.Sqrt, bias=eps1, scale=1.0 / DK).then_inc(S["oc_rt"], 1)
                wait(act, "proj_ev", layer, T_Z)
                go(GT[:, :], GT[:, :], ACT.Sigmoid).then_inc(S["gsig"], 1)
                wait(act, "oc_mm", layer, 3)
                for t in range(NT):
                    copy(oT[:, 2, :, t * P:(t + 1) * P], v3(B[2 + t][:, :], 4)).then_inc(S["oc_ev"], 1)
                ada_copy(at["oc"][0], 6, KK_)
                for m in range(8):
                    wait(act, "wo_mm", layer, m + 1)
                    copy(yT[:, m], B[m % 2][:, 0:TOK]).then_inc(S["wo_ev"], 1)
                wait(act, "wo_ev", layer, 8)
                square(yT, sqP)
                root(layer, 2)
                for n in at["n3"]:
                    ada_copy(n, 6, ada_buf)
                wait(act, "x_new", layer, 1)
                square(xT, sqT)
                root(layer, 3)
                modulate(layer, 2, 3)
                for n in at["h3"]:
                    ada_copy(n, 6, ada_buf)

                def silu(idx, r, later):
                    act.wait_ge(gu_g, idx + 1)
                    if later:
                        act.wait_ge(gu_h, idx - 1)
                    go(sgb[:, r], B[r][:, 0:TOK], ACT.Silu).then_inc(gu_s, 1)

                if layer == 0:
                    def upper_parts(j, it=None):
                        ff_arrived(act, j, it)
                        if j < 2:
                            freed(act, at_ring("ff_hi", j))
                        for raw, hi, _ in ff_parts(j):
                            copy(hi, raw).then_inc(w_hi, 1)

                    def unit(j, it=None):
                        upper_parts(j + 1, it)
                        for r in range(2):
                            silu(2 * j + r + (2 * FF_LOOP * it if it is not None else 0), r, j > 0)

                    wait(act, "h_a", layer, 8)
                    copy(hT_hi[:, 0:4], hT[:, 0:4]).then_inc(hs_a, 1)
                    upper_parts(0)
                    unit(0)
                    with act.Fori(0, 2) as it:
                        for j in range(1, 1 + FF_LOOP):
                            unit(j, it)
                    for j in range(1 + 2 * FF_LOOP, FF_GU):
                        unit(j)
                    for m in range(1, 8):
                        upper_parts(FF_GU + m)
                    act.wait_ge(down_ev, 8)
                else:
                    act.wait_ge(ht_mm, 2 * NT)
                    for n in range(2 * NT):
                        copy(h2tok[:, n // 2, 512 * (n % 2):512 * (n % 2 + 1)], B[H_BANK[n]][:, :]).then_inc(ht_ev, 1)
                    act.wait_ge(rl_c, 1)
                    go(m8[:, 1::8], m8[:, 1::8], ACT.Exp).then_inc(rl_e, 1)

                    def gathered(i):
                        for half in range(2):
                            act.wait_ge(ga_mm, 2 * i + half + 1)
                            copy(xg_hi[:, 4 * half:4 * half + 4], v3(B[4 + half][:, :], 4)).then_inc(ga_ev, 1)

                    def hidden_upper(j, i):
                        act.wait_ge(th_mm, M_GU * i + j + 1)
                        n = m_shape(j)[2] // P
                        copy(ehid_hi[:, 2 * j:2 * j + n], v3(B[2 + j % 2][:, 0:n * P], n)).then_inc(hh_ok, 1)

                    def ahead(j, h, i):
                        j2, i2 = (j + 2, i) if j + 2 < M_GU + M_DN else (j + 2 - M_GU - M_DN, i + 1)
                        m_used(act, j, h if m_shape(j) == m_shape(j2) else 1, i)
                        m_upper(act, j2, h, i2)

                    def item_upper(i, last):
                        for j in range(M_GU):
                            if j:
                                ahead(j, 0, i)
                            n = m_shape(j)[2]
                            act.wait_ge(mg_mm, G_IT * i + M_HALF * (j + 1))
                            if j >= 2:
                                act.wait_ge(mh_ok, M_GU * i + j - 1)
                            go(esg[:, j % 2, 0:n], B[j % 2][:, 0:n], ACT.Silu).then_inc(msg_ok, 1)
                            if j == 0:
                                ahead(0, 0, i)
                            ahead(j, 1, i)
                            if j:
                                hidden_upper(j - 1, i)
                        act.wait_ge(wt_mm, i + 1)
                        copy(scatT, B[6][:, 0:TOK]).then_inc(wt_ev, 1)
                        hidden_upper(M_GU - 1, i)
                        gathered(i + 1)
                        for j in range(M_GU, M_GU + M_DN):
                            if j < M_GU + 2 or not last:
                                for h in range(M_HALF):
                                    ahead(j, h, i)
                            if j % 2:
                                half = (j - M_GU) // 2
                                act.wait_ge(dn_mm, D_IT * i + M_HALF * 2 * (half + 1))
                                copy(ytok[:, 512 * half:512 * (half + 1)], B[2 + half][:, :]).then_inc(yt_ok, 1)

                    for j in range(2):
                        for h in range(M_HALF):
                            m_upper(act, j, h, 0)
                    gathered(0)
                    n_items = act.value_load(table[0:1, NI:NI + 1], min_val=MIN_ITEMS, max_val=NI - 1)
                    last_item = act.value_load(table[0:1, NI + 1:NI + 2], min_val=MIN_ITEMS - 1, max_val=NI - 2)
                    with act.Fori(0, last_item) as i:
                        item_upper(i, False)
                    item_upper(last_item, True)
                    act.wait_ge(sc_ad, KT * n_items + KT + 1)
                square(yT, sqP)
                root(layer, 4)
                for n in at["n4"]:
                    ada_copy(n, 6, ada_buf)
            for t in range(NT):
                for half in range(2):
                    act.wait_ge(xo_mm, 2 * t + half + 1)
                    copy(v3(GT[:, 0:3072], NT)[:, t, 512 * half:512 * (half + 1)], B[2 + 2 * t + half][:, :]).then_inc(xo_ev, 1)

        @block.vector
        def _(dve):
            v = nc.vector
            link = linker(dve, dve_step)

            def note(ins, name, layer, n):
                ins.then_inc(S[name], 1)
                wait(dve, name, layer, n)

            def note1(ins, signal):
                ins.then_inc(signal, 1)
                dve.wait_ge(signal, 1)

            def bc(ap, n):
                return ap.unsqueeze(2).to_broadcast([P, ap.shape[1], n])

            for i, (lo, n) in enumerate(((0, 64), (64, 96), (160, 24), (184, 120))):
                dve.wait_ge(rt_mm, 4)
                v.tensor_copy(rows[:, lo:lo + n], B[0][:, i * P:i * P + n]).then_inc(rt_ev, 1)
            dve.wait_ge(rt_ev, 4)
            dve.wait_ge(mask_in, 16)
            v.tensor_copy(lmask[:, :], RX[:, 6144:6144 + NMASK]).then_inc(bf_ok, 1)
            dve.wait_ge(xt_ev, 2 * NT)

            def ada_take(n, b):
                layer, i = divmod(n, ADA_U)
                dve.wait_ge(ada_t, n + 1)
                dst = mod[:, layer].rearrange("p a k s -> p (a k) s")[:, 4 * i:4 * i + 4]
                v.tensor_tensor(dst, v3(B[b + n % 2][:, 0:8], 4), bc(adab[:, layer, 4 * i:4 * i + 4], 2), ALU.add).then_inc(ada_cp, 1)
                if i in ADA_DONE:
                    dve.wait_ge(ada_cp, n + 1)
                    a, g = ADA_DONE[i]
                    m = mod[:, layer, a]
                    if a in (1, 4):
                        link(v.tensor_scalar(m, m, 1.0, None, ALU.add))
                    v.tensor_tensor(m, m, bc(nrmT[:, layer, g], 2), ALU.mult).then_inc(mod_ok, 1)

            def rstd(layer, q):
                wait(dve, "root", layer, q)
                note(v.reciprocal(rs[:, :], rs[:, :]), "rinv", layer, q)

            def normed(layer, n, a, units=()):
                note(v.tensor_tensor(hT, xT, rs[:, :].unsqueeze(1).to_broadcast([P, KT, TOK]), ALU.mult), "xn", layer, n)
                for u in units:
                    ada_take(u, 0)
                dve.wait_ge(mod_ok, 4 * layer + (1 if a == 0 else 3))
                for k in range(4, 8):
                    for s, lo, hi in SEG:
                        last = v.tensor_scalar(hT[:, k, lo:hi], hT[:, k, lo:hi], mod[:, layer, a + 1, k, s:s + 1],
                                               mod[:, layer, a, k, s:s + 1], ALU.mult, ALU.add)
                    last.then_inc(S["h_v"], 1)

            def add_branch(layer, q, a, n):
                rstd(layer, q)
                link(v.tensor_tensor(yT, yT, rs[:, :].unsqueeze(1).to_broadcast([P, KT, TOK]), ALU.mult))
                dve.wait_ge(mod_ok, 4 * layer + (2 if a == 2 else 4))
                for k in range(KT):
                    for s, lo, hi in SEG:
                        last = v.scalar_tensor_tensor(xT[:, k, lo:hi], yT[:, k, lo:hi], mod[:, layer, a, k, s:s + 1], xT[:, k, lo:hi],
                                                      ALU.mult, ALU.add)
                note(last, "x_new", layer, n)

            for layer in range(DEPTH):
                at = ADA_AT[layer]
                rstd(layer, 1)
                normed(layer, 1, 0, ADA_FIRST if layer == 0 else ())
                for n in at["n1"]:
                    ada_take(n, 6)
                v.memset(pre[:, :, 0:2], 0.0)
                v.memset(pre[:, :, CTX + 2:CTX + 6], 0.0)
                note(v.memset(pre[:, :, CROW - 2:CROW], 0.0), "pads", layer, 1)
                for j in range(12):
                    wait(dve, "proj_ev", layer, j + 1)
                    w = cwT[:, layer, :, j]
                    link(v.tensor_scalar(cv[:, j], pre[:, j, 0:COUT], w[:, 0:1], None, ALU.mult))
                    for k in range(1, CONV_K):
                        ins = v.scalar_tensor_tensor(cv[:, j], pre[:, j, k:k + COUT], w[:, k:k + 1], cv[:, j], ALU.mult, ALU.add)
                        if k < CONV_K - 1:
                            link(ins)
                    ins.then_inc(S["conv"], 1)
                wait(dve, "proj_ev", layer, T_BA + 3)
                dve.wait_ge(lw_in, 16 * (7 + 6 * layer))
                note(v.tensor_tensor(t1, ba[:, :, 8:16], dtb.unsqueeze(1).to_broadcast([P, NT, 8]), ALU.add), "ba_v", layer, 1)
                wait(dve, "a_sq", layer, 1)
                v.tensor_reduce(ass, asq.rearrange("p t (h d) -> p (t h) d", d=HD), AX.X, ALU.add).then_inc(S["a_ss"], 1)
                wait(dve, "ba_l", layer, 1)
                link(v.scalar_tensor_tensor(gg, t1, 0.0, t2, ALU.max, ALU.add))
                link(v.scalar_tensor_tensor(gg, gg, -1.0, expa.unsqueeze(1).to_broadcast([P, NT, 8]), ALU.mult, ALU.mult))
                v.tensor_scalar(gm[:, :, 0], gg, chsel[:, 0:1], None, ALU.mult)
                v.tensor_scalar(gm[:, :, 1], gg, chsel[:, 1:2], None, ALU.mult).then_inc(S["g_ok"], 1)
                for j in range(8):
                    wait(dve, "droot", layer, j + 1)
                    link(v.reciprocal(dsq[:, j], dsq[:, j]))
                    last = v.tensor_tensor(cv[:, j], cv[:, j], dsq[:, j], ALU.mult)
                last.then_inc(S["qkn"], 1)
                wait(dve, "a_rt", layer, 1)
                link(v.reciprocal(ass, ass))
                qk = qkv[:, :, 0:768].rearrange("p t (h d) -> p t h d", d=HD)
                link(v.tensor_tensor(qk, qk, v3(ass, NT).unsqueeze(3).to_broadcast([P, NT, 12, HD]), ALU.mult))
                for t in range(NT):
                    q2 = qkv[:, t, 0:768].rearrange("p (h d) -> p h d", d=HD)
                    v.tensor_tensor(q2[:, 0:8], q2[:, 0:8], qkgain[:, 0:64].unsqueeze(1).to_broadcast([P, 8, HD]), ALU.mult)
                    last = v.tensor_tensor(q2[:, 8:12], q2[:, 8:12], qkgain[:, 64:128].unsqueeze(1).to_broadcast([P, 4, HD]), ALU.mult)
                link(last)
                for t in (1, 2):
                    q5 = qkv[:, t, 0:768].rearrange("p (h a f q) -> p h a f q", h=12, a=2, f=2)
                    x1, x2 = q5[:, :, :, 0], q5[:, :, :, 1]
                    cos, sin = (rope[:, t - 1, f].unsqueeze(1).to_broadcast([P, 12, 2, HD // 4]) for f in range(2))
                    for o, x, f in ((rt[0], x1, cos), (rt[1], x2, sin), (rt[2], x1, sin), (rt[3], x2, cos)):
                        last = v.tensor_tensor(o, x, f, ALU.mult)
                    link(last)
                    v.tensor_tensor(x1, rt[0], rt[1], ALU.subtract)
                    last = v.tensor_tensor(x2, rt[2], rt[3], ALU.add)
                    if t == 1:
                        link(last)
                last.then_inc(S["a_ok"], 1)
                wait(dve, "v_rt", layer, 1)
                link(v.reciprocal(vss, vss))
                for t in range(NT):
                    last = v.scalar_tensor_tensor(vB[:, t], vB[:, t], vss[:, t:t + 1], ggain, ALU.mult, ALU.mult)
                last.then_inc(S["v_ok"], 1)
                wait(dve, "gc_mm", layer, 1)
                gps = B[4][:, 0:96].rearrange("p (t n) -> p t n", t=NT)
                link(v.tensor_copy(gcs, gps[:, :, 0:8]))
                v.tensor_tensor(edec, gps[:, :, 8:16], gcs, ALU.subtract)
                v.tensor_copy(egl.rearrange("p t c n -> p t (c n)"), gps[:, :, 16:32]).then_inc(S["gc_v"], 1)
                wait(dve, "gc_e", layer, 1)
                v.tensor_tensor(beg, beta, eg, ALU.mult).then_inc(S["beg"], 1)
                for t in range(NT):
                    wait(dve, "b_mm", layer, t + 1)
                    for g in range(4):
                        gs = slice(g * P, (g + 1) * P)
                        last = v.scalar_tensor_tensor(uB[:, t, gs], B[2 + t][:, gs], bsT[:, layer, g:g + 1], uB[:, t, gs],
                                                      ALU.add, ALU.mult)
                    last.then_inc(S["b_v"], 1)
                n_at = NT * HEADS
                for i in range(n_at + 1):
                    if i >= KT and i % KT == 3:
                        ada_take(at["at"][i // KT - 1], 0)
                    if i < n_at:
                        w = P if i < HEADS else TOK
                        wait(dve, "at_s", layer, i + 1)
                        link(v.tensor_reduce(amx[:, i:i + 1], B[2 + i % 2][:, 0:w], AX.X, ALU.max))
                        v.tensor_scalar(anm[:, i:i + 1], amx[:, i:i + 1], -(HD ** -0.5), None, ALU.mult).then_inc(S["at_m"], 1)
                    if i:
                        j = i - 1
                        w = P if j < HEADS else TOK
                        wait(dve, "at_e", layer, j + 1)
                        link(v.reciprocal(ars[:, j:j + 1], ars[:, j:j + 1]))
                        v.tensor_scalar(Pb[:, j % 2, 0:w], Pb[:, j % 2, 0:w], ars[:, j:j + 1], None, ALU.mult).then_inc(S["at_p"], 1)
                ada_take(at["at"][-1], 0)
                dve.wait_ge(kv_out, 32 * (layer + 1))
                wait(dve, "at_o", layer, 3)
                dve.wait_ge(bf_ok, 1)
                for pair in range(3):
                    for d in range(2):
                        t = TILE[pair][d]
                        wait(dve, "d_in", layer, 2 * pair + d + 1)
                        link(v.tensor_tensor(dn(d, B_W), v3(B[2 + 3 * d][:, :], 4), bc(gcs[:, t, 4 * d:4 * d + 4], P), ALU.subtract))
                        v.tensor_scalar(dn(d, B_M), dn(d, B_W), 0.0, None, ALU.max)
                        v.tensor_scalar(dn(d, B_QK), dn(d, B_W), 0.0, None, ALU.min).then_inc(S["d_d0"], 1)
                    for d in range(2):
                        wait(dve, "d_pool", layer, 2 * pair + d + 1)
                        v.tensor_tensor(dn(d, B_QK), v3(B[4 + 3 * d][:, :], 4), dn(d, B_QK), ALU.mult)
                        v.tensor_tensor(dn(d, B_M), v3(B[3 + 3 * d][:, :], 4), dn(d, B_M), ALU.mult).then_inc(S["d_m"], 1)
                    for d in range(2):
                        g = 2 * pair + d
                        m0, m1 = (lm[:, 0, i].unsqueeze(1).to_broadcast([P, DNH, P]) for i in (d, 1 - d))
                        eye = ident.unsqueeze(1).to_broadcast([P, DNH, P])
                        wait(dve, "d_mt", layer, g + 1)
                        note(v.tensor_copy(dn(d, B_MT), v3(B[2 + 3 * d][:, :], 4)), "d_mtc", layer, g + 1)
                        v.tensor_tensor(dn(d, B_T), dn(d, B_M), m0, ALU.mult)
                        link(v.tensor_tensor(dn(d, B_U), dn(d, B_MT), m1, ALU.mult))
                        v.tensor_tensor(dn(d, B_T), dn(d, B_T), eye, ALU.add)
                        v.tensor_tensor(dn(d, B_U), dn(d, B_U), eye, ALU.add).then_inc(S["d_t1"], 1)
                    dve.wait_ge(S["d_t1"], PER["d_t1"] * layer + 2 * pair + 2)
                    for s in range(1, len(LEVELS)):
                        for d in range(2):
                            n = 10 * pair + 2 * (s - 1) + d + 1
                            wait(dve, "d_du", layer, n)
                            if s < len(LEVELS) - 1:
                                v.tensor_tensor(dn(d, B_T), dn(d, B_T), v3(B[3 + 3 * d][:, :], 4), ALU.add)
                            note(v.tensor_tensor(dn(d, B_U), dn(d, B_U), v3(B[4 + 3 * d][:, :], 4), ALU.add), "d_up", layer, n)
                    for step in range(2):
                        for d in range(2):
                            n = 4 * pair + 2 * step + d
                            ch = step if d == 0 else 1 - step
                            r = slice(CHUNK * ch, CHUNK * (ch + 1))
                            wait(dve, "s_ws", layer, n + 1)
                            v.tensor_tensor(dn(d, B_VN)[r], dn(d, B_VU)[r], v3(B[2 + 3 * d][r, :], 4), ALU.subtract).then_inc(S["s_vn"], 1)
                        for d in range(2):
                            n = 4 * pair + 2 * step + d
                            t = TILE[pair][d]
                            ch = step if d == 0 else 1 - step
                            wait(dve, "s_o", layer, n + 1)
                            for h in range(DNH):
                                last = v.scalar_tensor_tensor(state[:, d, h], state[:, d, h], egl[:, t, ch, 4 * d + h:4 * d + h + 1],
                                                              B[4 + 3 * d][:, h * P:(h + 1) * P], ALU.mult, ALU.add)
                            note(last, "s_st", layer, n + 1)
                    for d in range(2):
                        t = TILE[pair][d]
                        if pair == 1 or (pair == 0 and d == 0):
                            ins = v.tensor_copy(osum[:, t], B[3 + 3 * d][:, :])
                        else:
                            ins = v.tensor_tensor(osum[:, t], B[3 + 3 * d][:, :], osum[:, t], ALU.add)
                        note(ins, "s_or", layer, 2 * pair + d + 1)
                for n in at["z"]:
                    ada_take(n, 0)
                wait(dve, "oc_sq", layer, 1)
                v.tensor_reduce(oss, RX[:, 6144:7680].rearrange("p (n e) -> p n e", e=DK), AX.X, ALU.add).then_inc(S["oc_ss"], 1)
                wait(dve, "oc_rt", layer, 1)
                link(v.reciprocal(oss, oss))
                o12 = OT[:, 3072:4608].rearrange("p (n e) -> p n e", e=DK)
                link(v.tensor_tensor(o12, o12, bc(oss, DK), ALU.mult))
                link(v.tensor_tensor(o12, o12, dngain[:, :].unsqueeze(1).to_broadcast([P, 12, DK]), ALU.mult))
                wait(dve, "proj_ev", layer, T_Z + 3)
                v.tensor_tensor(osum, osum, zs, ALU.mult).then_inc(S["oc_v"], 1)
                ada_take(at["oc"][0], 6)
                wait(dve, "gsig", layer, 1)
                for m in range(8):
                    wait(dve, "br_mm", layer, m + 1)
                    for b in range(3):
                        last = v.tensor_tensor(btmp[b], B[2 + 3 * (m % 2) + b][:, 0:TOK], gates[:, 8 * b + m], ALU.mult)
                    link(last)
                    link(v.tensor_tensor(btmp[0], btmp[0], btmp[1], ALU.add))
                    note(v.tensor_tensor(merged[:, m], btmp[0], btmp[2], ALU.add), "br_ev", layer, m + 1)
                dve.wait_ge(unparked, 16 * (layer + 1))
                add_branch(layer, 2, 2, 1)
                for n in at["n3"]:
                    ada_take(n, 6)
                rstd(layer, 3)
                normed(layer, 2, 3)
                for n in at["h3"]:
                    ada_take(n, 6)

                def hidden(idx, r):
                    dve.wait_ge(gu_s, idx + 1)
                    dve.wait_ge(gu_u, idx + 1)
                    hi, lo = (x[:, bass.ds(idx, 1)].rearrange("p a n -> p (a n)") for x in (hid_hi, hid_lo))
                    v.tensor_tensor(hidf[:, r], B[2 + r][:, 0:TOK], sgb[:, r], ALU.mult).then_inc(gu_f, 1)
                    dve.wait_ge(gu_f, idx + 1)
                    v.tensor_copy(hi, hidf[:, r]).then_inc(gu_hi, 1)
                    dve.wait_ge(gu_hi, idx + 1)
                    v.tensor_tensor(lo, hidf[:, r], hi.bitcast(F32), ALU.subtract).then_inc(gu_h, 1)

                def lower_parts(j, it=None):
                    for g, (raw, hi, lo) in enumerate(ff_parts(j)):
                        dve.wait_ge(w_hi, ff_part(j, it, g))
                        v.tensor_tensor(lo, raw, hi.bitcast(F32), ALU.subtract).then_inc(w_lo, 1)

                def unit(j, it=None):
                    lower_parts(j + 1, it)
                    for r in range(2):
                        hidden(2 * j + r + (2 * FF_LOOP * it if it is not None else 0), r)

                if layer == 0:
                    wait(dve, "h_v", layer, 8)
                    link(v.tensor_copy(hT_hi[:, 4:8], hT[:, 4:8]))
                    v.tensor_tensor(hT_lo[:, 4:8], hT[:, 4:8], hT_hi[:, 4:8].bitcast(F32), ALU.subtract).then_inc(hs_ok, 1)
                    dve.wait_ge(hs_a, 1)
                    v.tensor_tensor(hT_lo[:, 0:4], hT[:, 0:4], hT_hi[:, 0:4].bitcast(F32), ALU.subtract).then_inc(hs_ok, 1)
                    lower_parts(0)
                    unit(0)
                    with dve.Fori(0, 2) as it:
                        for j in range(1, 1 + FF_LOOP):
                            unit(j, it)
                    for j in range(1 + 2 * FF_LOOP, FF_GU):
                        unit(j)
                    for m in range(8):
                        if m < 7:
                            lower_parts(FF_GU + m + 1)
                        dve.wait_ge(down_mm, m + 1)
                        v.tensor_copy(yT[:, m], B[4 + m % 2][:, 0:TOK]).then_inc(down_ev, 1)
                    dve.wait_ge(down_ev, 8)
                else:
                    note1(v.memset(RX[:, 3072:6144], 0.0), sc_ad)
                    dve.wait_ge(rl_mm, 1)
                    lg = v3(t1.rearrange("p t n -> p (t n)"), NT)
                    link(v.tensor_copy(lg, v3(B[6][:, 0:24], NT)))
                    idx = i8.bitcast(U32)
                    for t in range(NT):
                        link(v.max(m8[:, 8 * t:8 * t + 8], lg[:, t]))
                        link(v.max_index(idx[:, 8 * t:8 * t + 8], m8[:, 8 * t:8 * t + 8], lg[:, t]))
                    v.tensor_copy(i8f, idx)
                    v.tensor_tensor(m8[:, 1::8], m8[:, 1::8], m8[:, 0::8], ALU.subtract).then_inc(rl_c, 1)
                    dve.wait_ge(rl_e, 1)
                    link(v.tensor_scalar(m8[:, 0::8], m8[:, 1::8], 1.0, None, ALU.add))
                    link(v.reciprocal(m8[:, 0::8], m8[:, 0::8]))
                    link(v.tensor_tensor(m8[:, 1::8], m8[:, 1::8], m8[:, 0::8], ALU.mult))
                    sel, picked = sel2
                    for t in range(NT):
                        for j, (oh, pk) in enumerate(((oh0, sel), (oh1, picked))):
                            c0 = 8 * t + j
                            v.tensor_scalar(oh[:, t], iota8, i8f[:, c0:c0 + 1], m8[:, c0:c0 + 1], ALU.is_equal, ALU.mult)
                            last = v.tensor_scalar(pk[:, t], iota8, i8f[:, c0:c0 + 1], None, ALU.is_equal)
                    link(last)
                    v.tensor_tensor(comb, oh0, oh1, ALU.add)
                    note1(v.tensor_tensor(sel, sel, picked, ALU.add), rl_ok)
                    for half in range(2):
                        v.memset(ytok[:, 512 * half:512 * (half + 1)], 0.0).then_inc(yt_ok, 1)
                    v.memset(scatT, 0.0).then_inc(wt_ev, 1)
                    dve.wait_ge(rk_mm, 1)
                    v.tensor_tensor(rank, v3(B[6][:, 32:56], NT), sel, ALU.mult)
                    link(v.tensor_copy(cnt, B[6][:, 56:64]))
                    link(v.tensor_scalar(nit, cnt, 0.0, None, ALU.is_gt))
                    for n in range(1, NT):
                        link(v.scalar_tensor_tensor(nit, cnt, float(SLOTS * n), nit, ALU.is_gt, ALU.add))
                    link(v.tensor_scalar(nit[:, 0:1], nit[:, 0:1], 1.0, None, ALU.max))
                    link(v.tensor_tensor(tri8, before, nit.unsqueeze(1).to_broadcast([P, NE, NE]), ALU.mult))
                    link(v.tensor_reduce(e_lo, tri8, AX.X, ALU.add))
                    link(v.tensor_tensor(e_hi, e_lo, nit, ALU.add))
                    lo, hi = (x.unsqueeze(1).to_broadcast([P, NI, NE]) for x in (e_lo, e_hi))
                    v.tensor_tensor(own, lo, bc(item, NE), ALU.is_le)
                    link(v.tensor_tensor(own2, hi, bc(item, NE), ALU.is_gt))
                    link(v.tensor_tensor(own, own, own2, ALU.mult))
                    link(v.tensor_tensor(own2, own, iota8.unsqueeze(1).to_broadcast([P, NI, NE]), ALU.mult))
                    link(v.tensor_reduce(it_e, own2, AX.X, ALU.add))
                    v.tensor_copy(table[:, 0:NI], it_e)
                    v.tensor_copy(table[:, NI:NI + 1], e_hi[:, NE - 1:NE])
                    v.tensor_scalar(table[:, NI + 1:NI + 2], e_hi[:, NE - 1:NE], 1.0, None, ALU.subtract).then_inc(tbl_ok, 1)
                    link(v.tensor_tensor(own2, own, lo, ALU.mult))
                    link(v.tensor_reduce(it_lo, own2, AX.X, ALU.add))
                    link(v.tensor_tensor(it_lo, item, it_lo, ALU.subtract))
                    link(v.tensor_scalar(it_lo, it_lo, float(SLOTS), None, ALU.mult))
                    own4 = own.unsqueeze(2).to_broadcast([P, NI, NT, NE])
                    link(v.tensor_tensor(oprod, own4, rank.unsqueeze(1).to_broadcast([P, NI, NT, NE]), ALU.mult))
                    link(v.tensor_reduce(it_rank, oprod, AX.X, ALU.add))
                    v.tensor_tensor(it_rank, it_rank, bc(it_lo, NT), ALU.subtract)
                    link(v.tensor_tensor(oprod, own4, comb.unsqueeze(1).to_broadcast([P, NI, NT, NE]), ALU.mult))
                    link(v.tensor_reduce(it_comb, oprod, AX.X, ALU.add))

                    def of_item(x, i):
                        ap = x[:, bass.ds(i, 1)].rearrange("p a t -> p (a t)")
                        return ap.unsqueeze(2).to_broadcast([P, NT, SLOTS])

                    def choose(i):
                        v.tensor_tensor(esel, slot1.unsqueeze(1).to_broadcast([P, NT, SLOTS]), of_item(it_rank, i),
                                        ALU.is_equal).then_inc(sel_ok, 1)

                    def add_up(i):
                        dve.wait_ge(sc_ad, KT * i + 1)
                        for m in range(KT):
                            dve.wait_ge(sc_mm, KT * i + m + 1)
                            v.tensor_tensor(yT[:, m], B[6 + m % 2][:, 0:TOK], yT[:, m], ALU.add).then_inc(sc_ad, 1)

                    def lower(j, i):
                        for h in range(M_HALF):
                            m_lower(dve, v, j, h, i, mv_lo)

                    def gathered(i):
                        for half in range(2):
                            dve.wait_ge(ga_ev, 2 * i + half + 1)
                            ks = slice(4 * half, 4 * half + 4)
                            v.tensor_tensor(xg_lo[:, ks], v3(B[4 + half][:, :], 4), xg_hi[:, ks].bitcast(F32),
                                            ALU.subtract).then_inc(ga_lo, 1)

                    def hidden_lower(j, i):
                        dve.wait_ge(hh_ok, M_GU * i + j + 1)
                        n = m_shape(j)[2] // P
                        ks = slice(2 * j, 2 * j + n)
                        v.tensor_tensor(ehid_lo[:, ks], v3(B[2 + j % 2][:, 0:n * P], n), ehid_hi[:, ks].bitcast(F32),
                                        ALU.subtract).then_inc(hl_ok, 1)

                    def item_lower(i, last):
                        dve.wait_ge(sel_ok, i + 1)
                        dve.wait_ge(ga_mm, 2 * i + 2)
                        v.tensor_tensor(wsel, esel, of_item(it_comb, i), ALU.mult).then_inc(wsel_ok, 1)
                        dve.wait_ge(wsel_ok, i + 1)
                        choose(i + 1)
                        for j in range(M_GU):
                            if 0 < j < M_GU - 2:
                                lower(j + 2, i)
                            n = m_shape(j)[2]
                            dve.wait_ge(msg_ok, M_GU * i + j + 1)
                            v.tensor_tensor(ehid[:, j % 2, 0:n], B[j % 2][:, n:2 * n], esg[:, j % 2, 0:n], ALU.mult).then_inc(mh_ok, 1)
                            if j == 0:
                                add_up(i)
                                lower(2, i)
                            else:
                                hidden_lower(j - 1, i)
                        hidden_lower(M_GU - 1, i)
                        gathered(i + 1)
                        for j in (M_GU + 2, M_GU + 3):
                            lower(j, i)
                        if not last:
                            for j in range(2):
                                lower(j, i + 1)

                    choose(0)
                    lower(0, 0)
                    gathered(0)
                    lower(1, 0)
                    n_items = dve.value_load(table[0:1, NI:NI + 1], min_val=MIN_ITEMS, max_val=NI - 1)
                    last_item = dve.value_load(table[0:1, NI + 1:NI + 2], min_val=MIN_ITEMS - 1, max_val=NI - 2)
                    with dve.Fori(0, last_item) as i:
                        item_lower(i, False)
                    item_lower(last_item, True)
                    add_up(n_items)
                    dve.wait_ge(sc_ad, KT * n_items + KT + 1)
                add_branch(layer, 4, 5, 2)
                for n in at["n4"]:
                    ada_take(n, 6)


_INS = ["x_prompt", "x_sample", "cache_attn_k", "cache_attn_v", "state_delta", "c", "c_ctx", "ada_w", "ada_b", "norms", "w_in",
        "qk_norm", "gmlp_norm", "gmlp_ws", "gmlp_bs", "dn_conv", "dn_a_log", "dn_dt_bias", "dn_norm", "w_branch", "w_out",
        "ffn_w_gate", "ffn_w_up", "ffn_w_down", "moe_router", "moe_w_gate", "moe_w_up", "moe_w_down"]
_OUTS = [(1, CTX, D), (1, LAT, D), (1, DEPTH, CTX, KVH, HD), (1, DEPTH, CTX, KVH, HD), (1, DEPTH, 2, DNH, DK, DK)]


def kernel(**inputs):
    import concourse.bacc as _bacc
    from concourse.bass_utils import run_bass_kernel_spmd as _run

    nc = _bacc.Bacc("TRN2", target_bir_lowering=False, num_devices=1)
    arrays = {"constants": constants()}
    args = [nc.dram_tensor("constants", (P, NCST), F32, kind="ExternalInput").ap()]
    for name in _INS:
        a = np.ascontiguousarray(inputs[name])
        arrays[f"in_{name}"] = a
        args.append(nc.dram_tensor(f"in_{name}", a.shape, mybir.dt.from_np(a.dtype), kind="ExternalInput").ap())
    args.append(nc.dram_tensor("xpark", (P, KT * TOK), F32, kind="Internal").ap())
    for i, shape in enumerate(_OUTS):
        args.append(nc.dram_tensor(f"out_{i}", shape, F32, kind="ExternalOutput").ap())
    build(nc, *args)
    r = _run(nc, [arrays], core_ids=[0])
    return tuple(r.results[0][f"out_{i}"] for i in range(len(_OUTS)))
```
